# Optimizing a Trainium2 kernel written in Bass

```python
import math
import jax
import jax.numpy as jnp
from jax import lax
import numpy as np

D_MODEL = 1024
BATCH = 1
SEQ = 1024
DEPTH = 1
DEC_BATCH = 8
DEC_SEQ = 4
PAST_LEN = 1024
PAGE_SIZE = 128

D_MIX = D_MODEL
D_ATT = D_MIX // 2
D_RWKV = D_MIX - D_ATT
A_HEADS = 4
A_DH = D_ATT // A_HEADS // 2
A_DK = 2 * A_DH
A_DV = 2 * A_DH
R_HEAD = 64
R_HEADS = D_RWKV // R_HEAD
LORA_W = 64
LORA_A = 64
LORA_G = 128
N_Q = A_HEADS * A_DK
N_K = A_HEADS * A_DK
N_V = A_HEADS * A_DV
N_SHIFT = 3 * D_RWKV + LORA_W + LORA_A + LORA_G
N_IN = N_Q + N_K + N_V + N_SHIFT
IN_SPLITS = (N_Q, N_Q + N_K, N_Q + N_K + N_V)
SHIFT_SPLITS = (D_RWKV, 2 * D_RWKV, 3 * D_RWKV, 3 * D_RWKV + LORA_W, 3 * D_RWKV + LORA_W + LORA_A)
D_FF = 2752
CONV_W = 3
D_PLE = 256
Q_BLOCK = 128
NORM_EPS = 1e-6
GN_EPS = 64e-5
ATT_SCALE = A_DH ** -0.5

kernel_name = 'hymba_diffattn_rwkv7_convffn_step'

def _rmsnorm(x, g):
    xf = x.astype(jnp.float32)
    y = xf * lax.rsqrt(jnp.mean(xf * xf, axis=-1, keepdims=True) + NORM_EPS)
    return (y * g.astype(jnp.float32)).astype(x.dtype)

def _diff_lambda(lq1, lk1, lq2, lk2, lam_init):
    f = lambda a: a.astype(jnp.float32)
    return jnp.exp(jnp.sum(f(lq1) * f(lk1))) - jnp.exp(jnp.sum(f(lq2) * f(lk2))) + lam_init

def _diff_attn_prompt(q, k, v, lam):
    b, s = q.shape[0], q.shape[1]
    nb = s // Q_BLOCK
    qb = jnp.moveaxis(q.reshape(b, nb, Q_BLOCK, A_HEADS, 2, A_DH), 1, 0)
    kpos = jnp.arange(s)

    def one_block(args):
        qi, i = args
        sc = jnp.einsum('bqhcd,bkhcd->bhcqk', qi, k).astype(jnp.float32) * ATT_SCALE
        qpos = i * Q_BLOCK + jnp.arange(Q_BLOCK)
        sc = jnp.where(kpos[None, :] <= qpos[:, None], sc, -jnp.inf)
        p = jax.nn.softmax(sc, axis=-1)
        wgt = p[:, :, 0] - lam * p[:, :, 1]
        return jnp.einsum('bhqk,bkhd->bqhd', wgt.astype(v.dtype), v)

    o = lax.map(one_block, (qb, jnp.arange(nb)))
    return jnp.moveaxis(o, 0, 1).reshape(b, s, A_HEADS, A_DV)

def _diff_attn_sample(q, k, v, k_past, v_past, lam):
    t = q.shape[1]
    n_past = k_past.shape[1]
    sp = jnp.einsum('bqhcd,bkhcd->bhcqk', q, k_past).astype(jnp.float32) * ATT_SCALE
    sn = jnp.einsum('bqhcd,bkhcd->bhcqk', q, k).astype(jnp.float32) * ATT_SCALE
    sn = jnp.where(jnp.tril(jnp.ones((t, t), dtype=bool)), sn, -jnp.inf)
    p = jax.nn.softmax(jnp.concatenate([sp, sn], axis=-1), axis=-1)
    wgt = (p[:, :, 0] - lam * p[:, :, 1]).astype(v.dtype)
    return (jnp.einsum('bhqk,bkhd->bqhd', wgt[..., :n_past], v_past)
            + jnp.einsum('bhqk,bkhd->bqhd', wgt[..., n_past:], v))

def _wkv_scan(s0, r, w, k, v, kk, a):
    def step(s, inp):
        r_t, w_t, k_t, v_t, kk_t, a_t = inp
        sa = jnp.einsum('bhvk,bhk->bhv', s, -kk_t)
        s = (s * w_t[:, :, None, :] + sa[..., None] * (kk_t * a_t)[:, :, None, :]
             + v_t[..., None] * k_t[:, :, None, :])
        return s, jnp.einsum('bhvk,bhk->bhv', s, r_t)

    xs = tuple(jnp.moveaxis(z, 1, 0) for z in (r, w, k, v, kk, a))
    s_fin, ys = lax.scan(step, s0, xs)
    return jnp.moveaxis(ys, 0, 1), s_fin

def _rwkv_group(pr, prev, wkv0, lp):
    b, t, _ = pr.shape
    f32 = jnp.float32
    shifted = jnp.concatenate([prev[:, None, :].astype(pr.dtype), pr[:, :-1]], axis=1)
    m = pr + (shifted - pr) * lp['mu_shift']
    r, k, v, xw, xa, xg = jnp.split(m, SHIFT_SPLITS, axis=-1)
    w_log = -jax.nn.softplus(-(lp['w0'] + jnp.tanh(xw) @ lp['w2']).astype(f32)) - 0.5
    decay = jnp.exp(-jnp.exp(w_log))
    a = jax.nn.sigmoid((lp['a0'] + xa @ lp['a2']).astype(f32))
    g = (jax.nn.sigmoid(xg) @ lp['g2']).astype(f32)
    hs = lambda z: z.astype(f32).reshape(b, t, R_HEADS, R_HEAD)
    r_h, k_h, v_h, a_h, w_h = hs(r), hs(k), hs(v), hs(a), hs(decay)
    kk = k_h * lp['k_k'].astype(f32).reshape(R_HEADS, R_HEAD)
    kk = kk / jnp.maximum(jnp.linalg.norm(kk, axis=-1, keepdims=True), 1e-12)
    k_h = k_h * (1.0 + (a_h - 1.0) * lp['k_a'].astype(f32).reshape(R_HEADS, R_HEAD))
    y, wkv = _wkv_scan(wkv0.astype(f32), r_h, w_h, k_h, v_h, kk, a_h)
    mean = jnp.mean(y, axis=-1, keepdims=True)
    var = jnp.mean(jnp.square(y - mean), axis=-1, keepdims=True)
    y = ((y - mean) * lax.rsqrt(var + GN_EPS)).reshape(b, t, D_RWKV)
    y = y * lp['ln_x_w'].astype(f32) + lp['ln_x_b'].astype(f32)
    bonus = jnp.sum(r_h * k_h * lp['r_k'].astype(f32), axis=-1, keepdims=True) * v_h
    y = (y + bonus.reshape(b, t, D_RWKV)) * g
    return y.astype(pr.dtype), pr[:, -1], wkv

def _conv_ffn(h, prev, lp):
    t = h.shape[1]
    u = h @ lp['w_up']
    ext = jnp.concatenate([prev.astype(u.dtype), u], axis=1)
    c = lp['conv_b'] + lp['conv_w'][0] * ext[:, 0:t]
    for j in range(1, CONV_W):
        c = c + lp['conv_w'][j] * ext[:, j:j + t]
    gate, val = jnp.split(c, 2, axis=-1)
    out = (jax.nn.gelu(gate, approximate=True) * val) @ lp['w_down']
    return out, ext[:, t:]

def _layer(x, pe, lp, lam_init, attend, shift0, wkv0, conv0):
    b, t, _ = x.shape
    h = _rmsnorm(x, lp['g_mix_pre'])
    proj = h @ lp['w_in']
    q, k, v, pr = jnp.split(proj, IN_SPLITS, axis=-1)
    q = q.reshape(b, t, A_HEADS, 2, A_DH)
    k4 = k.reshape(b, t, A_HEADS, 2, A_DH)
    v = v.reshape(b, t, A_HEADS, A_DV)
    lam = _diff_lambda(lp['lam_q1'], lp['lam_k1'], lp['lam_q2'], lp['lam_k2'], lam_init)
    o_att = attend(q, k4, v, lam)
    o_att = (_rmsnorm(o_att, lp['g_subln']) * (1.0 - lam_init)).reshape(b, t, D_ATT)
    o_rwkv, shift_new, wkv_new = _rwkv_group(pr, shift0, wkv0, lp)
    mix = jnp.concatenate([o_att.astype(x.dtype), o_rwkv], axis=-1) @ lp['w_o']
    x = x + _rmsnorm(mix, lp['g_mix_post'])
    f, conv_new = _conv_ffn(_rmsnorm(x, lp['g_ffn_pre']), conv0, lp)
    x = x + _rmsnorm(f, lp['g_ffn_post'])
    ple = (pe @ lp['w_ple']) * jax.nn.sigmoid(x @ lp['w_ple_gate'])
    x = x + _rmsnorm(ple, lp['g_ple'])
    return x, k.reshape(b, t, A_HEADS, A_DK), v, shift_new, wkv_new, conv_new

def setup_inputs(seed: int = 0) -> dict:
    key = jax.random.key(seed)
    keys = iter(jax.random.split(key, 64))

    def nrm(shape, scale):
        return jax.random.normal(next(keys), shape, jnp.float32) * scale

    def gain(shape):
        return 1.0 + nrm(shape, 0.05)

    L = DEPTH
    n_pages = PAST_LEN // PAGE_SIZE
    n_pool = (DEC_BATCH * n_pages * 5) // 4
    page_table = jax.random.permutation(next(keys), n_pool)[:DEC_BATCH * n_pages]
    page_table = page_table.reshape(DEC_BATCH, n_pages).astype(jnp.int32)
    return {
        'x_prompt': nrm((BATCH, SEQ, D_MODEL), 1.0),
        'x_sample': nrm((DEC_BATCH, DEC_SEQ, D_MODEL), 1.0),
        'p_prompt': nrm((L, BATCH, SEQ, D_PLE), 1.0),
        'p_sample': nrm((L, DEC_BATCH, DEC_SEQ, D_PLE), 1.0),
        'cache_k': nrm((L, n_pool, PAGE_SIZE, A_HEADS, A_DK), 1.0),
        'cache_v': nrm((L, n_pool, PAGE_SIZE, A_HEADS, A_DV), 1.0),
        'page_table': page_table,
        'state_shift': nrm((L, DEC_BATCH, N_SHIFT), 1.0),
        'state_wkv': nrm((L, DEC_BATCH, R_HEADS, R_HEAD, R_HEAD), 0.3),
        'state_conv': nrm((L, DEC_BATCH, CONV_W - 1, 2 * D_FF), 1.0),
        'g_mix_pre': gain((L, D_MODEL)),
        'w_in': nrm((L, D_MODEL, N_IN), D_MODEL ** -0.5),
        'lam_q1': nrm((L, A_DH), 0.1),
        'lam_k1': nrm((L, A_DH), 0.1),
        'lam_q2': nrm((L, A_DH), 0.1),
        'lam_k2': nrm((L, A_DH), 0.1),
        'g_subln': gain((L, A_DV)),
        'mu_shift': jax.random.uniform(next(keys), (L, N_SHIFT), jnp.float32),
        'w0': -3.0 + nrm((L, D_RWKV), 1.0),
        'w2': nrm((L, LORA_W, D_RWKV), 0.5 * LORA_W ** -0.5),
        'a0': nrm((L, D_RWKV), 0.1),
        'a2': nrm((L, LORA_A, D_RWKV), 0.5 * LORA_A ** -0.5),
        'g2': nrm((L, LORA_G, D_RWKV), LORA_G ** -0.5),
        'k_k': 0.85 + nrm((L, D_RWKV), 0.05),
        'k_a': gain((L, D_RWKV)),
        'r_k': nrm((L, R_HEADS, R_HEAD), 0.1),
        'ln_x_w': gain((L, D_RWKV)),
        'ln_x_b': nrm((L, D_RWKV), 0.01),
        'w_o': nrm((L, D_MIX, D_MODEL), D_MIX ** -0.5),
        'g_mix_post': gain((L, D_MODEL)),
        'g_ffn_pre': gain((L, D_MODEL)),
        'w_up': nrm((L, D_MODEL, 2 * D_FF), D_MODEL ** -0.5),
        'conv_w': nrm((L, CONV_W, 2 * D_FF), 0.3).at[:, CONV_W - 1].add(1.0),
        'conv_b': nrm((L, 2 * D_FF), 0.01),
        'w_down': nrm((L, D_FF, D_MODEL), D_FF ** -0.5),
        'g_ffn_post': gain((L, D_MODEL)),
        'w_ple': nrm((L, D_PLE, D_MODEL), D_PLE ** -0.5),
        'w_ple_gate': nrm((L, D_MODEL, D_MODEL), D_MODEL ** -0.5),
        'g_ple': gain((L, D_MODEL)),
    }

def reference(x_prompt, x_sample, p_prompt, p_sample, cache_k, cache_v, page_table,
              state_shift, state_wkv, state_conv, g_mix_pre, w_in, lam_q1, lam_k1,
              lam_q2, lam_k2, g_subln, mu_shift, w0, w2, a0, a2, g2, k_k, k_a, r_k,
              ln_x_w, ln_x_b, w_o, g_mix_post, g_ffn_pre, w_up, conv_w, conv_b, w_down,
              g_ffn_post, w_ple, w_ple_gate, g_ple):
    bp = x_prompt.shape[0]
    bd = x_sample.shape[0]
    n_past = page_table.shape[1] * cache_k.shape[2]
    xp, xs = x_prompt, x_sample
    kp_l, vp_l, ks_l, vs_l = [], [], [], []
    shp_l, wkp_l, cvp_l, shs_l, wks_l, cvs_l = [], [], [], [], [], []
    for l in range(DEPTH):
        lp = {
            'g_mix_pre': g_mix_pre[l], 'w_in': w_in[l], 'lam_q1': lam_q1[l], 'lam_k1': lam_k1[l],
            'lam_q2': lam_q2[l], 'lam_k2': lam_k2[l], 'g_subln': g_subln[l], 'mu_shift': mu_shift[l],
            'w0': w0[l], 'w2': w2[l], 'a0': a0[l], 'a2': a2[l], 'g2': g2[l], 'k_k': k_k[l],
            'k_a': k_a[l], 'r_k': r_k[l], 'ln_x_w': ln_x_w[l], 'ln_x_b': ln_x_b[l], 'w_o': w_o[l],
            'g_mix_post': g_mix_post[l], 'g_ffn_pre': g_ffn_pre[l], 'w_up': w_up[l],
            'conv_w': conv_w[l], 'conv_b': conv_b[l], 'w_down': w_down[l],
            'g_ffn_post': g_ffn_post[l], 'w_ple': w_ple[l], 'w_ple_gate': w_ple_gate[l],
            'g_ple': g_ple[l],
        }
        lam_init = 0.8 - 0.6 * math.exp(-0.3 * l)
        xp, kp, vp, shp, wkp, cvp = _layer(
            xp, p_prompt[l], lp, lam_init, _diff_attn_prompt,
            jnp.zeros((bp, N_SHIFT), xp.dtype),
            jnp.zeros((bp, R_HEADS, R_HEAD, R_HEAD), jnp.float32),
            jnp.zeros((bp, CONV_W - 1, 2 * D_FF), xp.dtype))
        k_past = cache_k[l][page_table].reshape(bd, n_past, A_HEADS, 2, A_DH)
        v_past = cache_v[l][page_table].reshape(bd, n_past, A_HEADS, A_DV)
        attend_s = lambda q, k, v, lam, kpast=k_past, vpast=v_past: _diff_attn_sample(q, k, v, kpast, vpast, lam)
        xs, ks, vs, shs, wks, cvs = _layer(
            xs, p_sample[l], lp, lam_init, attend_s,
            state_shift[l], state_wkv[l], state_conv[l])
        kp_l.append(kp); vp_l.append(vp); ks_l.append(ks); vs_l.append(vs)
        shp_l.append(shp); wkp_l.append(wkp.astype(state_wkv.dtype)); cvp_l.append(cvp)
        shs_l.append(shs); wks_l.append(wks.astype(state_wkv.dtype)); cvs_l.append(cvs)
    return (xp, xs, jnp.stack(kp_l), jnp.stack(vp_l), jnp.stack(ks_l), jnp.stack(vs_l),
            jnp.stack(shp_l), jnp.stack(wkp_l), jnp.stack(cvp_l),
            jnp.stack(shs_l), jnp.stack(wks_l), jnp.stack(cvs_l))


_drawn_inputs = setup_inputs


def setup_inputs(seed=0):
    import zlib

    import numpy as np

    out = dict(_drawn_inputs(seed))
    spreads = {}
    factors = {'lam_q2': 41.254, 'ln_x_w': 3.022, 'ln_x_b': 26.948, 'conv_b': 8.0, 'g_subln': 3.336}
    for name, (base, spread) in spreads.items():
        noise = np.random.default_rng([zlib.crc32(name.encode()), seed]).standard_normal(out[name].shape)
        drawn = base * np.exp(spread * noise) if base else spread * noise
        out[name] = jnp.asarray(drawn.astype(out[name].dtype))
    for name, factor in factors.items():
        out[name] = (out[name] * factor).astype(out[name].dtype)
    return out
```

```python
import math
from contextlib import ExitStack

import concourse.bass as bass
from concourse import mybir

F32 = mybir.dt.float32
F32R = mybir.dt.float32r
BF16 = mybir.dt.bfloat16
I32 = mybir.dt.int32
ALU = mybir.AluOpType
ACT = mybir.ActivationFunctionType
AX = mybir.AxisListType.X
ds = bass.ds

P = 128
D = 1024
KD = D // P
SEQ = 1024
NB, NT = 8, 4
NS = NB * NT
T = SEQ + NS
T3 = T // 3
HEADS, DH = 4, 64
PAGES, PAGE = 8, 128
POOL = 80
N_IN = 3328
MT_IN = N_IN // P
FF = 2752
FT = (FF + P - 1) // P
TH = T // 2
PLE = 256
EPS = 1e-6
GN_EPS = 64e-5
LAM_INIT = 0.8 - 0.6 * math.exp(0.0)
C = 64
NCH = SEQ // C
NEG = -1e30
E05 = math.exp(-0.5)

PCOL = {}
_n = 0
for _name, _w in (("g_mix_pre", 8), ("g_mix_post", 8), ("g_ffn_pre", 8), ("g_ffn_post", 8), ("g_ple", 8),
                  ("g_subln", 1), ("mu", 14), ("w0", 4), ("a0", 4), ("k_k", 4), ("k_a", 4), ("r_k", 4),
                  ("ln_w", 4), ("ln_b", 4), ("cw0", 2 * FT), ("cw1", 2 * FT), ("cw2", 2 * FT), ("cb", 2 * FT)):
    PCOL[_name] = _n
    _n += _w
NPARAM = _n


class Kit:

    def __init__(self, nc, top):
        self.nc, self.live = nc, []

    def sb(self, ctx, name, shape, dt=F32):
        return ctx.enter_context(self.nc.sbuf_tensor(name, shape, dt))

    def ps(self, ctx, name, shape, dt=F32):
        return ctx.enter_context(self.nc.psum_tensor(name, shape, dt))

    def sem(self, name):
        self.live.append(self.nc.alloc_semaphore(name=name))
        return self.live[-1]

    def retire(self):
        self.nc.clear_and_free_semaphores(self.live)
        self.nc.all_engine_barrier()
        self.live = []


def load_phase(kit, name, pairs):
    nc = kit.nc
    loaded_sp, loaded_act = kit.sem(name + "_loaded_sp"), kit.sem(name + "_loaded_act")
    with nc.Block() as block:
        @block.sync
        def _(sp):
            for dst, src in pairs[0::2]:
                sp.dma_start(dst, src).then_inc(loaded_sp, 16)
            sp.wait_ge(loaded_sp, 16 * len(pairs[0::2]))

        @block.scalar
        def _(act):
            for dst, src in pairs[1::2]:
                act.dma_start(dst, src).then_inc(loaded_act, 16)
            if len(pairs) > 1:
                act.wait_ge(loaded_act, 16 * len(pairs[1::2]))


def rms_rows(kit, name, X, R, tiles, width, ones, eps):
    nc = kit.nc
    squared, summed, totals, rooted = (kit.sem(f"{name}_{s}") for s in ("squared", "summed", "totals", "rooted"))
    nparts = (width + 511) // 512
    while width % nparts:
        nparts += 1
    part = width // nparts
    with ExitStack() as ctx:
        sq = kit.sb(ctx, name + "_sq", [P, 2, width])
        acc = kit.sb(ctx, name + "_acc", [P, width])
        tot = kit.ps(ctx, name + "_tot", [P, nparts, 512])
        block = ctx.enter_context(nc.Block())

        @block.scalar
        def _(act):
            for k in range(tiles):
                if k >= 2:
                    act.wait_ge(summed, k - 1)
                nc.scalar.activation(sq[:, k % 2, :], X[:, k, :], ACT.Square).then_inc(squared, 1)
            act.wait_ge(totals, 1)
            nc.scalar.activation(R.rearrange("p (n t) -> p n t", t=part), tot[:, :, 0:part], ACT.Sqrt,
                                 bias=eps).then_inc(rooted, 1)

        @block.vector
        def _(dve):
            for k in range(tiles):
                dve.wait_ge(squared, k + 1)
                if k == 0:
                    nc.vector.tensor_copy(acc[:], sq[:, 0, :]).then_inc(summed, 1)
                else:
                    dve.wait_ge(summed, k)
                    nc.vector.tensor_tensor(acc[:], acc[:], sq[:, k % 2, :], ALU.add).then_inc(summed, 1)
            dve.wait_ge(rooted, 1)
            nc.vector.reciprocal(R, R).then_inc(rooted, 1)
            dve.wait_ge(rooted, 2)

        @block.tensor
        def _(pe):
            pe.wait_ge(summed, tiles)
            for n in range(nparts):
                last = nc.tensor.matmul(tot[:, n, 0:part], ones, acc[:, n * part:(n + 1) * part],
                                        start=True, stop=True)
            last.then_inc(totals, 1)


def scale_split(kit, name, X, tiles, width, Hh, Hl, gain=None, R=None, store=None):
    nc = kit.nc
    scaled, high, low = (kit.sem(f"{name}_{s}") for s in ("scaled", "high", "low"))
    stored = [kit.sem(f"{name}_stored{b}") for b in range(2)] if store is not None else None
    with ExitStack() as ctx:
        tmp = kit.sb(ctx, name + "_tmp", [P, 2, width]) if gain is not None else None
        block = ctx.enter_context(nc.Block())

        @block.vector
        def _(dve):
            def scale(k):
                if k >= 2 and store is not None:
                    dve.wait_ge(stored[k % 2], 16 * (k // 2))
                elif k >= 2:
                    dve.wait_ge(low, k - 1)
                nc.vector.scalar_tensor_tensor(tmp[:, k % 2, :], X[:, k, :], gain(k), R(k),
                                               ALU.mult, ALU.mult).then_inc(scaled, 1)

            for k in range(tiles):
                if gain is not None:
                    scale(k)
                if store is None:
                    src = tmp[:, k % 2, :] if gain is not None else X[:, k, :]
                    dve.wait_ge(high, k + 1)
                    nc.vector.tensor_tensor(Hl[:, k, :], src, Hh[:, k, :].bitcast(F32),
                                            ALU.subtract).then_inc(low, 1)
            if store is None:
                dve.wait_ge(low, tiles)

        if store is None:
            @block.scalar
            def _(act):
                for k in range(tiles):
                    if gain is not None:
                        act.wait_ge(scaled, k + 1)
                    src = tmp[:, k % 2, :] if gain is not None else X[:, k, :]
                    nc.scalar.activation(Hh[:, k, :], src, ACT.Copy).then_inc(high, 1)
        else:
            @block.sync
            def _(sp):
                for k in range(tiles):
                    sp.wait_ge(scaled, k + 1)
                    sp.dma_start(store[:, k, :], tmp[:, k % 2, :]).then_inc(stored[k % 2], 16)
                for b in range(2):
                    sp.wait_ge(stored[b], 16 * (tiles // 2))


def add_scaled(kit, name, Y, gain, R, X):
    nc = kit.nc
    scaled, added = kit.sem(name + "_scaled"), kit.sem(name + "_added")
    with nc.Block() as block:
        @block.vector
        def _(dve):
            for k in range(KD):
                nc.vector.scalar_tensor_tensor(Y[:, k, :], Y[:, k, :], gain[:, k:k + 1], R,
                                               ALU.mult, ALU.mult).then_inc(scaled, 1)

        @block.gpsimd
        def _(pool):
            for k in range(KD):
                pool.wait_ge(scaled, k + 1)
                nc.gpsimd.tensor_tensor(X[:, k, :], X[:, k, :], Y[:, k, :], ALU.add).then_inc(added, 1)
            pool.wait_ge(added, KD)


class ToDram:

    def __init__(self, kit, ctx, name, parts, dst):
        self.nc, self.parts, self.dst = kit.nc, parts, dst
        self.out = kit.sb(ctx, name + "_out", [P, 2, len(parts), parts[0][1]])
        self.stored = [kit.sem(f"{name}_stored{b}") for b in range(2)]

    def act(self, act, m, b, turn, first):
        act.wait_ge(self.multiplied, (m + 1) * self.units)
        if not first:
            act.wait_ge(self.stored[b], turn * 16)
        self.nc.scalar.activation(self.out[:, b], self.acc[:, b, :, 0:self.parts[0][1]],
                                  ACT.Copy).then_inc(self.drained, 1)

    def pool(self, pool, m, b, turn, first):
        pool.wait_ge(self.drained, m + 1)
        pool.dma_start(self.dst(m), self.out[:, b].rearrange("p n t -> p (n t)")).then_inc(self.stored[b], 16)

    def pool_end(self, pool, ntiles):
        for b in range(2):
            pool.wait_ge(self.stored[b], 16 * (ntiles // 2))


class ToSbuf:

    def __init__(self, kit, ctx, name, parts, Y, scale=1.0):
        self.nc, self.parts, self.Y, self.scale = kit.nc, parts, Y, scale

    def act(self, act, m, b, turn, first):
        act.wait_ge(self.multiplied, (m + 1) * self.units)
        w = self.parts[0][1]
        out = self.Y[:, ds(m, 1), :].rearrange("p a (n t) -> p (a n) t", t=w)
        self.nc.scalar.activation(out, self.acc[:, b, :, 0:w], ACT.Copy,
                                  scale=self.scale).then_inc(self.drained, 1)


class Gate:

    def __init__(self, kit, ctx, name, parts, Y):
        self.nc, self.parts, self.Y = kit.nc, parts, Y
        self.th = kit.sb(ctx, name + "_th", [P, 2, T])
        self.gated = kit.sem(name + "_gated")

    def act(self, act, m, b, turn, first):
        act.wait_ge(self.multiplied, (m + 1) * self.units)
        if not first:
            act.wait_ge(self.gated, m - 1)
        w = self.parts[0][1]
        self.nc.scalar.activation(self.th[:, b].rearrange("p (n t) -> p n t", t=w), self.acc[:, b, :, 0:w],
                                  ACT.Tanh, scale=0.5).then_inc(self.drained, 1)

    def dve(self, dve, m, b, turn, first):
        dve.wait_ge(self.drained, m + 1)
        y = self.Y[:, ds(m, 1), :].rearrange("p a t -> p (a t)")
        self.nc.vector.scalar_tensor_tensor(y, self.th[:, b], 1.0, y, ALU.add, ALU.mult).then_inc(self.gated, 1)

    def dve_end(self, dve, ntiles):
        dve.wait_ge(self.gated, ntiles)


class ConvGate:

    def __init__(self, kit, ctx, name, parts, par, carry, states, conv_out, Gh, Gl, last):
        self.nc, self.parts, self.par, self.last = kit.nc, parts, par, last
        self.carry, self.states, self.conv_out, self.Gh, self.Gl = carry, states, conv_out, Gh, Gl
        self.prompt = TH - NS if last else TH
        self.wide = 2 + self.prompt + (NB * (2 + NT) if last else 0)
        self.u = kit.sb(ctx, name + "_u", [P, 2, self.wide])
        self.c = kit.sb(ctx, name + "_c", [P, 2, self.wide - 2])
        self.ge = kit.sb(ctx, name + "_ge", [P, self.wide - 2])
        self.g = kit.sb(ctx, name + "_g", [P, TH])
        self.S = {n: kit.sem(f"{name}_{n}") for n in ("led", "tap0", "tap1", "tap2", "saved", "gelued", "gated",
                                                      "g_high", "g_low")}

    def samples(self, z, off=0):
        return z[:, 2 + self.prompt:].rearrange("p (n t) -> p n t", t=2 + NT)

    def tap(self, name, m):
        return self.par[:, ds(m + PCOL[name], 1)]

    def act(self, act, m, b, turn, first):
        S, nc = self.S, self.nc
        w = self.parts[0][1]
        if b == 0 and not first:
            self.high(act, turn - 1)
        act.wait_ge(self.multiplied, m + 1)
        if not first:
            act.wait_ge(S["tap2"], m - 1)
            act.wait_ge(S["saved"], m - 1)
        u, acc = self.u[:, b], self.acc[:, b]
        if self.last:
            nc.scalar.activation(u[:, 2:2 + w], acc[:, 0, 0:w], ACT.Copy)
            nc.scalar.activation(u[:, 2 + w:2 + self.prompt], acc[:, 1, 0:self.prompt - w], ACT.Copy)
            ins = nc.scalar.activation(self.samples(u)[:, :, 2:],
                                       acc[:, 1, self.prompt - w:w].rearrange("p (n t) -> p n t", t=NT), ACT.Copy)
        else:
            ins = nc.scalar.activation(u[:, 2:].rearrange("p (n t) -> p n t", t=w), acc[:, :, 0:w], ACT.Copy)
        ins.then_inc(self.drained, 1)
        act.wait_ge(self.drained, m + 1)
        act.wait_ge(S["led"], m + 1)
        if not first:
            act.wait_ge(S["gated"], turn)
        n = self.wide - 2
        nc.scalar.activation(self.c[:, b], u[:, 0:n], ACT.Identity, bias=self.tap("cb", m),
                             scale=self.tap("cw0", m)).then_inc(S["tap0"], 1)
        if b == 1:
            act.wait_ge(S["tap2"], m)
            nc.scalar.activation(self.ge[:], self.c[:, 0], ACT.Gelu_apprx_tanh).then_inc(S["gelued"], 1)

    def high(self, act, turn):
        act.wait_ge(self.S["gated"], turn + 1)
        if not isinstance(turn, int) or turn > 0:
            act.wait_ge(self.S["g_low"], turn)
        self.nc.scalar.activation(self.Gh[:, ds(turn, 1), :].rearrange("p a t -> p (a t)"), self.g[:],
                                  ACT.Copy).then_inc(self.S["g_high"], 1)

    def act_end(self, act, ntiles):
        self.high(act, ntiles // 2 - 1)

    def low(self, dve, turn):
        dve.wait_ge(self.S["g_high"], turn + 1)
        gh, gl = (z[:, ds(turn, 1), :].rearrange("p a t -> p (a t)") for z in (self.Gh, self.Gl))
        self.nc.vector.tensor_tensor(gl, self.g[:], gh.bitcast(F32), ALU.subtract).then_inc(self.S["g_low"], 1)

    def dve(self, dve, m, b, turn, first):
        S, nc, n = self.S, self.nc, self.wide - 2
        if b == 0 and not first:
            self.low(dve, turn - 1)
        c, u = self.c[:, b], self.u[:, b]
        for k in (1, 2):
            dve.wait_ge(S[f"tap{k - 1}"], m + 1)
            nc.vector.scalar_tensor_tensor(c, u[:, k:k + n], self.tap(f"cw{k}", m), c, ALU.mult,
                                           ALU.add).then_inc(S[f"tap{k}"], 1)
        one = lambda z: z[:, ds(m, 1)].rearrange("p a t -> p (a t)")
        end = u[:, self.prompt:self.prompt + 2]
        if self.last:
            nc.vector.tensor_scalar(one(self.conv_out)[:, 0:2], end, 1.0, None, ALU.mult)
            nc.vector.tensor_scalar(one(self.conv_out)[:, 2:].rearrange("p (n t) -> p n t", t=2),
                                    self.samples(u)[:, :, NT:NT + 2], 1.0, None, ALU.mult).then_inc(S["saved"], 1)
        else:
            nc.vector.tensor_scalar(one(self.carry), end, 1.0, None, ALU.mult).then_inc(S["saved"], 1)
        if b == 1:
            dve.wait_ge(S["gelued"], turn + 1)
            dve.wait_ge(S["tap2"], m + 1)
            if not first:
                dve.wait_ge(S["g_low"], turn)
            g, ge, v = self.g, self.ge, self.c[:, 1]
            q = self.prompt
            if self.last:
                new = lambda z: z[:, 2 + q:2 + q + NB * (2 + NT) - 2]
                nc.vector.tensor_tensor(g[:, 0:q], ge[:, 0:q], v[:, 0:q], ALU.mult)
                at = lambda z: z[:, 2 + q:2 + q + (NB - 1) * (2 + NT)].rearrange("p (n t) -> p n t", t=2 + NT)
                nc.vector.tensor_tensor(g[:, q:TH - NT].rearrange("p (n t) -> p n t", t=NT), at(ge)[:, :, 0:NT],
                                        at(v)[:, :, 0:NT], ALU.mult)
                end = 2 + q + (NB - 1) * (2 + NT)
                ins = nc.vector.tensor_tensor(g[:, TH - NT:TH], ge[:, end:end + NT], v[:, end:end + NT], ALU.mult)
            else:
                ins = nc.vector.tensor_tensor(g[:], ge[:], v, ALU.mult)
            ins.then_inc(S["gated"], 1)

    def dve_end(self, dve, ntiles):
        self.low(dve, ntiles // 2 - 1)
        dve.wait_ge(self.S["g_low"], ntiles // 2)
        dve.wait_ge(self.S["saved"], ntiles)

    def pool(self, pool, m, b, turn, first):
        S, nc = self.S, self.nc
        if not first:
            pool.wait_ge(S["tap2"], m - 1)
            pool.wait_ge(S["saved"], m - 1)
        u = self.u[:, b]
        one = lambda z: z[:, ds(m, 1)]
        ins = nc.gpsimd.tensor_copy(u[:, 0:2], one(self.carry).rearrange("p a t -> p (a t)"))
        if self.last:
            ins = nc.gpsimd.tensor_copy(self.samples(u)[:, :, 0:2],
                                        one(self.states).rearrange("p a (n t) -> p (a n) t", t=2))
        ins.then_inc(S["led"], 1)


def run_tiles(eng, ntiles, step, trail=None):
    peeled = min(2 if trail else 1, ntiles // 2)
    for m in range(2 * peeled):
        step(m, m % 2, m // 2, m < 2)
        if trail and m >= 1:
            trail(m - 1, (m - 1) % 2, (m - 1) // 2, m - 1 < 2)
    if ntiles > 2 * peeled:
        with eng.Fori(peeled, ntiles // 2) as i:
            step(i * 2, 0, i, False)
            if trail:
                trail(i * 2 - 1, 1, i - 1, False)
            step(i * 2 + 1, 1, i, False)
            if trail:
                trail(i * 2, 0, i, False)
    if trail:
        trail(ntiles - 1, 1, ntiles // 2 - 1, ntiles == 2)


def project(kit, name, ntiles, kt, units, w_dram, Xh, Xl, parts, make_evac):
    nc = kit.nc
    rounded, residued, multiplied, drained = (kit.sem(f"{name}_{s}") for s in
                                              ("rounded", "residued", "multiplied", "drained"))
    fetched = [kit.sem(f"{name}_fetched{b}") for b in range(2)]
    passes = 3
    with ExitStack() as ctx:
        raw = kit.sb(ctx, name + "_raw", [P, 2, kt, P])
        wh = kit.sb(ctx, name + "_wh", [P, 2, kt, P], F32R)
        wl = kit.sb(ctx, name + "_wl", [P, 2, kt, P], F32R)
        acc = kit.ps(ctx, name + "_acc", [P, 2, len(parts), 512])
        ev = make_evac(ctx)
        ev.multiplied, ev.drained, ev.acc, ev.units = multiplied, drained, acc, units
        ev.name = name
        block = ctx.enter_context(nc.Block())

        def each_unit(m, b, turn):
            for u in range(units):
                local = b * units + u
                yield m * units + u, local % 2, turn * units + local // 2, u

        @block.sync
        def _(sp):
            def fetch(m, b, turn, first):
                for j, buf, use, u in each_unit(m, b, turn):
                    if not (isinstance(j, int) and j < 2):
                        sp.wait_ge(residued, j - 1)
                    src = w_dram[j] if isinstance(j, int) else w_dram[ds(j, 1)].rearrange("a p n -> (a p) n")
                    sp.dma_start(raw[:, buf].rearrange("p k m -> p (k m)"), src).then_inc(fetched[buf], 16)
            run_tiles(sp, ntiles, fetch)

        @block.scalar
        def _(act):
            def round_up(m, b, turn, first):
                for j, buf, use, u in each_unit(m, b, turn):
                    act.wait_ge(fetched[buf], (use + 1) * 16)
                    if not (isinstance(j, int) and j < 2):
                        act.wait_ge(multiplied, j - 1)
                    nc.scalar.activation(wh[:, buf], raw[:, buf], ACT.Copy).then_inc(rounded, 1)

            run_tiles(act, ntiles, round_up,
                      lambda m, b, turn, first: ev.act(act, m, b, turn, first))
            if hasattr(ev, "act_end"):
                ev.act_end(act, ntiles)

        @block.vector
        def _(dve):
            def residue(m, b, turn, first):
                for j, buf, use, u in each_unit(m, b, turn):
                    dve.wait_ge(rounded, j + 1)
                    nc.vector.tensor_tensor(wl[:, buf], raw[:, buf], wh[:, buf].bitcast(F32),
                                            ALU.subtract).then_inc(residued, 1)
            trail = (lambda m, b, turn, first: ev.dve(dve, m, b, turn, first)) if hasattr(ev, "dve") else None
            run_tiles(dve, ntiles, residue, trail)
            if hasattr(ev, "dve_end"):
                ev.dve_end(dve, ntiles)

        @block.tensor
        def _(pe):
            def multiply(m, b, turn, first):
                for j, buf, use, u in each_unit(m, b, turn):
                    pe.wait_ge(residued, j + 1)
                    if u == 0 and not first:
                        pe.wait_ge(drained, m - 1)
                    for n, (at, size) in enumerate(parts):
                        for k in range(kt):
                            for q, (w, x) in enumerate(((wh, Xh), (wh, Xl), (wl, Xh))):
                                last = nc.tensor.matmul(acc[:, b, n, 0:size], w[:, buf, k, :],
                                                        x[:, u * kt + k, at:at + size],
                                                        start=(u == 0 and k == 0 and q == 0),
                                                        stop=(u == units - 1 and k == kt - 1 and q == passes - 1))
                    last.then_inc(multiplied, 1)
            run_tiles(pe, ntiles, multiply)

        if hasattr(ev, "pool"):
            @block.gpsimd
            def _(pool):
                run_tiles(pool, ntiles, lambda m, b, turn, first: ev.pool(pool, m, b, turn, first))
                if hasattr(ev, "pool_end"):
                    ev.pool_end(pool, ntiles)


def attend_prompt(kit, proj, oT, ident, identb, causal, neg_lam):
    nc = kit.nc
    NQ = SEQ // P
    names = ("qkv_in", "v_turned", "v_kept", "scored", "peaked", "biased", "exped", "inverted", "coefd",
             "w_first", "weighted", "turned", "kept", "summed", "evacuated", "head_out")
    S = {n: kit.sem("ap_" + n) for n in names}
    SCALE = DH ** -0.5
    with ExitStack() as ctx:
        qkv = kit.sb(ctx, "ap_qkv", [P, 3, SEQ])
        vt = kit.sb(ctx, "ap_vt", [P, NQ, P])
        pexp = kit.sb(ctx, "ap_pexp", [P, 2, 2, SEQ])
        wgt = kit.sb(ctx, "ap_wgt", [P, 2, SEQ])
        wT = kit.sb(ctx, "ap_wT", [P, 2, NQ, P])
        small = kit.sb(ctx, "ap_small", [P, 2, 10])
        out = kit.sb(ctx, "ap_out", [P, SEQ])
        sc = kit.ps(ctx, "ap_sc", [P, 2, SEQ])
        tp = kit.ps(ctx, "ap_tp", [P, NQ, P])
        pv = kit.ps(ctx, "ap_pv", [P, 2, 512])
        block = ctx.enter_context(nc.Block())

        @block.sync
        def _(sp):
            def head(h, first):
                if not first:
                    sp.wait_ge(S["summed"], h * NQ)
                    sp.wait_ge(S["v_turned"], h)
                for j in range(3):
                    src = proj[j * HEADS + h] if first else proj[ds(h + j * HEADS, 1)].rearrange("a p t -> (a p) t")
                    sp.dma_start(qkv[:, j], src[:, 0:SEQ]).then_inc(S["qkv_in"], 16)
                sp.wait_ge(S["evacuated"], (h + 1) * NQ)
                dst = oT[h] if first else oT[ds(h, 1)].rearrange("a p t -> (a p) t")
                sp.dma_start(dst[:, 0:SEQ], out[:]).then_inc(S["head_out"], 16)
            head(0, True)
            with sp.Fori(1, HEADS) as h:
                head(h, False)
            sp.wait_ge(S["head_out"], 16 * HEADS)

        @block.tensor
        def _(pe):
            def back(h, i, first):
                s = h * NQ + i
                pe.wait_ge(S["weighted"], s + 1)
                if not (first and i == 0):
                    pe.wait_ge(S["kept"], s)
                for j in range(i + 1):
                    last = nc.tensor.transpose(tp[:, j, :], wgt[:, i % 2, j * P:(j + 1) * P], ident)
                last.then_inc(S["turned"], 1)
                if i == 0:
                    pe.wait_ge(S["v_kept"], h + 1)
                pe.wait_ge(S["kept"], s + 1)
                if not (first and i < 2):
                    pe.wait_ge(S["evacuated"], s - 1)
                for j in range(i + 1):
                    last = nc.tensor.matmul(pv[:, i % 2, 0:P], vt[:, j, :], wT[:, i % 2, j, :],
                                            start=(j == 0), stop=(j == i))
                last.then_inc(S["summed"], 1)

            def head(h, first):
                pe.wait_ge(S["qkv_in"], (h + 1) * 48)
                if not first:
                    pe.wait_ge(S["kept"], h * NQ)
                for j in range(NQ):
                    last = nc.tensor.transpose(tp[:, j, :], qkv[:, 2, j * P:(j + 1) * P], ident)
                last.then_inc(S["v_turned"], 1)
                for i in range(NQ):
                    s = h * NQ + i
                    if not (first and i == 0):
                        pe.wait_ge(S["exped"], 2 * s)
                    keys = (i + 1) * P
                    for c in range(2):
                        rows = slice(c * DH, (c + 1) * DH)
                        for at in range(0, keys, 512):
                            n = min(512, keys - at)
                            diag = at + n == keys
                            last = nc.tensor.matmul(sc[:, c, at:at + n], qkv[rows, 0, i * P:(i + 1) * P],
                                                    qkv[rows, 1, at:at + n], start=True, stop=not diag)
                            if diag:
                                last = nc.tensor.matmul(sc[:, c, i * P:keys], identb, causal,
                                                        start=False, stop=True)
                    last.then_inc(S["scored"], 1)
                    if i == 0:
                        pe.wait_ge(S["v_kept"], h + 1)
                    if i >= 1:
                        back(h, i - 1, first)
                back(h, NQ - 1, first)

            head(0, True)
            with pe.Fori(1, HEADS) as h:
                head(h, False)

        @block.vector
        def _(dve):
            def head(h, first):
                for i in range(NQ):
                    s, b, keys = h * NQ + i, i % 2, (i + 1) * P
                    dve.wait_ge(S["scored"], s + 1)
                    nc.vector.tensor_reduce(small[:, b, 0:2], sc[:, :, 0:keys], AX, ALU.max).then_inc(S["peaked"], 1)
                    dve.wait_ge(S["peaked"], s + 1)
                    nc.vector.tensor_scalar(small[:, b, 2:4], small[:, b, 0:2], -SCALE, None,
                                            ALU.mult).then_inc(S["biased"], 1)
                    dve.wait_ge(S["exped"], 2 * s + 2)
                    nc.vector.reciprocal(small[:, b, 6:8], small[:, b, 4:6]).then_inc(S["inverted"], 1)
                    dve.wait_ge(S["inverted"], s + 1)
                    nc.vector.tensor_scalar(small[:, b, 8:9], small[:, b, 7:8], neg_lam, None,
                                            ALU.mult).then_inc(S["coefd"], 1)
                    if not (first and i < 2):
                        dve.wait_ge(S["turned"], s - 1)
                    nc.vector.tensor_scalar(wgt[:, b, 0:keys], pexp[:, b, 0, 0:keys], small[:, b, 6:7], None,
                                            ALU.mult).then_inc(S["w_first"], 1)
                    dve.wait_ge(S["coefd"], s + 1)
                    dve.wait_ge(S["w_first"], s + 1)
                    nc.vector.scalar_tensor_tensor(wgt[:, b, 0:keys], pexp[:, b, 1, 0:keys], small[:, b, 8:9],
                                                   wgt[:, b, 0:keys], ALU.mult, ALU.add).then_inc(S["weighted"], 1)
            head(0, True)
            with dve.Fori(1, HEADS) as h:
                head(h, False)

        @block.scalar
        def _(act):
            def keep(h, i, first):
                s, b = h * NQ + i, i % 2
                act.wait_ge(S["turned"], s + 1)
                if not (first and i < 2):
                    act.wait_ge(S["summed"], s - 1)
                nc.scalar.activation(wT[:, b, 0:i + 1, :], tp[:, 0:i + 1, :], ACT.Copy).then_inc(S["kept"], 1)

            def leave(h, i, first):
                s = h * NQ + i
                act.wait_ge(S["summed"], s + 1)
                if not first and i == 0:
                    act.wait_ge(S["head_out"], 16 * h)
                nc.scalar.activation(out[:, i * P:(i + 1) * P], pv[:, i % 2, 0:P],
                                     ACT.Copy).then_inc(S["evacuated"], 1)

            def head(h, first):
                act.wait_ge(S["v_turned"], h + 1)
                if not first:
                    act.wait_ge(S["summed"], h * NQ)
                nc.scalar.activation(vt[:], tp[:], ACT.Copy).then_inc(S["v_kept"], 1)
                for i in range(NQ):
                    s, b, keys = h * NQ + i, i % 2, (i + 1) * P
                    act.wait_ge(S["biased"], s + 1)
                    if not (first and i < 2):
                        act.wait_ge(S["weighted"], s - 1)
                    for c in range(2):
                        nc.scalar.activation(pexp[:, b, c, 0:keys], sc[:, c, 0:keys], ACT.Exp,
                                             bias=small[:, b, 2 + c:3 + c], scale=SCALE,
                                             accum_out=small[:, b, 4 + c:5 + c]).then_inc(S["exped"], 1)
                    if i >= 1:
                        keep(h, i - 1, first)
                        leave(h, i - 1, first)
                keep(h, NQ - 1, first)
                leave(h, NQ - 1, first)
            head(0, True)
            with act.Fori(1, HEADS) as h:
                head(h, False)


def attend_sample(kit, a, proj, oT, ident, identb, neg_lam_rows):
    nc = kit.nc
    SCALE = DH ** -0.5
    W = PAGES * PAGE + NS
    names = ("table_in", "small_in", "q_zeroed", "q_placed", "v_turned", "v_kept", "scored", "peaked", "biased",
             "exped", "inverted", "scaled", "combined", "turned", "kept", "summed", "evacuated", "stored", "q_picked")
    S = {n: kit.sem("as_" + n) for n in names}
    k_in = [kit.sem(f"as_k_in{b}") for b in range(2)]
    v_in = [kit.sem(f"as_v_in{b}") for b in range(2)]
    with ExitStack() as ctx:
        table = kit.sb(ctx, "as_table", [1, NB * PAGES], I32)
        qkv = kit.sb(ctx, "as_qkv", [P, 3, HEADS, NS])
        qd = kit.sb(ctx, "as_qd", [P, NB, HEADS, 32])
        qb = kit.sb(ctx, "as_qb", [P, 2, HEADS, 32])
        vnew = kit.sb(ctx, "as_vnew", [NS, HEADS, P])
        mask = kit.sb(ctx, "as_mask", [P, NB * NS], BF16)
        comb = kit.sb(ctx, "as_comb", [P, 18])
        kT = kit.sb(ctx, "as_kT", [P, 2, PAGES, HEADS, PAGE])
        vp = kit.sb(ctx, "as_vp", [P, 2, PAGES, HEADS * P])
        pexp = kit.sb(ctx, "as_pexp", [P, 2, W])
        small = kit.sb(ctx, "as_small", [P, 2, 6])
        combs = kit.sb(ctx, "as_combs", [P, 2, 16])
        wT = kit.sb(ctx, "as_wT", [P, 2, PAGES + 1, 16])
        out = kit.sb(ctx, "as_out", [P, HEADS, NS])
        sc = kit.ps(ctx, "as_sc", [P, 3 * 512])
        tp = kit.ps(ctx, "as_tp", [P, 512])
        pv = kit.ps(ctx, "as_pv", [P, 512])
        vps = kit.ps(ctx, "as_vps", [P, 512])
        block = ctx.enter_context(nc.Block())

        def pages(eng, n, b, dst, pool_dram, arrived):
            for j in range(PAGES):
                page = eng.value_load(table[0:1, ds(n * PAGES + j, 1)], min_val=0, max_val=POOL - 1)
                eng.dma_start(dst[:, b, j].rearrange("p h c -> p (h c)") if len(dst.shape) == 5 else dst[:, b, j],
                              pool_dram[ds(page, 1)].rearrange("a p n -> (a p) n")).then_inc(arrived[b], 16)

        @block.sync
        def _(sp):
            sp.dma_start(table[:], a["table"]).then_inc(S["table_in"], 16)
            for j in range(3):
                sp.dma_start(qkv[:, j], proj[j * HEADS:(j + 1) * HEADS, :, SEQ:T].rearrange("h p t -> p h t"))\
                    .then_inc(S["small_in"], 16)
            sp.dma_start(mask[:], a["new_mask"]).then_inc(S["small_in"], 16)
            sp.dma_start(comb[:, 0:17], a["comb"]).then_inc(S["small_in"], 16)
            sp.wait_ge(S["table_in"], 16)
            pages(sp, 0, 0, kT, a["k_pool"], k_in)
            pages(sp, 1, 1, kT, a["k_pool"], k_in)
            with sp.Fori(1, NB // 2) as i:
                for b in range(2):
                    sp.wait_ge(S["scored"], i * 2 + b - 1)
                    pages(sp, i * 2 + b, b, kT, a["k_pool"], k_in)
            sp.wait_ge(S["evacuated"], NB)
            sp.dma_start(oT.rearrange("h p t -> p h t")[:, :, SEQ:T], out[:]).then_inc(S["stored"], 16)
            sp.wait_ge(S["stored"], 16)

        @block.gpsimd
        def _(pool):
            nc.gpsimd.memset(qd[:], 0.0).then_inc(S["q_zeroed"], 1)
            pool.wait_ge(S["small_in"], 16 * 5)
            pool.wait_ge(S["q_zeroed"], 1)
            for c in range(2):
                rows = slice(c * DH, (c + 1) * DH)
                for h in range(HEADS):
                    nc.gpsimd.tensor_copy(qd[rows, :, h, c * NT:(c + 1) * NT],
                                          qkv[rows, 0, h, :].rearrange("p (n t) -> p n t", t=NT))\
                        .then_inc(S["q_placed"], 1)
            pool.wait_ge(S["q_placed"], 2 * HEADS)

            def pick(n, b, first):
                if not first:
                    pool.wait_ge(S["scored"], n - 1)
                nc.gpsimd.tensor_copy(qb[:, b], qd[:, ds(n, 1)].rearrange("p a h c -> p (a h) c"))\
                    .then_inc(S["q_picked"], 1)
            pick(0, 0, True)
            pick(1, 1, True)
            with pool.Fori(1, NB // 2) as i:
                for b in range(2):
                    pick(i * 2 + b, b, False)

        @block.tensor
        def _(pe):
            pe.wait_ge(S["small_in"], 16 * 5)
            for h in range(HEADS):
                last = nc.tensor.transpose(vps[0:NS, h * P:(h + 1) * P], qkv[:, 2, h, :], ident)
            last.then_inc(S["v_turned"], 1)
            pe.wait_ge(S["v_kept"], 1)

            def back(n, b, turn, first):
                pe.wait_ge(S["combined"], n + 1)
                if not first:
                    pe.wait_ge(S["kept"], n)
                for j in range(PAGES + 1):
                    keys = PAGE if j < PAGES else NS
                    last = nc.tensor.matmul(tp[0:keys, j * 16:(j + 1) * 16],
                                            pexp[:, b, j * PAGE:j * PAGE + keys], combs[:, b, :],
                                            start=True, stop=True)
                last.then_inc(S["turned"], 1)
                pe.wait_ge(v_in[b], (turn + 1) * 16 * PAGES)
                pe.wait_ge(S["kept"], n + 1)
                if not first:
                    pe.wait_ge(S["evacuated"], n)
                for h in range(HEADS):
                    for j in range(PAGES + 1):
                        if j < PAGES:
                            v, w = vp[:, b, j, h * P:(h + 1) * P], wT[:, b, j, h * NT:(h + 1) * NT]
                        else:
                            v, w = vnew[:, h, :], wT[0:NS, b, j, h * NT:(h + 1) * NT]
                        last = nc.tensor.matmul(pv[:, h * NT:(h + 1) * NT], v, w, start=(j == 0), stop=(j == PAGES))
                last.then_inc(S["summed"], 1)

            def front(n, b, turn, first):
                pe.wait_ge(k_in[b], (turn + 1) * 16 * PAGES)
                pe.wait_ge(S["q_picked"], n + 1)
                if not (isinstance(n, int) and n == 0):
                    pe.wait_ge(S["exped"], n)
                for h in range(HEADS):
                    rows = slice(32 * h, 32 * h + 32)
                    for half in range(2):
                        last = nc.tensor.matmul(sc[rows, half * 512:(half + 1) * 512], qb[:, b, h, :],
                                                kT[:, b, half * 4:half * 4 + 4, h, :], start=True, stop=True)
                    last = nc.tensor.matmul(sc[rows, 1024:W], qb[:, b, h, :], qkv[:, 1, h, :],
                                            start=True, stop=False, skip_group_check=True)
                nc.tensor.matmul(sc[:, 1024:W], identb, mask[:, ds(n * NS, NS)], start=False, stop=True,
                                 skip_group_check=True).then_inc(S["scored"], 1)

            front(0, 0, 0, True)
            front(1, 1, 0, True)
            back(0, 0, 0, True)
            front(2, 0, 1, False)
            back(1, 1, 0, False)
            front(3, 1, 1, False)
            back(2, 0, 1, False)
            with pe.Fori(2, NB // 2) as i:
                front(i * 2, 0, i, False)
                back(i * 2 - 1, 1, i - 1, False)
                front(i * 2 + 1, 1, i, False)
                back(i * 2, 0, i, False)
            back(NB - 1, 1, NB // 2 - 1, False)

        @block.vector
        def _(dve):
            dve.wait_ge(S["v_turned"], 1)
            nc.vector.tensor_copy(vnew[:].rearrange("p h c -> p (h c)"), vps[0:NS, :]).then_inc(S["v_kept"], 1)

            def front(n, b, first):
                dve.wait_ge(S["scored"], n + 1)
                nc.vector.tensor_reduce(small[:, b, 0:1], sc[:, 0:W], AX, ALU.max).then_inc(S["peaked"], 1)
                dve.wait_ge(S["peaked"], n + 1)
                nc.vector.tensor_scalar(small[:, b, 1:2], small[:, b, 0:1], -SCALE, None,
                                        ALU.mult).then_inc(S["biased"], 1)
                dve.wait_ge(S["exped"], n + 1)
                nc.vector.reciprocal(small[:, b, 3:4], small[:, b, 2:3]).then_inc(S["inverted"], 1)
                dve.wait_ge(S["inverted"], n + 1)
                nc.vector.tensor_scalar(small[:, b, 4:5], small[:, b, 3:4], neg_lam_rows, None,
                                        ALU.mult).then_inc(S["scaled"], 1)
                dve.wait_ge(S["scaled"], n + 1)
                if not first:
                    dve.wait_ge(S["turned"], n - 1)
                nc.vector.tensor_scalar(combs[:, b, :], comb[:, 0:16], small[:, b, 4:5], None,
                                        ALU.mult).then_inc(S["combined"], 1)

            def back(n, b, first):
                dve.wait_ge(S["turned"], n + 1)
                if not first:
                    dve.wait_ge(S["summed"], n - 1)
                nc.vector.tensor_copy(wT[:, b, 0:PAGES, :], tp[:, 0:PAGES * 16].rearrange("p (j c) -> p j c", c=16))
                nc.vector.tensor_copy(wT[0:NS, b, PAGES, :], tp[0:NS, PAGES * 16:(PAGES + 1) * 16])\
                    .then_inc(S["kept"], 1)
                dve.wait_ge(S["summed"], n + 1)
                nc.vector.tensor_copy(out[:, :, ds(n * NT, NT)],
                                      pv[:, 0:HEADS * NT].rearrange("p (h t) -> p h t", t=NT))\
                    .then_inc(S["evacuated"], 1)
            front(0, 0, True)
            front(1, 1, True)
            back(0, 0, True)
            front(2, 0, False)
            back(1, 1, True)
            front(3, 1, False)
            back(2, 0, False)
            with dve.Fori(2, NB // 2) as i:
                front(i * 2, 0, False)
                back(i * 2 - 1, 1, False)
                front(i * 2 + 1, 1, False)
                back(i * 2, 0, False)
            back(NB - 1, 1, False)

        @block.scalar
        def _(act):
            act.wait_ge(S["table_in"], 16)
            pages(act, 0, 0, vp, a["v_pool"], v_in)
            pages(act, 1, 1, vp, a["v_pool"], v_in)

            def step(n, b, first):
                act.wait_ge(S["biased"], n + 1)
                if not first:
                    act.wait_ge(S["turned"], n - 1)
                nc.scalar.activation(pexp[:, b, :], sc[:, 0:W], ACT.Exp, bias=small[:, b, 1:2], scale=SCALE,
                                     accum_out=small[:, b, 2:3]).then_inc(S["exped"], 1)
            step(0, 0, True)
            step(1, 1, True)
            with act.Fori(1, NB // 2) as i:
                for b in range(2):
                    act.wait_ge(S["summed"], i * 2 + b - 1)
                    pages(act, i * 2 + b, b, vp, a["v_pool"], v_in)
                    step(i * 2 + b, b, False)

NPAIR = 4
NSTEP = 6
NLEV = 6


def rwkv_mix(kit, ctx, a, proj, param, dsts):
    nc = kit.nc
    S = {n: kit.sem("mx_" + n) for n in ("state_in", "differed", "mixed")}
    cur_in = [kit.sem(f"mx_cur_in{b}") for b in range(2)]
    with ExitStack() as inner:
        cur = kit.sb(inner, "mx_cur", [P, 2, T])
        dif = kit.sb(inner, "mx_dif", [P, 2, T])
        st = kit.sb(inner, "mx_st", [P, 14, NB])
        block = inner.enter_context(nc.Block())

        @block.sync
        def _(sp):
            sp.dma_start(st[:], a["shiftT"]).then_inc(S["state_in"], 16)
            for j in range(14):
                if j >= 2:
                    sp.wait_ge(S["mixed"], j - 1)
                sp.dma_start(cur[:, j % 2], proj[12 + j]).then_inc(cur_in[j % 2], 16)

        @block.gpsimd
        def _(pool):
            pool.wait_ge(S["state_in"], 16)
            for j in range(14):
                b = j % 2
                pool.wait_ge(cur_in[b], 16 * (j // 2 + 1))
                if j >= 2:
                    pool.wait_ge(S["mixed"], j - 1)
                c, d = cur[:, b], dif[:, b]
                cs, dd = (z[:, SEQ:].rearrange("p (n t) -> p n t", t=NT) for z in (c, d))
                nc.gpsimd.tensor_tensor(d[:, 1:SEQ], c[:, 0:SEQ - 1], c[:, 1:SEQ], ALU.subtract).then_inc(S["differed"], 1)
                nc.gpsimd.tensor_scalar(d[:, 0:1], c[:, 0:1], -1.0, None, ALU.mult).then_inc(S["differed"], 1)
                nc.gpsimd.tensor_tensor(dd[:, :, 1:NT], cs[:, :, 0:NT - 1], cs[:, :, 1:NT],
                                        ALU.subtract).then_inc(S["differed"], 1)
                nc.gpsimd.tensor_tensor(dd[:, :, 0], st[:, j, :], cs[:, :, 0], ALU.subtract).then_inc(S["differed"], 1)

        @block.vector
        def _(dve):
            for j in range(14):
                dve.wait_ge(S["differed"], 4 * (j + 1))
                nc.vector.scalar_tensor_tensor(dsts[j], dif[:, j % 2], param("mu", 14)[:, j:j + 1], cur[:, j % 2],
                                               ALU.mult, ALU.add).then_inc(S["mixed"], 1)
            dve.wait_ge(S["mixed"], 14)


def rwkv_prepare(kit, ctx, a, param, Rm, Km, V, X12, XG, NR, Bc, Kc, BON, G, ELC, SD):
    nc = kit.nc
    names = ("w_in", "kaed", "tanhed", "z", "za", "g", "ss", "rks", "th", "ta", "g_kept", "rooted", "e_in",
             "e_ex", "e_neg", "lw", "av", "kk", "sq", "ssm", "inv", "kn", "bv", "fv", "kp", "rk", "rk2", "bonus",
             "lin", "lex", "nr0", "nr1", "bc", "kc", "elc", "sd", "sdw", "xg1", "xg2")
    S = {n: kit.sem("rp_" + n) for n in names}
    with ExitStack() as inner:
        w2 = kit.sb(inner, "rp_w2", [P, 512])
        g2 = kit.sb(inner, "rp_g2", [P, 512])
        blk = kit.sb(inner, "rp_blk", [P, P])
        reset = kit.sb(inner, "rp_reset", [P, SEQ], BF16)
        hc = kit.sb(inner, "rp_hc", [P, 12])
        tw = kit.sb(inner, "rp_tw", [P, T])
        tv = kit.sb(inner, "rp_tv", [P, T])
        ta = kit.sb(inner, "rp_ta", [P, T])
        tk = kit.sb(inner, "rp_tk", [P, T])
        tq = kit.sb(inner, "rp_tq", [P, T])
        tl = kit.sb(inner, "rp_tl", [P, 2, SEQ])
        te = kit.sb(inner, "rp_te", [P, 3, SEQ])
        pz = kit.ps(inner, "rp_pz", [P, 3, 512])
        pq = kit.ps(inner, "rp_pq", [P, 3, 512])
        block = inner.enter_context(nc.Block())
        part = lambda z: z.rearrange("p (n t) -> p n t", t=T3)

        @block.sync
        def _(sp):
            for dst, src in ((w2[0:64, :], a["w2"]), (w2[64:128, :], a["a2"]), (g2[:], a["g2"]),
                             (blk[:], a["blockones"]), (reset[:], a["reset"])):
                sp.dma_start(dst, src).then_inc(S["w_in"], 16)

        @block.tensor
        def _(pe):
            def product(psum, lhsT, rhs, sem):
                for n in range(3):
                    last = nc.tensor.matmul(psum[:, n, 0:T3], lhsT, rhs[:, n * T3:(n + 1) * T3], start=True, stop=True)
                last.then_inc(S[sem], 1)
            pe.wait_ge(S["w_in"], 80)
            for p in range(NPAIR):
                cs = slice(p * P, (p + 1) * P)
                pe.wait_ge(S["tanhed"], 1)
                if p:
                    pe.wait_ge(S["bonus"], p)
                product(pz, w2[0:64, cs], X12[0:64, :], "z")
                if p:
                    pe.wait_ge(S["ssm"], p)
                product(pq, w2[64:128, cs], X12[64:128, :], "za")
                pe.wait_ge(S["th"], p + 1)
                pe.wait_ge(S["xg2"], 1)
                product(pz, g2[:, cs], XG, "g")
                pe.wait_ge(S["ta"], p + 1)
                pe.wait_ge(S["sq"], p + 1)
                product(pq, blk[:], tq, "ss")
                pe.wait_ge(S["g_kept"], p + 1)
                pe.wait_ge(S["rk2"], p + 1)
                product(pz, blk[:], tq, "rks")

        @block.scalar
        def _(act):
            nc.scalar.activation(X12[0:64, :], X12[0:64, :], ACT.Tanh).then_inc(S["tanhed"], 1)
            nc.scalar.activation(XG, XG, ACT.Tanh, scale=0.5).then_inc(S["xg1"], 1)
            act.wait_ge(S["kaed"], 3)
            for p in range(NPAIR):
                act.wait_ge(S["z"], p + 1)
                if p:
                    act.wait_ge(S["lw"], p)
                nc.scalar.activation(part(tw[:]), pz[:, :, 0:T3], ACT.Tanh, bias=hc[:, p:p + 1],
                                     scale=0.5).then_inc(S["th"], 1)
                act.wait_ge(S["za"], p + 1)
                if p:
                    act.wait_ge(S["fv"], p)
                    act.wait_ge(S["bv"], p)
                    act.wait_ge(S["sd"], 5 * p)
                nc.scalar.activation(part(ta[:]), pq[:, :, 0:T3], ACT.Tanh, bias=hc[:, 4 + p:5 + p],
                                     scale=0.5).then_inc(S["ta"], 1)
                act.wait_ge(S["g"], p + 1)
                nc.scalar.activation(part(G[:, p]), pz[:, :, 0:T3], ACT.Copy).then_inc(S["g_kept"], 1)
                act.wait_ge(S["lin"], p + 1)
                if p:
                    act.wait_ge(S["nr1"], p)
                    act.wait_ge(S["nr0"], p)
                    act.wait_ge(S["bc"], p)
                    act.wait_ge(S["kc"], p)
                    act.wait_ge(S["elc"], p)
                nc.scalar.activation(te[:, 0], tl[:, 0], ACT.Exp).then_inc(S["e_in"], 1)
                nc.scalar.activation(te[:, 2], tl[:, 0], ACT.Exp, scale=-1.0).then_inc(S["e_neg"], 1)
                act.wait_ge(S["lex"], p + 1)
                nc.scalar.activation(te[:, 1], tl[:, 1], ACT.Exp).then_inc(S["e_ex"], 1)
                nc.scalar.activation(SD[:, p, 0, :], tv[:, SEQ:T], ACT.Exp).then_inc(S["sdw"], 1)
                act.wait_ge(S["ssm"], p + 1)
                nc.scalar.activation(tq[:], tq[:], ACT.Sqrt).then_inc(S["rooted"], 1)

        @block.vector
        def _(dve):
            kap = param("k_a", 4)
            nc.vector.tensor_scalar(hc[:, 0:4], param("w0", 4), 0.5, None, ALU.mult).then_inc(S["kaed"], 1)
            nc.vector.tensor_scalar(hc[:, 4:8], param("a0", 4), 0.5, None, ALU.mult).then_inc(S["kaed"], 1)
            nc.vector.tensor_scalar(hc[:, 8:12], kap, -1.0, 1.0, ALU.mult, ALU.add).then_inc(S["kaed"], 1)
            dve.wait_ge(S["kaed"], 3)
            dve.wait_ge(S["xg1"], 1)
            nc.vector.tensor_scalar(XG, XG, 1.0, 0.5, ALU.add, ALU.mult).then_inc(S["xg2"], 1)
            dve.wait_ge(S["w_in"], 80)
            for p in range(NPAIR):
                col = lambda name: param(name, 4)[:, p:p + 1]
                r, k, v = Rm[:, p], Km[:, p], V[:, p]
                if p:
                    dve.wait_ge(S["kn"], p)
                    dve.wait_ge(S["bv"], p)
                    dve.wait_ge(S["nr0"], p)
                    dve.wait_ge(S["sd"], 5 * p)
                nc.vector.tensor_scalar(tk[:], k, col("k_k"), None, ALU.mult).then_inc(S["kk"], 1)
                dve.wait_ge(S["kk"], p + 1)
                if p:
                    dve.wait_ge(S["rks"], p)
                nc.vector.tensor_tensor(tq[:], tk[:], tk[:], ALU.mult).then_inc(S["sq"], 1)
                dve.wait_ge(S["th"], p + 1)
                if p:
                    dve.wait_ge(S["sdw"], p)
                nc.vector.tensor_scalar(tv[:], tw[:], 1.0, -E05 / 2, ALU.add, ALU.mult).then_inc(S["lw"], 1)
                dve.wait_ge(S["lw"], p + 1)
                if p:
                    dve.wait_ge(S["e_ex"], p)
                    dve.wait_ge(S["e_neg"], p)
                nc.vector.tensor_tensor_scan(tl[:, 0], reset[:], tv[:, 0:SEQ], 0.0, ALU.mult,
                                             ALU.add).then_inc(S["lin"], 1)
                dve.wait_ge(S["ta"], p + 1)
                nc.vector.tensor_scalar(ta[:], ta[:], 0.5, 0.5, ALU.mult, ALU.add).then_inc(S["av"], 1)
                dve.wait_ge(S["ss"], p + 1)
                nc.vector.tensor_scalar(part(tq[:]), pq[:, :, 0:T3], 1e-24, None, ALU.max).then_inc(S["ssm"], 1)
                dve.wait_ge(S["rooted"], p + 1)
                nc.vector.reciprocal(tq[:], tq[:]).then_inc(S["inv"], 1)
                dve.wait_ge(S["inv"], p + 1)
                nc.vector.tensor_tensor(tk[:], tk[:], tq[:], ALU.mult).then_inc(S["kn"], 1)
                dve.wait_ge(S["av"], p + 1)
                dve.wait_ge(S["kn"], p + 1)
                nc.vector.tensor_scalar(tq[:], ta[:], col("k_a"), hc[:, 8 + p:9 + p], ALU.mult,
                                        ALU.add).then_inc(S["fv"], 1)
                dve.wait_ge(S["fv"], p + 1)
                nc.vector.tensor_tensor(k, k, tq[:], ALU.mult).then_inc(S["kp"], 1)
                nc.vector.tensor_tensor(ta[:], tk[:], ta[:], ALU.mult).then_inc(S["bv"], 1)
                dve.wait_ge(S["kp"], p + 1)
                nc.vector.tensor_scalar(tq[:], r, col("r_k"), None, ALU.mult).then_inc(S["rk"], 1)
                dve.wait_ge(S["rk"], p + 1)
                nc.vector.tensor_tensor(tq[:], tq[:], k, ALU.mult).then_inc(S["rk2"], 1)
                dve.wait_ge(S["e_ex"], p + 1)
                nc.vector.scalar_tensor_tensor(NR[:, p, 0, :], tk[:, 0:SEQ], -1.0, te[:, 1], ALU.mult,
                                               ALU.mult).then_inc(S["nr0"], 1)
                dve.wait_ge(S["e_in"], p + 1)
                nc.vector.tensor_copy(ELC[:, p, :], te[:, 0].rearrange("p (c t) -> p c t", t=C)[:, :, C - 1])\
                    .then_inc(S["elc"], 1)
                dve.wait_ge(S["rks"], p + 1)
                nc.vector.tensor_tensor(part(BON[:, p]), pz[:, :, 0:T3], part(v), ALU.mult).then_inc(S["bonus"], 1)

        @block.gpsimd
        def _(pool):
            for p in range(NPAIR):
                r, k, v = Rm[:, p], Km[:, p], V[:, p]
                pool.wait_ge(S["lin"], p + 1)
                if p:
                    pool.wait_ge(S["e_ex"], p)
                nc.gpsimd.tensor_tensor(tl[:, 1], tl[:, 0], tv[:, 0:SEQ], ALU.subtract).then_inc(S["lex"], 1)
                pool.wait_ge(S["e_in"], p + 1)
                nc.gpsimd.tensor_tensor(NR[:, p, 1, :], r[:, 0:SEQ], te[:, 0], ALU.mult).then_inc(S["nr1"], 1)
                pool.wait_ge(S["bv"], p + 1)
                pool.wait_ge(S["e_neg"], p + 1)
                nc.gpsimd.tensor_tensor(Bc[:, p], ta[:, 0:SEQ], te[:, 2], ALU.mult).then_inc(S["bc"], 1)
                pool.wait_ge(S["kp"], p + 1)
                nc.gpsimd.tensor_tensor(Kc[:, p], k[:, 0:SEQ], te[:, 2], ALU.mult).then_inc(S["kc"], 1)
                for q, src in ((1, tk[:]), (2, ta[:]), (3, k), (4, r), (5, v)):
                    nc.gpsimd.tensor_copy(SD[:, p, q, :], src[:, SEQ:T]).then_inc(S["sd"], 1)
            pool.wait_ge(S["sd"], 5 * NPAIR)


def rwkv_chunks(kit, a, NR, Bc, Kc, V, ELC, Y, state_out):
    nc = kit.nc
    names = ("const_in", "zeroed", "placed", "p12", "turn", "kept", "adi0", "adi", "m3", "m2", "m4",
             "u", "vbd", "vst", "tw", "tst", "wst", "wbd", "rhs", "rhs_kept", "sa", "sa_kept", "st", "st_sum", "st_new",
             "y", "y_kept", "state_out")
    S = {n: kit.sem("rc_" + n) for n in names}
    with ExitStack() as ctx:
        strict = kit.sb(ctx, "rc_strict", [P, 512])
        incl = kit.sb(ctx, "rc_incl", [P, 256])
        levbd = kit.sb(ctx, "rc_levbd", [P, NLEV, 512])
        levst = kit.sb(ctx, "rc_levst", [P, NLEV, 256])
        pairbd = kit.sb(ctx, "rc_pairbd", [P, 512])
        eyebd = kit.sb(ctx, "rc_eyebd", [P, 512])
        eyest = kit.sb(ctx, "rc_eyest", [P, 256])
        ident = kit.sb(ctx, "rc_ident", [P, P])
        bd = kit.sb(ctx, "rc_bd", [P, 4, NPAIR, P])
        turned = kit.sb(ctx, "rc_turned", [P, 3, NPAIR, P])
        adi = kit.sb(ctx, "rc_adi", [P, NPAIR, P])
        m2 = kit.sb(ctx, "rc_m2", [P, NPAIR, P])
        m3 = kit.sb(ctx, "rc_m3", [P, NPAIR, C])
        m4 = kit.sb(ctx, "rc_m4", [P, NPAIR, C])
        vbd = kit.sb(ctx, "rc_vbd", [P, NPAIR, P])
        vst = kit.sb(ctx, "rc_vst", [P, NPAIR, C])
        tst = kit.sb(ctx, "rc_tst", [P, NPAIR, C])
        wst = kit.sb(ctx, "rc_wst", [P, NPAIR, C])
        wbd = kit.sb(ctx, "rc_wbd", [P, NPAIR, P])
        rhs = kit.sb(ctx, "rc_rhs", [P, NPAIR, P])
        sa = kit.sb(ctx, "rc_sa", [P, NPAIR, P])
        state = kit.sb(ctx, "rc_state", [P, 2, NPAIR, P])
        tsum = kit.sb(ctx, "rc_tsum", [P, NPAIR, P])
        p1, p2, ptr, pu, ptw, prs, pst, py = (kit.ps(ctx, "rc_" + n, [P, NPAIR, P]) for n in
                                              ("p1", "p2", "ptr", "pu", "ptw", "prs", "pst", "py"))
        block = ctx.enter_context(nc.Block())
        flat = lambda z: z.rearrange("p a b -> p (a b)")
        four = lambda z: z.rearrange("p (a h c) -> p a h c", a=NPAIR, h=2)

        def spread(z):
            return z.unsqueeze(2).broadcast_to([P, NPAIR, 2, C])

        consts = ((strict, "strict"), (incl, "incl"), (levbd, "levbd"), (levst, "levst"), (pairbd, "pairbd"),
                  (eyebd, "eyebd"), (eyest, "eyest"), (ident, "ident"))

        @block.sync
        def _(sp):
            for dst, src in consts:
                sp.dma_start(dst[:], a[src]).then_inc(S["const_in"], 16)
            sp.wait_ge(S["st_new"], NPAIR * NCH)
            for h in range(2):
                rows = slice(h * C, (h + 1) * C)
                sp.dma_start(state_out[rows], state[rows, 0, :, h * C:(h + 1) * C]).then_inc(S["state_out"], 16)
            sp.wait_ge(S["state_out"], 32)

        @block.gpsimd
        def _(pool):
            nc.gpsimd.memset(bd[:], 0.0).then_inc(S["zeroed"], 1)
            nc.gpsimd.memset(state[:], 0.0).then_inc(S["zeroed"], 1)
            pool.wait_ge(S["zeroed"], 2)
            pool.wait_ge(S["const_in"], 16 * len(consts))

            def chunk(c, first):
                if not first:
                    pool.wait_ge(S["rhs"], c)
                    pool.wait_ge(S["turn"], 3 * c)
                for q, src in enumerate((Bc, Kc, V, NR[:, :, 0, :])):
                    for h in range(2):
                        rows = slice(h * C, (h + 1) * C)
                        nc.gpsimd.tensor_copy(bd[rows, q, :, h * C:(h + 1) * C],
                                              src[rows, :, ds(c * C, C)]).then_inc(S["placed"], 1)
                pool.wait_ge(S["adi0"], c + 1)
                nc.gpsimd.tensor_tensor(flat(adi[:]), flat(adi[:]), eyebd[:], ALU.add).then_inc(S["adi"], 1)
            chunk(0, True)
            with pool.Fori(1, NCH) as c:
                chunk(c, False)

        @block.tensor
        def _(pe):
            pe.wait_ge(S["const_in"], 16 * len(consts))

            def chunk(c, b, first, i):
                pe.wait_ge(S["placed"], 8 * c + 8)
                if not first:
                    pe.wait_ge(S["m3"], c)
                    pe.wait_ge(S["m4"], c)
                for q, dst in ((0, p1), (1, p2)):
                    for p in range(NPAIR):
                        last = nc.tensor.matmul(dst[:, p, :], bd[:, q, p, :], NR[:, p, :, ds(c * C, C)],
                                                start=True, stop=True)
                    last.then_inc(S["p12"], 1)
                for q in range(3):
                    if not (first and q == 0):
                        pe.wait_ge(S["kept"], 3 * c + q)
                    for p in range(NPAIR):
                        last = nc.tensor.transpose(ptr[:, p, :], bd[:, q, p, :], ident[:])
                    last.then_inc(S["turn"], 1)
                for lev in range(NLEV):
                    n = c * NLEV + lev
                    pe.wait_ge(S["adi"], c + 1)
                    if lev:
                        pe.wait_ge(S["tst"], c * NLEV + lev if lev > 1 else c * NLEV + 1)
                    if not (first and lev == 0):
                        pe.wait_ge(S["vbd"], n)
                        pe.wait_ge(S["vst"], n)
                    for p in range(NPAIR):
                        t = tst[:, p, :] if lev else eyest[:].rearrange("p (a c) -> p a c", c=C)[:, p, :]
                        last = nc.tensor.matmul(pu[:, p, 0:C], adi[:, p, :], t, start=True, stop=True)
                    last.then_inc(S["u"], 1)
                    pe.wait_ge(S["vbd"], n + 1)
                    pe.wait_ge(S["vst"], n + 1)
                    if not (first and lev == 0):
                        pe.wait_ge(S["wbd"], n)
                        pe.wait_ge(S["wst"], n)
                        pe.wait_ge(S["tst"], n)
                    for p in range(NPAIR):
                        w = wst[:, p, :] if lev else eyest[:].rearrange("p (a c) -> p a c", c=C)[:, p, :]
                        if lev < NLEV - 1:
                            tl = wbd[:, p, :] if lev else eyebd[:].rearrange("p (a c) -> p a c", c=P)[:, p, :]
                            nc.tensor.matmul(pu[:, p, C:P], tl, vst[:, p, :], start=True, stop=True)
                        last = nc.tensor.matmul(ptw[:, p, C:P], vbd[:, p, :], w, start=True, stop=True)
                    last.then_inc(S["tw"], 1)
                pe.wait_ge(S["m2"], c + 1)
                pe.wait_ge(S["kept"], 3 * c + 3)
                if not first:
                    pe.wait_ge(S["st_new"], NPAIR * c)
                    pe.wait_ge(S["sa_kept"], c)
                for p in range(NPAIR):
                    nc.tensor.matmul(prs[:, p, :], m2[:, p, :], turned[:, 2, p, :], start=True, stop=False)
                    last = nc.tensor.matmul(prs[:, p, :], bd[:, 3, p, :], state[:, b, p, :], start=False, stop=True)
                last.then_inc(S["rhs"], 1)
                pe.wait_ge(S["rhs_kept"], c + 1)
                pe.wait_ge(S["wbd"], (c + 1) * NLEV)
                for p in range(NPAIR):
                    last = nc.tensor.matmul(prs[:, p, :], wbd[:, p, :], rhs[:, p, :], start=True, stop=True)
                last.then_inc(S["sa"], 1)
                pe.wait_ge(S["sa_kept"], c + 1)
                for p in range(NPAIR):
                    nc.tensor.matmul(pst[:, p, :], turned[:, 0, p, :], sa[:, p, :], start=True, stop=False)
                    last = nc.tensor.matmul(pst[:, p, :], turned[:, 1, p, :], turned[:, 2, p, :], start=False, stop=True)
                last.then_inc(S["st"], 1)
                pe.wait_ge(S["m3"], c + 1)
                pe.wait_ge(S["m4"], c + 1)
                if not first:
                    pe.wait_ge(S["y_kept"], c)
                for p in range(NPAIR):
                    nc.tensor.matmul(py[:, p, 0:C], state[:, b, p, :], NR[:, p, 1, ds(c * C, C)], start=True, stop=False)
                    nc.tensor.matmul(py[:, p, 0:C], sa[:, p, :], m3[:, p, :], start=False, stop=False)
                    last = nc.tensor.matmul(py[:, p, 0:C], turned[:, 2, p, :], m4[:, p, :], start=False, stop=True)
                last.then_inc(S["y"], 1)
            chunk(0, 0, True, 0)
            chunk(1, 1, False, 0)
            with pe.Fori(1, NCH // 2) as i:
                chunk(i * 2, 0, False, i)
                chunk(i * 2 + 1, 1, False, i)

        @block.vector
        def _(dve):
            dve.wait_ge(S["const_in"], 16 * len(consts))
            dve.wait_ge(S["zeroed"], 2)

            def chunk(c, b, first):
                dve.wait_ge(S["p12"], 2 * c + 1)
                if not first:
                    dve.wait_ge(S["u"], c * NLEV)
                nc.vector.tensor_tensor(four(flat(adi[:])), spread(p1[:, :, 0:C]), four(strict[:]),
                                        ALU.mult).then_inc(S["adi0"], 1)
                if not first:
                    dve.wait_ge(S["y"], c)
                nc.vector.tensor_tensor(m3[:], p1[:, :, C:P], incl[:].rearrange("p (a c) -> p a c", c=C),
                                        ALU.mult).then_inc(S["m3"], 1)
                dve.wait_ge(S["p12"], 2 * c + 2)
                nc.vector.tensor_tensor(four(flat(m2[:])), spread(p2[:, :, 0:C]), four(strict[:]),
                                        ALU.mult).then_inc(S["m2"], 1)
                nc.vector.tensor_tensor(m4[:], p2[:, :, C:P], incl[:].rearrange("p (a c) -> p a c", c=C),
                                        ALU.mult).then_inc(S["m4"], 1)
                for lev in range(NLEV):
                    n = c * NLEV + lev
                    dve.wait_ge(S["u"], n + 1)
                    if not (first and lev == 0):
                        dve.wait_ge(S["tw"], n)
                    nc.vector.tensor_tensor(four(flat(vbd[:])), spread(pu[:, :, 0:C]), four(levbd[:, lev, :]),
                                            ALU.mult).then_inc(S["vbd"], 1)
                    nc.vector.tensor_tensor(vst[:], pu[:, :, 0:C], levst[:, lev, :].rearrange("p (a c) -> p a c", c=C),
                                            ALU.mult).then_inc(S["vst"], 1)
                    dve.wait_ge(S["wst"], n + 1)
                    if not first and lev == 0:
                        dve.wait_ge(S["sa"], c)
                    nc.vector.tensor_tensor(four(flat(wbd[:])), spread(wst[:]), four(pairbd[:]),
                                            ALU.mult).then_inc(S["wbd"], 1)
                dve.wait_ge(S["rhs"], c + 1)
                nc.vector.tensor_copy(rhs[:], prs[:]).then_inc(S["rhs_kept"], 1)
                dve.wait_ge(S["st"], c + 1)
                if not first:
                    dve.wait_ge(S["st_new"], NPAIR * c)
                nc.vector.tensor_tensor(tsum[:], pst[:], state[:, b], ALU.add).then_inc(S["st_sum"], 1)
                dve.wait_ge(S["st_sum"], c + 1)
                if not first:
                    dve.wait_ge(S["y"], c)
                for p in range(NPAIR):
                    nc.vector.tensor_scalar(state[:, 1 - b, p, :], tsum[:, p, :], ELC[:, p, ds(c, 1)], None,
                                            ALU.mult).then_inc(S["st_new"], 1)
            chunk(0, 0, True)
            chunk(1, 1, False)
            with dve.Fori(1, NCH // 2) as i:
                chunk(i * 2, 0, False)
                chunk(i * 2 + 1, 1, False)

        @block.scalar
        def _(act):
            def chunk(c, first):
                for q in range(3):
                    act.wait_ge(S["turn"], 3 * c + q + 1)
                    if not first:
                        act.wait_ge(S["y"], c)
                    nc.scalar.activation(turned[:, q], ptr[:], ACT.Copy).then_inc(S["kept"], 1)
                for lev in range(NLEV):
                    n = c * NLEV + lev
                    act.wait_ge(S["tw"], n + 1)
                    if lev < NLEV - 1:
                        nc.scalar.activation(tst[:], pu[:, :, C:P], ACT.Copy).then_inc(S["tst"], 1)
                    else:
                        act.sem_inc(S["tst"], 1)
                    if not (first and lev == 0):
                        act.wait_ge(S["wbd"], n)
                    nc.scalar.activation(wst[:], ptw[:, :, C:P], ACT.Copy).then_inc(S["wst"], 1)
                act.wait_ge(S["sa"], c + 1)
                nc.scalar.activation(sa[:], prs[:], ACT.Copy).then_inc(S["sa_kept"], 1)
                act.wait_ge(S["y"], c + 1)
                nc.scalar.activation(Y[:, :, ds(c * C, C)], py[:, :, 0:C], ACT.Copy).then_inc(S["y_kept"], 1)
            chunk(0, True)
            with act.Fori(1, NCH) as c:
                chunk(c, False)
            act.wait_ge(S["y_kept"], NCH)


def rwkv_samples(kit, a, o, ident, SD, Y):
    nc = kit.nc
    names = ("turned", "kept", "out_sd", "vec_in", "state_in", "halved", "mul", "stored", "y_out", "y_in",
             "y_turned", "y_kept")
    S = {n: kit.sem("rs_" + n) for n in names}
    NV = NB * 8
    with ExitStack() as ctx:
        sdt = kit.sb(ctx, "rs_sdt", [NS, 8, NSTEP, 64])
        vec = kit.sb(ctx, "rs_vec", [P, NT, NSTEP, 64])
        v2 = kit.sb(ctx, "rs_v2", [P, NT, 32])
        st = kit.sb(ctx, "rs_st", [P, 32, 64])
        tmp = kit.sb(ctx, "rs_tmp", [P, 32, 64])
        sav = kit.sb(ctx, "rs_sa", [P, 32])
        ys = kit.sb(ctx, "rs_y", [P, NT, 32])
        yt = kit.sb(ctx, "rs_yt", [NS, 512])
        pt = kit.ps(ctx, "rs_pt", [NS, NSTEP, 512])
        py = kit.ps(ctx, "rs_py", [P, 512])
        block = ctx.enter_context(nc.Block())
        sd, ysd = o["sd"], o["ysd"]

        @block.sync
        def _(sp):
            for h in range(2):
                sp.dma_start(st[h * 64:(h + 1) * 64], a["wkv"][:, h]).then_inc(S["state_in"], 16)
            sp.wait_ge(S["kept"], 1)
            sp.dma_start(sd, sdt[:]).then_inc(S["out_sd"], 16)
            sp.wait_ge(S["out_sd"], 16)
            for h in range(2):
                for n in range(NB):
                    at = h * 64 + n * 8
                    sp.dma_start(vec[at:at + 8], sd[n * NT:(n + 1) * NT].rearrange("t h q k -> h t (q k)"))\
                        .then_inc(S["vec_in"], 16)
            sp.wait_ge(S["stored"], NT)
            for h in range(2):
                sp.dma_start(o["wkv_sample"][:, h], st[h * 64:(h + 1) * 64]).then_inc(S["y_out"], 16)
                for n in range(NB):
                    at = h * 64 + n * 8
                    sp.dma_start(ysd[n * NT:(n + 1) * NT, :, h].rearrange("t h v -> h t v"), ys[at:at + 8])\
                        .then_inc(S["y_out"], 16)
            sp.wait_ge(S["y_out"], 16 * (2 + 2 * NB))
            sp.dma_start(yt[:], ysd.rearrange("t h a v -> t (h a v)")).then_inc(S["y_in"], 16)

        @block.tensor
        def _(pe):
            for q in range(NSTEP):
                for p in range(NPAIR):
                    last = nc.tensor.transpose(pt[:, q, p * P:(p + 1) * P], SD[:, p, q, :], ident)
            last.then_inc(S["turned"], 1)
            pe.wait_ge(S["y_in"], 16)
            for p in range(NPAIR):
                last = nc.tensor.transpose(py[:, p * NS:(p + 1) * NS], yt[:, p * P:(p + 1) * P], ident[0:NS, 0:NS])
            last.then_inc(S["y_turned"], 1)

        @block.vector
        def _(dve):
            dve.wait_ge(S["turned"], 1)
            nc.vector.tensor_copy(sdt[:].rearrange("t h q k -> t q h k"),
                                  pt[:].rearrange("t q (h k) -> t q h k", k=64)).then_inc(S["kept"], 1)
            dve.wait_ge(S["vec_in"], 16 * 2 * NB)
            dve.wait_ge(S["state_in"], 32)
            for h in range(2):
                rows = slice(h * 64, (h + 1) * 64)
                nc.vector.tensor_copy(v2[rows], vec[rows, :, 5, h * 32:(h + 1) * 32]).then_inc(S["halved"], 1)
            dve.wait_ge(S["halved"], 2)
            count = 0
            for t in range(NT):
                along_v = lambda q: vec[:, t, q, :].unsqueeze(1).broadcast_to([P, 32, 64])
                along_k = lambda z: z.unsqueeze(2).broadcast_to([P, 32, 64])
                steps = (
                    (tmp[:], st[:], along_v(1), ALU.mult), (sav[:], tmp[:], None, ALU.add),
                    (st[:], st[:], along_v(0), ALU.mult),
                    (tmp[:], along_k(sav[:]), along_v(2), ALU.mult), (st[:], st[:], tmp[:], ALU.subtract),
                    (tmp[:], along_k(v2[:, t, :]), along_v(3), ALU.mult), (st[:], st[:], tmp[:], ALU.add),
                    (tmp[:], st[:], along_v(4), ALU.mult), (ys[:, t, :], tmp[:], None, ALU.add))
                for n, (out, x, y, op) in enumerate(steps):
                    if y is None:
                        ins = nc.vector.tensor_reduce(out, x, AX, op)
                    else:
                        ins = nc.vector.tensor_tensor(out, x, y, op)
                    ins.then_inc(S["mul"], 1)
                    count += 1
                    dve.wait_ge(S["mul"], count)
                dve.sem_inc(S["stored"], 1)
            dve.wait_ge(S["y_turned"], 1)
            nc.vector.tensor_copy(Y[:, :, SEQ:T], py[:, 0:NPAIR * NS].rearrange("p (a t) -> p a t", t=NS))\
                .then_inc(S["y_kept"], 1)
            dve.wait_ge(S["y_kept"], 1)


def rwkv_finish(kit, blk64, epsg, param, Y, BON, G, mix_out):
    nc = kit.nc
    names = ("mean", "centred", "squared", "var", "rooted", "inverted", "normed", "affine", "bonused", "gated", "stored")
    S = {n: kit.sem("rf_" + n) for n in names}
    with ExitStack() as ctx:
        dev = kit.sb(ctx, "rf_dev", [P, 2, T])
        sq = kit.sb(ctx, "rf_sq", [P, 2, T])
        rs = kit.sb(ctx, "rf_rs", [P, 2, T])
        pm = kit.ps(ctx, "rf_pm", [P, 3, 512])
        pvv = kit.ps(ctx, "rf_pv", [P, 3, 512])
        block = ctx.enter_context(nc.Block())
        part = lambda z: z.rearrange("p (n t) -> p n t", t=T3)

        @block.tensor
        def _(pe):
            for p in range(NPAIR):
                if p:
                    pe.wait_ge(S["centred"], p)
                for n in range(3):
                    last = nc.tensor.matmul(pm[:, n, 0:T3], blk64, Y[:, p, n * T3:(n + 1) * T3], start=True, stop=True)
                last.then_inc(S["mean"], 1)
                pe.wait_ge(S["squared"], p + 1)
                if p:
                    pe.wait_ge(S["rooted"], p)
                for n in range(3):
                    last = nc.tensor.matmul(pvv[:, n, 0:T3], blk64, sq[:, p % 2, n * T3:(n + 1) * T3],
                                            start=True, stop=True)
                last.then_inc(S["var"], 1)

        @block.scalar
        def _(act):
            for p in range(NPAIR):
                act.wait_ge(S["centred"], p + 1)
                if p >= 2:
                    act.wait_ge(S["inverted"], p - 1)
                nc.scalar.activation(sq[:, p % 2], dev[:, p % 2], ACT.Square).then_inc(S["squared"], 1)
                act.wait_ge(S["var"], p + 1)
                if p >= 2:
                    act.wait_ge(S["normed"], p - 1)
                nc.scalar.activation(part(rs[:, p % 2]), pvv[:, :, 0:T3], ACT.Sqrt, bias=epsg).then_inc(S["rooted"], 1)

        @block.vector
        def _(dve):
            for p in range(NPAIR):
                b = p % 2
                dve.wait_ge(S["mean"], p + 1)
                if p >= 2:
                    dve.wait_ge(S["affine"], p - 1)
                nc.vector.tensor_tensor(part(dev[:, b]), part(Y[:, p]), pm[:, :, 0:T3], ALU.subtract)\
                    .then_inc(S["centred"], 1)
                dve.wait_ge(S["rooted"], p + 1)
                nc.vector.reciprocal(rs[:, b], rs[:, b]).then_inc(S["inverted"], 1)
                dve.wait_ge(S["inverted"], p + 1)
                nc.vector.tensor_tensor(dev[:, b], dev[:, b], rs[:, b], ALU.mult).then_inc(S["normed"], 1)
                dve.wait_ge(S["normed"], p + 1)
                nc.vector.tensor_scalar(Y[:, p], dev[:, b], param("ln_w", 4)[:, p:p + 1], param("ln_b", 4)[:, p:p + 1],
                                        ALU.mult, ALU.add).then_inc(S["affine"], 1)

        @block.gpsimd
        def _(pool):
            for p in range(NPAIR):
                pool.wait_ge(S["affine"], p + 1)
                nc.gpsimd.tensor_tensor(Y[:, p], Y[:, p], BON[:, p], ALU.add).then_inc(S["bonused"], 1)
                pool.wait_ge(S["bonused"], p + 1)
                nc.gpsimd.tensor_tensor(Y[:, p], Y[:, p], G[:, p], ALU.mult).then_inc(S["gated"], 1)

        @block.sync
        def _(sp):
            for p in range(NPAIR):
                sp.wait_ge(S["gated"], p + 1)
                sp.dma_start(mix_out[p], Y[:, p]).then_inc(S["stored"], 16)
            sp.wait_ge(S["stored"], 16 * NPAIR)


def build(nc, a, o):
    with ExitStack() as top:
        kit = Kit(nc, top)
        par = kit.sb(top, "par", [P, NPARAM])
        ones = kit.sb(top, "ones", [P, P])
        epsc = kit.sb(top, "epsc", [P, 2])
        param = lambda name, n: par[:, PCOL[name]:PCOL[name] + n]

        ident = kit.sb(top, "ident", [P, P])
        identb = kit.sb(top, "identb", [P, P], BF16)
        causal = kit.sb(top, "causal", [P, P], BF16)
        lam = kit.sb(top, "lam", [P, 8])
        oR = o["oR"].rearrange("(h p) t -> h p t", p=P)
        oT = o["oT"].rearrange("(h p) t -> h p t", p=P)

        gain = lambda name: lambda k: param(name, KD)[:, k:k + 1]

        load_phase(kit, "ld_c", [(ident[:], a["ident"]), (identb[:], a["identb"]), (causal[:], a["causal"]),
                                 (par[:], a["par"])])
        made, chain = kit.sem("made"), kit.sem("lam_chain")
        with ExitStack() as ctx:
            lq = kit.sb(ctx, "lq", [P, 4, DH])
            prod = kit.sb(ctx, "lprod", [P, 2, DH])
            comb1 = kit.sb(ctx, "lcomb", [P, 17])
            load_phase(kit, "ld_l", [(lq[:], a["lams"]), (comb1[:], a["comb"])])
            block = ctx.enter_context(nc.Block())

            @block.scalar
            def _(act):
                act.wait_ge(chain, 3)
                nc.scalar.activation(lam[:, 2:4], lam[:, 0:2], ACT.Exp).then_inc(chain, 1)

            @block.vector
            def _(dve):
                nc.vector.memset(ones[:], 1.0 / D).then_inc(made, 1)
                nc.vector.memset(epsc[:, 0:1], EPS).then_inc(made, 1)
                nc.vector.memset(epsc[:, 1:2], GN_EPS).then_inc(made, 1)
                nc.vector.tensor_tensor(prod[:], lq[:, 0:2], lq[:, 2:4], ALU.mult).then_inc(chain, 1)
                dve.wait_ge(chain, 1)
                nc.vector.tensor_reduce(lam[:, 0:2], prod[:], AX, ALU.add).then_inc(chain, 2)
                dve.wait_ge(chain, 4)
                nc.vector.tensor_tensor(lam[:, 4:5], lam[:, 3:4], lam[:, 2:3], ALU.subtract).then_inc(chain, 1)
                dve.wait_ge(chain, 5)
                nc.vector.tensor_scalar(lam[:, 4:5], lam[:, 4:5], -LAM_INIT, None, ALU.add).then_inc(chain, 1)
                dve.wait_ge(chain, 6)
                nc.vector.tensor_scalar(lam[:, 5:6], lam[:, 4:5], -1.0, comb1[:, 16:17], ALU.add,
                                        ALU.mult).then_inc(chain, 1)
                dve.wait_ge(chain, 7)
                nc.vector.tensor_scalar(lam[:, 5:6], lam[:, 5:6], 1.0, None, ALU.add).then_inc(chain, 1)
                dve.wait_ge(chain, 8)
                dve.wait_ge(made, 3)

        x_view = a["xT"].rearrange("(k p) t -> p k t", p=P)

        proj = o["projT"].rearrange("(m p) t -> m p t", p=P)

        with ExitStack() as ctx:
            Hh = kit.sb(ctx, "Hh", [P, KD, T], F32R)
            Hl = kit.sb(ctx, "Hl", [P, KD, T], F32R)
            with ExitStack() as inner:
                X = kit.sb(inner, "X", [P, KD, T])
                R = kit.sb(inner, "R", [P, T])
                load_phase(kit, "ld_x", [(X[:, k], x_view[:, k]) for k in range(KD)])
                rms_rows(kit, "rms_x", X, R[:], KD, T, ones[:], epsc[:, 0:1])
                scale_split(kit, "split_x", X, KD, T, Hh, Hl, gain("g_mix_pre"), lambda k: R[:])
            parts = [(n * T3, T3) for n in range(3)]
            project(kit, "in", MT_IN, KD, 1, a["w_in"], Hh, Hl, parts,
                    lambda c: ToDram(kit, c, "in", parts, lambda m: proj[m] if isinstance(m, int) else
                                     proj[ds(m, 1)].rearrange("a p t -> (a p) t")))

        attend_prompt(kit, proj, oT, ident[:], identb[:], causal[:], lam[:, 4:5])
        attend_sample(kit, a, proj, oT, ident[:], identb[:], lam[:, 5:6])

        kit.retire()

        with ExitStack() as ctx:
            V = kit.sb(ctx, "V", [P, NPAIR, T])
            NR = kit.sb(ctx, "NR", [P, NPAIR, 2, SEQ])
            Bc = kit.sb(ctx, "Bc", [P, NPAIR, SEQ])
            Kc = kit.sb(ctx, "Kc", [P, NPAIR, SEQ])
            BON = kit.sb(ctx, "BON", [P, NPAIR, T])
            G = kit.sb(ctx, "G", [P, NPAIR, T])
            ELC = kit.sb(ctx, "ELC", [P, NPAIR, NCH])
            SD = kit.sb(ctx, "SD", [P, NPAIR, NSTEP, NS])
            with ExitStack() as inner:
                Rm = kit.sb(inner, "Rm", [P, NPAIR, T])
                Km = kit.sb(inner, "Km", [P, NPAIR, T])
                X12 = kit.sb(inner, "X12", [P, T])
                XG = kit.sb(inner, "XG", [P, T])
                dsts = [z[:, p] for z in (Rm, Km, V) for p in range(NPAIR)] + [X12[:], XG[:]]
                rwkv_mix(kit, ctx, a, proj, param, dsts)
                rwkv_prepare(kit, ctx, a, param, Rm, Km, V, X12, XG[:], NR, Bc, Kc, BON, G, ELC, SD)
            with ExitStack() as inner:
                Y = kit.sb(inner, "Y", [P, NPAIR, T])
                rwkv_chunks(kit, a, NR, Bc, Kc, V, ELC, Y, o["wkv_prompt"])
                kit.retire()
                rwkv_samples(kit, a, o, ident[:], SD, Y)
                blk64 = kit.sb(inner, "blk64", [P, P])
                load_phase(kit, "ld_b", [(blk64[:], a["blockmean"])])
                rwkv_finish(kit, blk64[:], epsc[:, 1:2], param, Y, BON, G, oR)


        kit.retire()
        third = [(n * T3, T3) for n in range(3)]
        quarter = [(0, TH // 2), (TH // 2, TH // 2)]
        x1 = o["x1T"].rearrange("(k p) t -> p k t", p=P)
        h2 = o["h2T"].rearrange("(k p) t -> p k t", p=P)
        fT = o["fT"].rearrange("(k p) t -> p k t", p=P)

        with ExitStack() as ctx:
            Y = kit.sb(ctx, "mixed", [P, KD, T])
            with ExitStack() as inner:
                Hh = kit.sb(inner, "Mh", [P, KD, T], F32R)
                Hl = kit.sb(inner, "Ml", [P, KD, T], F32R)
                with ExitStack() as pre:
                    ones_head = kit.sb(pre, "ones_head", [P, P])
                    R4 = kit.sb(pre, "R4", [P, HEADS, T])
                    gs = kit.sb(pre, "gs", [P, 1])
                    load_phase(kit, "ld_m", [(ones_head[:], a["headmean"])]
                               + [(Y[:, h], oT[h]) for h in range(4)] + [(Y[:, 4 + h], oR[h]) for h in range(4)])
                    subln = kit.sem("subln")
                    with nc.Block() as block:
                        @block.vector
                        def _(dve):
                            nc.vector.tensor_scalar(gs[:], param("g_subln", 1), 1.0 - LAM_INIT, None,
                                                    ALU.mult).then_inc(subln, 1)
                            dve.wait_ge(subln, 1)
                    for n in range(2):
                        rms_rows(kit, f"rms_o{n}", Y[:, 2 * n:2 * n + 2, :].rearrange("p (o k) t -> p o (k t)", o=1),
                                 R4[:, 2 * n:2 * n + 2, :].rearrange("p k t -> p (k t)"), 1, 2 * T, ones_head[:],
                                 epsc[:, 0:1])
                    scale_split(kit, "split_o", Y, 4, T, Hh, Hl, lambda k: gs[:], lambda k: R4[:, k, :])
                    scale_split(kit, "split_r", Y[:, 4:8], 4, T, Hh[:, 4:8], Hl[:, 4:8])
                project(kit, "wo", KD, KD, 1, a["w_o"], Hh, Hl, third, lambda c: ToSbuf(kit, c, "wo", third, Y))
            X = kit.sb(ctx, "X1", [P, KD, T])
            R = kit.sb(ctx, "R1", [P, T])
            load_phase(kit, "ld_x1", [(X[:, k], x_view[:, k]) for k in range(KD)])
            rms_rows(kit, "rms_m", Y, R[:], KD, T, ones[:], epsc[:, 0:1])
            add_scaled(kit, "add_m", Y, param("g_mix_post", KD), R[:], X)
            rms_rows(kit, "rms_f", X, R[:], KD, T, ones[:], epsc[:, 0:1])
            scale_split(kit, "store_h2", X, KD, T, None, None, gain("g_ffn_pre"), lambda k: R[:], store=h2)
            load_phase(kit, "st_x1", [(x1[:, k], X[:, k]) for k in range(KD)])
        kit.retire()

        with ExitStack() as ctx:
            carry = kit.sb(ctx, "carry", [P, 2 * FT, 2])
            states = kit.sb(ctx, "states", [P, 2 * FT, 2 * NB])
            conv_out = kit.sb(ctx, "conv_out", [P, 2 * FT, 2 + 2 * NB])
            cleared = kit.sem("carry_cleared")
            load_phase(kit, "ld_st", [(states[:], a["convT"])])
            with nc.Block() as block:
                @block.vector
                def _(dve):
                    nc.vector.memset(carry[:], 0.0).then_inc(cleared, 1)
                    dve.wait_ge(cleared, 1)
            for half in range(2):
                with ExitStack() as inner:
                    Gh = kit.sb(inner, f"Gh{half}", [P, FT, TH], F32R)
                    Gl = kit.sb(inner, f"Gl{half}", [P, FT, TH], F32R)
                    with ExitStack() as up:
                        Hh = kit.sb(up, f"Uh{half}", [P, KD, TH], F32R)
                        Hl = kit.sb(up, f"Ul{half}", [P, KD, TH], F32R)
                        with ExitStack() as pre:
                            H = kit.sb(pre, f"H2{half}", [P, KD, TH])
                            load_phase(kit, f"ld_h{half}", [(H[:, k], h2[:, k, half * TH:(half + 1) * TH])
                                                            for k in range(KD)])
                            scale_split(kit, f"split_h{half}", H, KD, TH, Hh, Hl)
                        project(kit, f"up{half}", 2 * FT, KD, 1, a["w_up"], Hh, Hl, quarter,
                                lambda c: ConvGate(kit, c, f"cg{half}", quarter, par, carry, states, conv_out, Gh, Gl,
                                                   half == 1))
                    down = o["fT"].rearrange("(m p) t -> m p t", p=P)[:, :, half * TH:(half + 1) * TH]
                    project(kit, f"dn{half}", KD, FT // 2, 2, a["w_down"], Gh, Gl, quarter,
                            lambda c: ToDram(kit, c, f"dn{half}", quarter, lambda m: down[m] if isinstance(m, int) else
                                             down[ds(m, 1)].rearrange("a p t -> (a p) t")))
                kit.retire()
            load_phase(kit, "st_cv", [(o["conv_out"], conv_out[:])])

        with ExitStack() as ctx:
            X = kit.sb(ctx, "X2", [P, KD, T])
            R = kit.sb(ctx, "R2", [P, T])
            Y = kit.sb(ctx, "Y2", [P, KD, T])
            load_phase(kit, "ld_f", [(X[:, k], x1[:, k]) for k in range(KD)] + [(Y[:, k], fT[:, k]) for k in range(KD)])
            rms_rows(kit, "rms_d", Y, R[:], KD, T, ones[:], epsc[:, 0:1])
            add_scaled(kit, "add_d", Y, param("g_ffn_post", KD), R[:], X)
            with ExitStack() as inner:
                Eh = kit.sb(inner, "Eh", [P, PLE // P, T], F32R)
                El = kit.sb(inner, "El", [P, PLE // P, T], F32R)
                with ExitStack() as pre:
                    E = kit.sb(pre, "E", [P, PLE // P, T])
                    load_phase(kit, "ld_p", [(E[:], a["pT"].rearrange("(k p) t -> p k t", p=P))])
                    scale_split(kit, "split_p", E, PLE // P, T, Eh, El)
                project(kit, "ple", KD, PLE // P, 1, a["w_ple"], Eh, El, third,
                        lambda c: ToSbuf(kit, c, "ple", third, Y, 0.5))
            with ExitStack() as inner:
                Hh = kit.sb(inner, "X2h", [P, KD, T], F32R)
                Hl = kit.sb(inner, "X2l", [P, KD, T], F32R)
                scale_split(kit, "split_x2", X, KD, T, Hh, Hl)
                project(kit, "pg", KD, KD, 1, a["w_gate"], Hh, Hl, third, lambda c: Gate(kit, c, "pg", third, Y))
            rms_rows(kit, "rms_p", Y, R[:], KD, T, ones[:], epsc[:, 0:1])
            add_scaled(kit, "add_p", Y, param("g_ple", KD), R[:], X)
            load_phase(kit, "st_y", [(o["yT"].rearrange("(k p) t -> p k t", p=P)[:, k], X[:, k]) for k in range(KD)])

OUTS = {"yT": (D, T), "projT": (N_IN, T), "wkv_prompt": (P, NPAIR, C), "wkv_sample": (NB * 8, 2, 32, 64),
        "conv_out": (P, 2 * FT, 2 + 2 * NB)}
SCRATCH = {"oT": (512, T), "oR": (512, T), "x1T": (D, T), "h2T": (D, T), "fT": (D, T),
           "sd": (NS, 8, NSTEP, 64), "ysd": (NS, 8, 2, 32)}


def kernel(**inputs):
    import numpy as np
    import concourse.bacc as bacc
    from concourse import mybir as mb
    from concourse.bass_utils import run_bass_kernel_spmd

    bf16 = mb.dt.np(mb.dt.bfloat16)
    v = {n: np.asarray(x) for n, x in inputs.items()}

    def cols(x, n):
        x = np.ascontiguousarray(x, dtype=x.dtype).reshape(-1)
        return np.pad(x, (0, n * P - x.size)).reshape(n, P).T

    def halves(x):
        g, u = cols(x[:FF], FT), cols(x[FF:], FT)
        return np.stack([g, u], axis=2).reshape(P, 2 * FT)

    def tiles(w, kt, units):
        k, m = units * kt * P, -(-w.shape[1] // P) * P
        w = np.pad(w, ((0, k - w.shape[0]), (0, m - w.shape[1])))
        w = w.reshape(units, kt, P, m // P, P).transpose(3, 0, 2, 1, 4)
        return np.ascontiguousarray(w).reshape(m // P * units, P, kt * P)

    def tokens(p, s):
        return np.ascontiguousarray(np.concatenate([p.reshape(SEQ, -1), s.reshape(NS, -1)]).T)

    par = np.ascontiguousarray(np.concatenate(
        [cols(v[n][0], 8) for n in ("g_mix_pre", "g_mix_post", "g_ffn_pre", "g_ffn_post", "g_ple")]
        + [cols(v["g_subln"][0], 1), cols(v["mu_shift"][0], 14)]
        + [cols(v[n][0], 4) for n in ("w0", "a0", "k_k", "k_a", "r_k", "ln_x_w", "ln_x_b")]
        + [halves(v["conv_w"][0, j]) for j in range(3)] + [halves(v["conv_b"][0])], axis=1))
    comb = np.zeros((P, 17), np.float32)
    new_mask = np.full((P, NB, NS), NEG, np.float32)
    for h in range(HEADS):
        for c in range(2):
            for t in range(NT):
                row = 32 * h + NT * c + t
                comb[row, NT * h + t] = 1.0
                comb[row, 16] = c
                for n in range(NB):
                    new_mask[row, n, NT * n:NT * n + t + 1] = 0.0
    j, h2 = np.arange(P) % C, np.arange(P) // C
    i = np.arange(C)
    same = h2[:, None] == np.arange(2)[None, :]

    def bd4(m):
        return np.tile((m[:, None, :] * same[:, :, None]).reshape(P, P), (1, NPAIR)).astype(np.float32)

    def st4(m):
        return np.tile(m, (1, NPAIR)).astype(np.float32)

    lev = [(j[:, None] == i[None, :]) | ((j[:, None] >> (n + 1) == i[None, :] >> (n + 1))
                                         & (j[:, None] >> n > i[None, :] >> n)) for n in range(NLEV)]
    new_mask = new_mask.reshape(P, NB * NS).astype(bf16)
    wu = v["w_up"][0]
    sc = v["state_conv"][0].reshape(NB * 2, 2 * FF)
    convT = np.ascontiguousarray(np.stack([halves(row) for row in sc], axis=2))
    gate, val = tiles(wu[:, :FF], KD, 1), tiles(wu[:, FF:], KD, 1)
    arrays = {
        "xT": tokens(v["x_prompt"], v["x_sample"]),
        "pT": tokens(v["p_prompt"], v["p_sample"]),
        "par": par,
        "w_in": tiles(v["w_in"][0], KD, 1),
        "w_o": tiles(v["w_o"][0], KD, 1),
        "w_up": np.ascontiguousarray(np.stack([gate, val], axis=1)).reshape(2 * FT, P, KD * P),
        "w_down": tiles(v["w_down"][0], FT // 2, 2),
        "w_ple": tiles(v["w_ple"][0], PLE // P, 1),
        "w_gate": tiles(v["w_ple_gate"][0], KD, 1),
        "headmean": np.full((P, P), 1 / P, np.float32),
        "convT": convT,
        "ident": np.eye(P, dtype=np.float32),
        "identb": np.eye(P, dtype=bf16),
        "causal": np.where(np.arange(P)[None, :] > np.arange(P)[:, None], NEG, 0.0).astype(bf16),
        "lams": np.tile(np.stack([v[n][0] for n in ("lam_q1", "lam_q2", "lam_k1", "lam_k2")])[None], (P, 1, 1)),
        "comb": comb,
        "w2": v["w2"][0], "a2": v["a2"][0], "g2": v["g2"][0],
        "blockones": np.kron(np.eye(2), np.ones((C, C))).astype(np.float32),
        "blockmean": np.kron(np.eye(2), np.full((C, C), 1 / C)).astype(np.float32),
        "reset": np.tile((np.arange(SEQ) % C != 0)[None], (P, 1)).astype(bf16),
        "strict": bd4(j[:, None] < i[None, :]), "incl": st4(j[:, None] <= i[None, :]),
        "levbd": np.stack([bd4(m) for m in lev], axis=1), "levst": np.stack([st4(m) for m in lev], axis=1),
        "pairbd": bd4(np.ones((P, C))), "eyebd": bd4(j[:, None] == i[None, :]), "eyest": st4(j[:, None] == i[None, :]),
        "shiftT": np.ascontiguousarray(v["state_shift"][0].reshape(NB, 14, P).transpose(2, 1, 0)),
        "wkv": v["state_wkv"][0].reshape(NB * 8, 2, 32, 64),
        "new_mask": new_mask,
        "table": v["page_table"].reshape(1, -1),
        "k_pool": np.ascontiguousarray(v["cache_k"][0].transpose(0, 3, 2, 1)).reshape(POOL, P, HEADS * PAGE),
        "v_pool": v["cache_v"][0].reshape(POOL, PAGE, HEADS * P),
    }

    nc = bacc.Bacc("TRN2", target_bir_lowering=False, num_devices=1)
    a = {n: nc.dram_tensor("dram_" + n, x.shape, mb.dt.from_np(x.dtype), kind="ExternalInput").ap()
         for n, x in arrays.items()}
    o = {n: nc.dram_tensor("dram_" + n, s, mb.dt.float32, kind="ExternalOutput").ap() for n, s in OUTS.items()}
    o.update({n: nc.dram_tensor("dram_" + n, s, mb.dt.float32).ap() for n, s in SCRATCH.items()})
    build(nc, a, o)
    r = run_bass_kernel_spmd(nc, [{"dram_" + n: x for n, x in arrays.items()}], core_ids=[0]).results[0]
    y, proj, wp, ws, cv = (r["dram_" + n] for n in OUTS)
    kT, vT, sh = proj[512:1024], proj[1024:1536], proj[1536:]
    last = [SEQ + n * NT + NT - 1 for n in range(NB)]

    def split(z, shape):
        z = np.ascontiguousarray(z.T)
        return z[:SEQ].reshape(1, 1, SEQ, *shape), z[SEQ:].reshape(1, NB, NT, *shape)

    y_prompt, y_sample = (z[0] for z in split(y, (D,)))
    (kp, ks), (vp, vs) = split(kT, (HEADS, P)), split(vT, (HEADS, P))
    wp = wp.reshape(2, C, NPAIR, C).transpose(2, 0, 3, 1).reshape(1, 1, 8, C, C)
    cv = cv.reshape(P, FT, 2, 18).transpose(3, 2, 1, 0).reshape(18, 2, FT * P)[:, :, :FF].reshape(18, 2 * FF)
    return (y_prompt, y_sample, kp, vp, ks, vs, sh[:, SEQ - 1].reshape(1, 1, -1), np.ascontiguousarray(wp),
            cv[0:2].reshape(1, 1, 2, -1), np.ascontiguousarray(sh[:, last].T)[None], ws.reshape(1, NB, 8, C, C),
            cv[2:].reshape(1, NB, 2, -1))
```

```python
import math
from contextlib import ExitStack

import concourse.bass as bass
from concourse import mybir

F32 = mybir.dt.float32
F32R = mybir.dt.float32r
BF16 = mybir.dt.bfloat16
I32 = mybir.dt.int32
ALU = mybir.AluOpType
ACT = mybir.ActivationFunctionType
AX = mybir.AxisListType.X
ds = bass.ds

P = 128
D = 1024
KD = D // P
SEQ = 1024
NB, NT = 8, 4
NS = NB * NT
T = SEQ + NS
T3 = T // 3
HEADS, DH = 4, 64
PAGES, PAGE = 8, 128
POOL = 80
N_IN = 3328
MT_IN = N_IN // P
FF = 2752
FT = (FF + P - 1) // P
TH = T // 2
PLE = 256
EPS = 1e-6
GN_EPS = 64e-5
LAM_INIT = 0.8 - 0.6 * math.exp(0.0)
C = 64
NCH = SEQ // C
NEG = -1e30
E05 = math.exp(-0.5)

PCOL = {}
_n = 0
for _name, _w in (("g_mix_pre", 8), ("g_mix_post", 8), ("g_ffn_pre", 8), ("g_ffn_post", 8), ("g_ple", 8),
                  ("g_subln", 1), ("mu", 14), ("w0", 4), ("a0", 4), ("k_k", 4), ("k_a", 4), ("r_k", 4),
                  ("ln_w", 4), ("ln_b", 4), ("cw0", 2 * FT), ("cw1", 2 * FT), ("cw2", 2 * FT), ("cb", 2 * FT)):
    PCOL[_name] = _n
    _n += _w
NPARAM = _n


class Kit:

    def __init__(self, nc, top):
        self.nc, self.live = nc, []

    def sb(self, ctx, name, shape, dt=F32):
        return ctx.enter_context(self.nc.sbuf_tensor(name, shape, dt))

    def ps(self, ctx, name, shape, dt=F32):
        return ctx.enter_context(self.nc.psum_tensor(name, shape, dt))

    def sem(self, name):
        self.live.append(self.nc.alloc_semaphore(name=name))
        return self.live[-1]

    def retire(self):
        self.nc.clear_and_free_semaphores(self.live)
        self.nc.all_engine_barrier()
        self.live = []


def load_phase(kit, name, pairs):
    nc = kit.nc
    loaded_sp, loaded_act = kit.sem(name + "_loaded_sp"), kit.sem(name + "_loaded_act")
    with nc.Block() as block:
        @block.sync
        def _(sp):
            for dst, src in pairs[0::2]:
                sp.dma_start(dst, src).then_inc(loaded_sp, 16)
            sp.wait_ge(loaded_sp, 16 * len(pairs[0::2]))

        @block.scalar
        def _(act):
            for dst, src in pairs[1::2]:
                act.dma_start(dst, src).then_inc(loaded_act, 16)
            if len(pairs) > 1:
                act.wait_ge(loaded_act, 16 * len(pairs[1::2]))


def rms_rows(kit, name, X, R, tiles, width, ones, eps):
    nc = kit.nc
    squared, summed, totals, rooted = (kit.sem(f"{name}_{s}") for s in ("squared", "summed", "totals", "rooted"))
    nparts = (width + 511) // 512
    while width % nparts:
        nparts += 1
    part = width // nparts
    with ExitStack() as ctx:
        sq = kit.sb(ctx, name + "_sq", [P, 2, width])
        acc = kit.sb(ctx, name + "_acc", [P, width])
        tot = kit.ps(ctx, name + "_tot", [P, nparts, 512])
        block = ctx.enter_context(nc.Block())

        @block.scalar
        def _(act):
            for k in range(tiles):
                if k >= 2:
                    act.wait_ge(summed, k - 1)
                nc.scalar.activation(sq[:, k % 2, :], X[:, k, :], ACT.Square).then_inc(squared, 1)
            act.wait_ge(totals, 1)
            nc.scalar.activation(R.rearrange("p (n t) -> p n t", t=part), tot[:, :, 0:part], ACT.Sqrt,
                                 bias=eps).then_inc(rooted, 1)

        @block.vector
        def _(dve):
            for k in range(tiles):
                dve.wait_ge(squared, k + 1)
                if k == 0:
                    nc.vector.tensor_copy(acc[:], sq[:, 0, :]).then_inc(summed, 1)
                else:
                    dve.wait_ge(summed, k)
                    nc.vector.tensor_tensor(acc[:], acc[:], sq[:, k % 2, :], ALU.add).then_inc(summed, 1)
            dve.wait_ge(rooted, 1)
            nc.vector.reciprocal(R, R).then_inc(rooted, 1)
            dve.wait_ge(rooted, 2)

        @block.tensor
        def _(pe):
            pe.wait_ge(summed, tiles)
            for n in range(nparts):
                last = nc.tensor.matmul(tot[:, n, 0:part], ones, acc[:, n * part:(n + 1) * part],
                                        start=True, stop=True)
            last.then_inc(totals, 1)


def scale_split(kit, name, X, tiles, width, Hh, Hl, gain=None, R=None, store=None):
    nc = kit.nc
    scaled, high, low = (kit.sem(f"{name}_{s}") for s in ("scaled", "high", "low"))
    stored = [kit.sem(f"{name}_stored{b}") for b in range(2)] if store is not None else None
    with ExitStack() as ctx:
        tmp = kit.sb(ctx, name + "_tmp", [P, 2, width]) if gain is not None else None
        block = ctx.enter_context(nc.Block())

        @block.vector
        def _(dve):
            def scale(k):
                if k >= 2 and store is not None:
                    dve.wait_ge(stored[k % 2], 16 * (k // 2))
                elif k >= 2:
                    dve.wait_ge(low, k - 1)
                nc.vector.scalar_tensor_tensor(tmp[:, k % 2, :], X[:, k, :], gain(k), R(k),
                                               ALU.mult, ALU.mult).then_inc(scaled, 1)

            for k in range(tiles):
                if gain is not None:
                    scale(k)
                if store is None:
                    src = tmp[:, k % 2, :] if gain is not None else X[:, k, :]
                    dve.wait_ge(high, k + 1)
                    nc.vector.tensor_tensor(Hl[:, k, :], src, Hh[:, k, :].bitcast(F32),
                                            ALU.subtract).then_inc(low, 1)
            if store is None:
                dve.wait_ge(low, tiles)

        if store is None:
            @block.scalar
            def _(act):
                for k in range(tiles):
                    if gain is not None:
                        act.wait_ge(scaled, k + 1)
                    src = tmp[:, k % 2, :] if gain is not None else X[:, k, :]
                    nc.scalar.activation(Hh[:, k, :], src, ACT.Copy).then_inc(high, 1)
        else:
            @block.sync
            def _(sp):
                for k in range(tiles):
                    sp.wait_ge(scaled, k + 1)
                    sp.dma_start(store[:, k, :], tmp[:, k % 2, :]).then_inc(stored[k % 2], 16)
                for b in range(2):
                    sp.wait_ge(stored[b], 16 * (tiles // 2))


def add_scaled(kit, name, Y, gain, R, X):
    nc = kit.nc
    scaled, added = kit.sem(name + "_scaled"), kit.sem(name + "_added")
    with nc.Block() as block:
        @block.vector
        def _(dve):
            for k in range(KD):
                nc.vector.scalar_tensor_tensor(Y[:, k, :], Y[:, k, :], gain[:, k:k + 1], R,
                                               ALU.mult, ALU.mult).then_inc(scaled, 1)

        @block.gpsimd
        def _(pool):
            for k in range(KD):
                pool.wait_ge(scaled, k + 1)
                nc.gpsimd.tensor_tensor(X[:, k, :], X[:, k, :], Y[:, k, :], ALU.add).then_inc(added, 1)
            pool.wait_ge(added, KD)


class ToDram:

    def __init__(self, kit, ctx, name, parts, dst):
        self.nc, self.parts, self.dst = kit.nc, parts, dst
        self.out = kit.sb(ctx, name + "_out", [P, 2, len(parts), parts[0][1]])
        self.stored = [kit.sem(f"{name}_stored{b}") for b in range(2)]

    def act(self, act, m, b, turn, first):
        act.wait_ge(self.multiplied, (m + 1) * self.units)
        if not first:
            act.wait_ge(self.stored[b], turn * 16)
        self.nc.scalar.activation(self.out[:, b], self.acc[:, b, :, 0:self.parts[0][1]],
                                  ACT.Copy).then_inc(self.drained, 1)

    def pool(self, pool, m, b, turn, first):
        pool.wait_ge(self.drained, m + 1)
        pool.dma_start(self.dst(m), self.out[:, b].rearrange("p n t -> p (n t)")).then_inc(self.stored[b], 16)

    def pool_end(self, pool, ntiles):
        for b in range(2):
            pool.wait_ge(self.stored[b], 16 * (ntiles // 2))


class ToSbuf:

    def __init__(self, kit, ctx, name, parts, Y, scale=1.0):
        self.nc, self.parts, self.Y, self.scale = kit.nc, parts, Y, scale

    def act(self, act, m, b, turn, first):
        act.wait_ge(self.multiplied, (m + 1) * self.units)
        w = self.parts[0][1]
        out = self.Y[:, ds(m, 1), :].rearrange("p a (n t) -> p (a n) t", t=w)
        self.nc.scalar.activation(out, self.acc[:, b, :, 0:w], ACT.Copy,
                                  scale=self.scale).then_inc(self.drained, 1)


class Gate:

    def __init__(self, kit, ctx, name, parts, Y):
        self.nc, self.parts, self.Y = kit.nc, parts, Y
        self.th = kit.sb(ctx, name + "_th", [P, 2, T])
        self.gated = kit.sem(name + "_gated")

    def act(self, act, m, b, turn, first):
        act.wait_ge(self.multiplied, (m + 1) * self.units)
        if not first:
            act.wait_ge(self.gated, m - 1)
        w = self.parts[0][1]
        self.nc.scalar.activation(self.th[:, b].rearrange("p (n t) -> p n t", t=w), self.acc[:, b, :, 0:w],
                                  ACT.Tanh, scale=0.5).then_inc(self.drained, 1)

    def dve(self, dve, m, b, turn, first):
        dve.wait_ge(self.drained, m + 1)
        y = self.Y[:, ds(m, 1), :].rearrange("p a t -> p (a t)")
        self.nc.vector.scalar_tensor_tensor(y, self.th[:, b], 1.0, y, ALU.add, ALU.mult).then_inc(self.gated, 1)

    def dve_end(self, dve, ntiles):
        dve.wait_ge(self.gated, ntiles)


class ConvGate:

    def __init__(self, kit, ctx, name, parts, par, carry, states, conv_out, Gh, Gl, last):
        self.nc, self.parts, self.par, self.last = kit.nc, parts, par, last
        self.carry, self.states, self.conv_out, self.Gh, self.Gl = carry, states, conv_out, Gh, Gl
        self.prompt = TH - NS if last else TH
        self.wide = 2 + self.prompt + (NB * (2 + NT) if last else 0)
        self.u = kit.sb(ctx, name + "_u", [P, 2, self.wide])
        self.c = kit.sb(ctx, name + "_c", [P, 2, self.wide - 2])
        self.ge = kit.sb(ctx, name + "_ge", [P, self.wide - 2])
        self.g = kit.sb(ctx, name + "_g", [P, TH])
        self.S = {n: kit.sem(f"{name}_{n}") for n in ("led", "tap0", "tap1", "tap2", "saved", "gelued", "gated",
                                                      "g_high", "g_low")}

    def samples(self, z, off=0):
        return z[:, 2 + self.prompt:].rearrange("p (n t) -> p n t", t=2 + NT)

    def tap(self, name, m):
        return self.par[:, ds(m + PCOL[name], 1)]

    def act(self, act, m, b, turn, first):
        S, nc = self.S, self.nc
        w = self.parts[0][1]
        if b == 0 and not first:
            self.high(act, turn - 1)
        act.wait_ge(self.multiplied, m + 1)
        if not first:
            act.wait_ge(S["tap2"], m - 1)
            act.wait_ge(S["saved"], m - 1)
        u, acc = self.u[:, b], self.acc[:, b]
        if self.last:
            nc.scalar.activation(u[:, 2:2 + w], acc[:, 0, 0:w], ACT.Copy)
            nc.scalar.activation(u[:, 2 + w:2 + self.prompt], acc[:, 1, 0:self.prompt - w], ACT.Copy)
            ins = nc.scalar.activation(self.samples(u)[:, :, 2:],
                                       acc[:, 1, self.prompt - w:w].rearrange("p (n t) -> p n t", t=NT), ACT.Copy)
        else:
            ins = nc.scalar.activation(u[:, 2:].rearrange("p (n t) -> p n t", t=w), acc[:, :, 0:w], ACT.Copy)
        ins.then_inc(self.drained, 1)
        act.wait_ge(self.drained, m + 1)
        act.wait_ge(S["led"], m + 1)
        if not first:
            act.wait_ge(S["gated"], turn)
        n = self.wide - 2
        nc.scalar.activation(self.c[:, b], u[:, 0:n], ACT.Identity, bias=self.tap("cb", m),
                             scale=self.tap("cw0", m)).then_inc(S["tap0"], 1)
        if b == 1:
            act.wait_ge(S["tap2"], m)
            nc.scalar.activation(self.ge[:], self.c[:, 0], ACT.Gelu_apprx_tanh).then_inc(S["gelued"], 1)

    def high(self, act, turn):
        act.wait_ge(self.S["gated"], turn + 1)
        if not isinstance(turn, int) or turn > 0:
            act.wait_ge(self.S["g_low"], turn)
        self.nc.scalar.activation(self.Gh[:, ds(turn, 1), :].rearrange("p a t -> p (a t)"), self.g[:],
                                  ACT.Copy).then_inc(self.S["g_high"], 1)

    def act_end(self, act, ntiles):
        self.high(act, ntiles // 2 - 1)

    def low(self, dve, turn):
        dve.wait_ge(self.S["g_high"], turn + 1)
        gh, gl = (z[:, ds(turn, 1), :].rearrange("p a t -> p (a t)") for z in (self.Gh, self.Gl))
        self.nc.vector.tensor_tensor(gl, self.g[:], gh.bitcast(F32), ALU.subtract).then_inc(self.S["g_low"], 1)

    def dve(self, dve, m, b, turn, first):
        S, nc, n = self.S, self.nc, self.wide - 2
        if b == 0 and not first:
            self.low(dve, turn - 1)
        c, u = self.c[:, b], self.u[:, b]
        for k in (1, 2):
            dve.wait_ge(S[f"tap{k - 1}"], m + 1)
            nc.vector.scalar_tensor_tensor(c, u[:, k:k + n], self.tap(f"cw{k}", m), c, ALU.mult,
                                           ALU.add).then_inc(S[f"tap{k}"], 1)
        one = lambda z: z[:, ds(m, 1)].rearrange("p a t -> p (a t)")
        end = u[:, self.prompt:self.prompt + 2]
        if self.last:
            nc.vector.tensor_scalar(one(self.conv_out)[:, 0:2], end, 1.0, None, ALU.mult)
            nc.vector.tensor_scalar(one(self.conv_out)[:, 2:].rearrange("p (n t) -> p n t", t=2),
                                    self.samples(u)[:, :, NT:NT + 2], 1.0, None, ALU.mult).then_inc(S["saved"], 1)
        else:
            nc.vector.tensor_scalar(one(self.carry), end, 1.0, None, ALU.mult).then_inc(S["saved"], 1)
        if b == 1:
            dve.wait_ge(S["gelued"], turn + 1)
            dve.wait_ge(S["tap2"], m + 1)
            if not first:
                dve.wait_ge(S["g_low"], turn)
            g, ge, v = self.g, self.ge, self.c[:, 1]
            q = self.prompt
            if self.last:
                new = lambda z: z[:, 2 + q:2 + q + NB * (2 + NT) - 2]
                nc.vector.tensor_tensor(g[:, 0:q], ge[:, 0:q], v[:, 0:q], ALU.mult)
                at = lambda z: z[:, 2 + q:2 + q + (NB - 1) * (2 + NT)].rearrange("p (n t) -> p n t", t=2 + NT)
                nc.vector.tensor_tensor(g[:, q:TH - NT].rearrange("p (n t) -> p n t", t=NT), at(ge)[:, :, 0:NT],
                                        at(v)[:, :, 0:NT], ALU.mult)
                end = 2 + q + (NB - 1) * (2 + NT)
                ins = nc.vector.tensor_tensor(g[:, TH - NT:TH], ge[:, end:end + NT], v[:, end:end + NT], ALU.mult)
            else:
                ins = nc.vector.tensor_tensor(g[:], ge[:], v, ALU.mult)
            ins.then_inc(S["gated"], 1)

    def dve_end(self, dve, ntiles):
        self.low(dve, ntiles // 2 - 1)
        dve.wait_ge(self.S["g_low"], ntiles // 2)
        dve.wait_ge(self.S["saved"], ntiles)

    def pool(self, pool, m, b, turn, first):
        S, nc = self.S, self.nc
        if not first:
            pool.wait_ge(S["tap2"], m - 1)
            pool.wait_ge(S["saved"], m - 1)
        u = self.u[:, b]
        one = lambda z: z[:, ds(m, 1)]
        ins = nc.gpsimd.tensor_copy(u[:, 0:2], one(self.carry).rearrange("p a t -> p (a t)"))
        if self.last:
            ins = nc.gpsimd.tensor_copy(self.samples(u)[:, :, 0:2],
                                        one(self.states).rearrange("p a (n t) -> p (a n) t", t=2))
        ins.then_inc(S["led"], 1)


def run_tiles(eng, ntiles, step, trail=None):
    peeled = min(2 if trail else 1, ntiles // 2)
    for m in range(2 * peeled):
        step(m, m % 2, m // 2, m < 2)
        if trail and m >= 1:
            trail(m - 1, (m - 1) % 2, (m - 1) // 2, m - 1 < 2)
    if ntiles > 2 * peeled:
        with eng.Fori(peeled, ntiles // 2) as i:
            step(i * 2, 0, i, False)
            if trail:
                trail(i * 2 - 1, 1, i - 1, False)
            step(i * 2 + 1, 1, i, False)
            if trail:
                trail(i * 2, 0, i, False)
    if trail:
        trail(ntiles - 1, 1, ntiles // 2 - 1, ntiles == 2)


def project(kit, name, ntiles, kt, units, w_dram, Xh, Xl, parts, make_evac):
    nc = kit.nc
    rounded, residued, multiplied, drained = (kit.sem(f"{name}_{s}") for s in
                                              ("rounded", "residued", "multiplied", "drained"))
    fetched = [kit.sem(f"{name}_fetched{b}") for b in range(2)]
    passes = 3
    with ExitStack() as ctx:
        raw = kit.sb(ctx, name + "_raw", [P, 2, kt, P])
        wh = kit.sb(ctx, name + "_wh", [P, 2, kt, P], F32R)
        wl = kit.sb(ctx, name + "_wl", [P, 2, kt, P], F32R)
        acc = kit.ps(ctx, name + "_acc", [P, 2, len(parts), 512])
        ev = make_evac(ctx)
        ev.multiplied, ev.drained, ev.acc, ev.units = multiplied, drained, acc, units
        ev.name = name
        block = ctx.enter_context(nc.Block())

        def each_unit(m, b, turn):
            for u in range(units):
                local = b * units + u
                yield m * units + u, local % 2, turn * units + local // 2, u

        @block.sync
        def _(sp):
            def fetch(m, b, turn, first):
                for j, buf, use, u in each_unit(m, b, turn):
                    if not (isinstance(j, int) and j < 2):
                        sp.wait_ge(residued, j - 1)
                    src = w_dram[j] if isinstance(j, int) else w_dram[ds(j, 1)].rearrange("a p n -> (a p) n")
                    sp.dma_start(raw[:, buf].rearrange("p k m -> p (k m)"), src).then_inc(fetched[buf], 16)
            run_tiles(sp, ntiles, fetch)

        @block.scalar
        def _(act):
            def round_up(m, b, turn, first):
                for j, buf, use, u in each_unit(m, b, turn):
                    act.wait_ge(fetched[buf], (use + 1) * 16)
                    if not (isinstance(j, int) and j < 2):
                        act.wait_ge(multiplied, j - 1)
                    nc.scalar.activation(wh[:, buf], raw[:, buf], ACT.Copy).then_inc(rounded, 1)

            run_tiles(act, ntiles, round_up,
                      lambda m, b, turn, first: ev.act(act, m, b, turn, first))
            if hasattr(ev, "act_end"):
                ev.act_end(act, ntiles)

        @block.vector
        def _(dve):
            def residue(m, b, turn, first):
                for j, buf, use, u in each_unit(m, b, turn):
                    dve.wait_ge(rounded, j + 1)
                    nc.vector.tensor_tensor(wl[:, buf], raw[:, buf], wh[:, buf].bitcast(F32),
                                            ALU.subtract).then_inc(residued, 1)
            trail = (lambda m, b, turn, first: ev.dve(dve, m, b, turn, first)) if hasattr(ev, "dve") else None
            run_tiles(dve, ntiles, residue, trail)
            if hasattr(ev, "dve_end"):
                ev.dve_end(dve, ntiles)

        @block.tensor
        def _(pe):
            def multiply(m, b, turn, first):
                for j, buf, use, u in each_unit(m, b, turn):
                    pe.wait_ge(residued, j + 1)
                    if u == 0 and not first:
                        pe.wait_ge(drained, m - 1)
                    for n, (at, size) in enumerate(parts):
                        for k in range(kt):
                            for q, (w, x) in enumerate(((wh, Xh), (wh, Xl), (wl, Xh))):
                                last = nc.tensor.matmul(acc[:, b, n, 0:size], w[:, buf, k, :],
                                                        x[:, u * kt + k, at:at + size],
                                                        start=(u == 0 and k == 0 and q == 0),
                                                        stop=(u == units - 1 and k == kt - 1 and q == passes - 1))
                    last.then_inc(multiplied, 1)
            run_tiles(pe, ntiles, multiply)

        if hasattr(ev, "pool"):
            @block.gpsimd
            def _(pool):
                run_tiles(pool, ntiles, lambda m, b, turn, first: ev.pool(pool, m, b, turn, first))
                if hasattr(ev, "pool_end"):
                    ev.pool_end(pool, ntiles)


def run_units(eng, stages):
    per = 2 * SEQ // P

    def step(j, u):
        for stage, lag in stages:
            if isinstance(j, int) and not 0 <= per * j + u - lag < HEADS // 2 * per:
                continue
            if u >= lag:
                stage(j, u - lag)
            else:
                stage(j - 1, u - lag + per)

    for u in range(per):
        step(0, u)
    with eng.Fori(1, HEADS // 2) as j:
        for u in range(per):
            step(j, u)
    for u in range(max(lag for _, lag in stages)):
        step(HEADS // 2, u)


def attend_prompt(kit, proj, oT, ident, identb, causal, neg_lam):
    nc = kit.nc
    NQ = SEQ // P
    names = ("qk_in", "v_in", "v_turned", "v_kept", "scored", "peaked", "biased", "exped", "inverted", "coefd",
             "w_first", "weighted", "turned", "kept", "summed", "evacuated", "high", "low")
    S = {n: kit.sem("ap_" + n) for n in names}
    head_out = [kit.sem(f"ap_head_out{b}") for b in range(2)]
    SCALE = DH ** -0.5
    with ExitStack() as ctx:
        dup = kit.sb(ctx, "ap_dup", [P, 2, 2, SEQ])
        qs = kit.sb(ctx, "ap_qs", [P, 2, 2, SEQ], F32R)
        kh = kit.sb(ctx, "ap_kh", [P, 2, 2, SEQ], F32R)
        kl = kit.sb(ctx, "ap_kl", [P, 2, 2, SEQ], F32R)
        vin = kit.sb(ctx, "ap_vin", [P, SEQ])
        vt = kit.sb(ctx, "ap_vt", [P, 2, NQ, P])
        pexp = kit.sb(ctx, "ap_pexp", [P, 2, 2, SEQ])
        wgt = kit.sb(ctx, "ap_wgt", [P, 2, SEQ])
        wT = kit.sb(ctx, "ap_wT", [P, 2, NQ, P])
        small = kit.sb(ctx, "ap_small", [P, 2, 10])
        out = kit.sb(ctx, "ap_out", [P, 2, SEQ])
        sc = kit.ps(ctx, "ap_sc", [P, 2, SEQ])
        tp = kit.ps(ctx, "ap_tp", [P, NQ, P])
        pv = kit.ps(ctx, "ap_pv", [P, 2, 512])
        block = ctx.enter_context(nc.Block())
        unit = lambda j, u: j * (2 * NQ) + u
        head_of = lambda j, u: j * 2 + u // NQ
        early = lambda j, u, n: isinstance(j, int) and j * 2 * NQ + u < n

        @block.sync
        def _(sp):
            def load(h, first):
                if not first:
                    sp.wait_ge(S["low"], h * 4)
                tile = lambda n: proj[n] if isinstance(n, int) else proj[ds(n, 1)].rearrange("a p t -> (a p) t")
                for n in range(2):
                    src = tile(h + n * HEADS)[:, 0:SEQ].rearrange("(c r) t -> r c t", c=2)
                    for rows in (slice(0, DH), slice(DH, P)):
                        sp.dma_start(dup[rows, n], src).then_inc(S["qk_in"], 16)
                if not first:
                    sp.wait_ge(S["v_turned"], h)
                sp.dma_start(vin[:], tile(h + 2 * HEADS)[:, 0:SEQ]).then_inc(S["v_in"], 16)

            def head(h, b):
                load(h + 1, False)
                sp.wait_ge(S["evacuated"], (h + 1) * NQ)
                dst = oT[h] if isinstance(h, int) else oT[ds(h, 1)].rearrange("a p t -> (a p) t")
                sp.dma_start(dst[:, 0:SEQ], out[:, b]).then_inc(head_out[b], 16)

            load(0, True)
            for b in range(2):
                head(b, b)
            with sp.Fori(1, HEADS // 2) as j:
                for b in range(2):
                    head(j * 2 + b, b)
            for b in range(2):
                sp.wait_ge(head_out[b], 16 * (HEADS // 2))
            sp.wait_ge(S["v_in"], 16 * (HEADS + 1))

        @block.tensor
        def _(pe):
            def score(j, u):
                s, h, hb, i = unit(j, u), head_of(j, u), u // NQ, u % NQ
                if i == 0:
                    pe.wait_ge(S["high"], (h + 1) * 4)
                    pe.wait_ge(S["low"], (h + 1) * 4)
                keys = (i + 1) * P
                for c in range(2):
                    if not early(j, u, 1):
                        pe.wait_ge(S["exped"], s * 2 - 1 + c)
                    for at in range(0, keys, 512):
                        n = min(512, keys - at)
                        diag = at + n == keys
                        for k in (kh, kl):
                            last = nc.tensor.matmul(sc[:, c, at:at + n], qs[:, hb, c, i * P:(i + 1) * P],
                                                    k[:, hb, c, at:at + n], start=(k is kh),
                                                    stop=(k is kl and not diag))
                        if diag:
                            last = nc.tensor.matmul(sc[:, c, i * P:keys], identb, causal, start=False, stop=True)
                    last.then_inc(S["scored"], 1)

            def turn_v(j, u):
                s, h, i = unit(j, u), head_of(j, u), u % NQ
                if i != 1:
                    return
                pe.wait_ge(S["v_in"], (h + 1) * 16)
                if not early(j, u, NQ):
                    pe.wait_ge(S["kept"], s - 2)
                for n in range(NQ):
                    last = nc.tensor.transpose(tp[:, n, :], vin[:, n * P:(n + 1) * P], ident)
                last.then_inc(S["v_turned"], 1)

            def turn(j, u):
                s, h, i = unit(j, u), head_of(j, u), u % NQ
                pe.wait_ge(S["weighted"], s + 1)
                if not early(j, u, 1):
                    pe.wait_ge(S["kept"], s)
                if early(j, u, 1):
                    pe.wait_ge(S["v_kept"], 1)
                elif i == NQ - 1 and not (isinstance(j, int) and h == HEADS - 1):
                    pe.wait_ge(S["v_kept"], h + 2)
                for n in range(i + 1):
                    last = nc.tensor.transpose(tp[:, n, :], wgt[:, u % 2, n * P:(n + 1) * P], ident)
                last.then_inc(S["turned"], 1)

            def values(j, u):
                s, h, hb, i = unit(j, u), head_of(j, u), u // NQ, u % NQ
                if i == 0:
                    pe.wait_ge(S["v_kept"], h + 1)
                pe.wait_ge(S["kept"], s + 1)
                if not early(j, u, 2):
                    pe.wait_ge(S["evacuated"], s - 1)
                for n in range(i + 1):
                    last = nc.tensor.matmul(pv[:, u % 2, 0:P], vt[:, hb, n, :], wT[:, u % 2, n, :],
                                            start=(n == 0), stop=(n == i))
                last.then_inc(S["summed"], 1)

            run_units(pe, ((score, 0), (turn_v, 0), (turn, 2), (values, 3)))

        @block.vector
        def _(dve):
            def low(h, hb, part):
                n, c = part // 2, part % 2
                dve.wait_ge(S["high"], h * 4 + part + 1)
                if n == 0:
                    nc.vector.tensor_tensor(qs[DH:P, hb, c], dup[DH:P, 0, c], qs[DH:P, hb, c].bitcast(F32),
                                            ALU.subtract).then_inc(S["low"], 1)
                else:
                    nc.vector.tensor_tensor(kl[:, hb, c], dup[:, 1, c], kh[:, hb, c].bitcast(F32),
                                            ALU.subtract).then_inc(S["low"], 1)

            def peak(j, u):
                s, b, keys = unit(j, u), u % 2, (u % NQ + 1) * P
                for c in range(2):
                    dve.wait_ge(S["scored"], s * 2 + c + 1)
                    nc.vector.tensor_reduce(small[:, b, c:c + 1], sc[:, c, 0:keys], AX, ALU.max)\
                        .then_inc(S["peaked"], 1)
                    dve.wait_ge(S["peaked"], s * 2 + c + 1)
                    nc.vector.tensor_scalar(small[:, b, 2 + c:3 + c], small[:, b, c:c + 1], -SCALE, None,
                                            ALU.mult).then_inc(S["biased"], 1)

            def weight(j, u):
                s, b, keys = unit(j, u), u % 2, (u % NQ + 1) * P
                dve.wait_ge(S["exped"], s * 2 + 2)
                nc.vector.reciprocal(small[:, b, 6:8], small[:, b, 4:6]).then_inc(S["inverted"], 1)
                dve.wait_ge(S["inverted"], s + 1)
                nc.vector.tensor_scalar(small[:, b, 8:9], small[:, b, 7:8], neg_lam, None,
                                        ALU.mult).then_inc(S["coefd"], 1)
                if not early(j, u, 2):
                    dve.wait_ge(S["turned"], s - 1)
                nc.vector.tensor_scalar(wgt[:, b, 0:keys], pexp[:, b, 0, 0:keys], small[:, b, 6:7], None,
                                        ALU.mult).then_inc(S["w_first"], 1)
                dve.wait_ge(S["coefd"], s + 1)
                dve.wait_ge(S["w_first"], s + 1)
                nc.vector.scalar_tensor_tensor(wgt[:, b, 0:keys], pexp[:, b, 1, 0:keys], small[:, b, 8:9],
                                               wgt[:, b, 0:keys], ALU.mult, ALU.add).then_inc(S["weighted"], 1)

            def split(j, u):
                if u % NQ >= NQ - 4:
                    low(head_of(j, u) + 1, 1 - u // NQ, u % NQ - (NQ - 4))

            for part in range(4):
                low(0, 0, part)
            run_units(dve, ((peak, 0), (weight, 1), (split, 0)))

        @block.scalar
        def _(act):
            def high(h, hb, part):
                n, c = part // 2, part % 2
                nc.scalar.activation((qs, kh)[n][:, hb, c], dup[:, n, c], ACT.Copy).then_inc(S["high"], 1)

            def split(j, u):
                i, h = u % NQ, head_of(j, u) + 1
                if i >= NQ - 5 and i < NQ - 1:
                    if i == NQ - 5:
                        act.wait_ge(S["qk_in"], h * 64 + 64)
                        if not early(j, u, NQ):
                            act.wait_ge(S["scored"], (h - 1) * (2 * NQ))
                    high(h, 1 - u // NQ, i - (NQ - 5))

            def keep_v(j, u):
                h, hb = head_of(j, u), u // NQ
                if u % NQ != 1:
                    return
                act.wait_ge(S["v_turned"], h + 1)
                if not early(j, u, 2 * NQ):
                    act.wait_ge(S["summed"], (h - 1) * NQ)
                nc.scalar.activation(vt[:, hb], tp[:], ACT.Copy).then_inc(S["v_kept"], 1)

            def exponential(j, u):
                s, b, keys = unit(j, u), u % 2, (u % NQ + 1) * P
                if not early(j, u, 2):
                    act.wait_ge(S["weighted"], s - 1)
                for c in range(2):
                    act.wait_ge(S["biased"], s * 2 + c + 1)
                    nc.scalar.activation(pexp[:, b, c, 0:keys], sc[:, c, 0:keys], ACT.Exp,
                                         bias=small[:, b, 2 + c:3 + c], scale=SCALE,
                                         accum_out=small[:, b, 4 + c:5 + c]).then_inc(S["exped"], 1)

            def keep(j, u):
                s, b, i = unit(j, u), u % 2, u % NQ
                act.wait_ge(S["turned"], s + 1)
                if not early(j, u, 2):
                    act.wait_ge(S["summed"], s - 1)
                nc.scalar.activation(wT[:, b, 0:i + 1, :], tp[:, 0:i + 1, :], ACT.Copy).then_inc(S["kept"], 1)

            def leave(j, u):
                s, h, hb, i = unit(j, u), head_of(j, u), u // NQ, u % NQ
                act.wait_ge(S["summed"], s + 1)
                if i == 0 and not early(j, u, 2 * NQ):
                    act.wait_ge(head_out[hb], j * 16)
                nc.scalar.activation(out[:, hb, i * P:(i + 1) * P], pv[:, u % 2, 0:P],
                                     ACT.Copy).then_inc(S["evacuated"], 1)

            act.wait_ge(S["qk_in"], 64)
            for part in range(4):
                high(0, 0, part)
            run_units(act, ((keep_v, 0), (exponential, 0), (keep, 2), (leave, 3), (split, 0)))


def attend_sample(kit, a, proj, oT, ident, identb, neg_lam_rows):
    nc = kit.nc
    SCALE = DH ** -0.5
    W = PAGES * PAGE + NS
    names = ("table_in", "small_in", "q_zeroed", "q_placed", "v_turned", "v_kept", "scored", "peaked", "biased",
             "exped", "inverted", "scaled", "combined", "turned", "kept", "summed", "evacuated", "stored", "q_picked",
             "w_zeroed", "out_turned", "out_kept")
    S = {n: kit.sem("as_" + n) for n in names}
    k_in = [kit.sem(f"as_k_in{b}") for b in range(2)]
    v_in = [kit.sem(f"as_v_in{b}") for b in range(2)]
    with ExitStack() as ctx:
        table = kit.sb(ctx, "as_table", [1, NB * PAGES], I32)
        qkv = kit.sb(ctx, "as_qkv", [P, 3, HEADS, NS])
        qd = kit.sb(ctx, "as_qd", [P, NB, HEADS, 32])
        qb = kit.sb(ctx, "as_qb", [P, 2, HEADS, 32])
        vnew = kit.sb(ctx, "as_vnew", [NS, HEADS, P])
        mask = kit.sb(ctx, "as_mask", [P, NB * NS], BF16)
        comb = kit.sb(ctx, "as_comb", [P, 18])
        kT = kit.sb(ctx, "as_kT", [P, 2, PAGES, HEADS, PAGE])
        vp = kit.sb(ctx, "as_vp", [P, 2, PAGES, HEADS * P])
        pexp = kit.sb(ctx, "as_pexp", [P, 2, W])
        small = kit.sb(ctx, "as_small", [P, 2, 6])
        combs = kit.sb(ctx, "as_combs", [P, 2, 16])
        wT = kit.sb(ctx, "as_wT", [P, 2, PAGES + 1, HEADS, 32])
        rows_out = kit.sb(ctx, "as_rows_out", [P, NB, P])
        out = kit.sb(ctx, "as_out", [P, HEADS, NS])
        sc = kit.ps(ctx, "as_sc", [P, 3 * 512])
        tp = kit.ps(ctx, "as_tp", [P, 512])
        pv = kit.ps(ctx, "as_pv", [P, 512])
        vps = kit.ps(ctx, "as_vps", [P, 512])
        ot = kit.ps(ctx, "as_ot", [P, NB, P])
        block = ctx.enter_context(nc.Block())

        def pages(eng, n, b, dst, pool_dram, arrived):
            for j in range(PAGES):
                page = eng.value_load(table[0:1, ds(n * PAGES + j, 1)], min_val=0, max_val=POOL - 1)
                eng.dma_start(dst[:, b, j].rearrange("p h c -> p (h c)") if len(dst.shape) == 5 else dst[:, b, j],
                              pool_dram[ds(page, 1)].rearrange("a p n -> (a p) n")).then_inc(arrived[b], 16)

        @block.sync
        def _(sp):
            sp.dma_start(table[:], a["table"]).then_inc(S["table_in"], 16)
            for j in range(3):
                sp.dma_start(qkv[:, j], proj[j * HEADS:(j + 1) * HEADS, :, SEQ:T].rearrange("h p t -> p h t"))\
                    .then_inc(S["small_in"], 16)
            sp.dma_start(mask[:], a["new_mask"]).then_inc(S["small_in"], 16)
            sp.dma_start(comb[:, 0:17], a["comb"]).then_inc(S["small_in"], 16)
            sp.wait_ge(S["table_in"], 16)
            pages(sp, 0, 0, kT, a["k_pool"], k_in)
            pages(sp, 1, 1, kT, a["k_pool"], k_in)
            with sp.Fori(1, NB // 2) as i:
                for b in range(2):
                    sp.wait_ge(S["scored"], i * 2 + b - 1)
                    pages(sp, i * 2 + b, b, kT, a["k_pool"], k_in)
            sp.wait_ge(S["out_kept"], 1)
            sp.dma_start(oT.rearrange("h p t -> p h t")[:, :, SEQ:T], out[:]).then_inc(S["stored"], 16)
            sp.wait_ge(S["stored"], 16)

        @block.gpsimd
        def _(pool):
            nc.gpsimd.memset(qd[:], 0.0).then_inc(S["q_zeroed"], 1)
            nc.gpsimd.memset(wT[:], 0.0).then_inc(S["w_zeroed"], 1)
            pool.wait_ge(S["small_in"], 16 * 5)
            pool.wait_ge(S["q_zeroed"], 1)
            pool.wait_ge(S["w_zeroed"], 1)
            for c in range(2):
                rows = slice(c * DH, (c + 1) * DH)
                for h in range(HEADS):
                    nc.gpsimd.tensor_copy(qd[rows, :, h, c * NT:(c + 1) * NT],
                                          qkv[rows, 0, h, :].rearrange("p (n t) -> p n t", t=NT))\
                        .then_inc(S["q_placed"], 1)
            pool.wait_ge(S["q_placed"], 2 * HEADS)

            def pick(n, b, first):
                if not first:
                    pool.wait_ge(S["scored"], n - 1)
                nc.gpsimd.tensor_copy(qb[:, b], qd[:, ds(n, 1)].rearrange("p a h c -> p (a h) c"))\
                    .then_inc(S["q_picked"], 1)
            pick(0, 0, True)
            pick(1, 1, True)
            pool.wait_ge(S["table_in"], 16)
            pages(pool, 0, 0, vp, a["v_pool"], v_in)
            pages(pool, 1, 1, vp, a["v_pool"], v_in)
            with pool.Fori(1, NB // 2) as i:
                for b in range(2):
                    pick(i * 2 + b, b, False)
                    pool.wait_ge(S["summed"], i * 2 + b - 1)
                    pages(pool, i * 2 + b, b, vp, a["v_pool"], v_in)

        @block.tensor
        def _(pe):
            pe.wait_ge(S["small_in"], 16 * 5)
            for h in range(HEADS):
                last = nc.tensor.transpose(vps[0:NS, h * P:(h + 1) * P], qkv[:, 2, h, :], ident)
            last.then_inc(S["v_turned"], 1)
            pe.wait_ge(S["v_kept"], 1)

            def back(n, b, turn, first):
                pe.wait_ge(S["combined"], n + 1)
                if not first:
                    pe.wait_ge(S["kept"], n)
                for j in range(PAGES + 1):
                    keys = PAGE if j < PAGES else NS
                    last = nc.tensor.matmul(tp[0:keys, j * 16:(j + 1) * 16],
                                            pexp[:, b, j * PAGE:j * PAGE + keys], combs[:, b, :],
                                            start=True, stop=True)
                last.then_inc(S["turned"], 1)
                pe.wait_ge(v_in[b], (turn + 1) * 16 * PAGES)
                pe.wait_ge(S["kept"], n + 1)
                if not first:
                    pe.wait_ge(S["evacuated"], n)
                for h in range(HEADS):
                    for j in range(PAGES + 1):
                        if j < PAGES:
                            v, w = vp[:, b, j, h * P:(h + 1) * P], wT[:, b, j, h, :]
                        else:
                            v, w = vnew[:, h, :], wT[0:NS, b, j, h, :]
                        last = nc.tensor.matmul(pv[32 * h:32 * h + 32, 0:P], w, v, start=(j == 0), stop=(j == PAGES))
                last.then_inc(S["summed"], 1)

            def front(n, b, turn, first):
                pe.wait_ge(k_in[b], (turn + 1) * 16 * PAGES)
                pe.wait_ge(S["q_picked"], n + 1)
                if not (isinstance(n, int) and n == 0):
                    pe.wait_ge(S["exped"], n)
                for h in range(HEADS):
                    rows = slice(32 * h, 32 * h + 32)
                    for half in range(2):
                        last = nc.tensor.matmul(sc[rows, half * 512:(half + 1) * 512], qb[:, b, h, :],
                                                kT[:, b, half * 4:half * 4 + 4, h, :], start=True, stop=True)
                    last = nc.tensor.matmul(sc[rows, 1024:W], qb[:, b, h, :], qkv[:, 1, h, :],
                                            start=True, stop=False, skip_group_check=True)
                nc.tensor.matmul(sc[:, 1024:W], identb, mask[:, ds(n * NS, NS)], start=False, stop=True,
                                 skip_group_check=True).then_inc(S["scored"], 1)

            front(0, 0, 0, True)
            front(1, 1, 0, True)
            back(0, 0, 0, True)
            front(2, 0, 1, False)
            back(1, 1, 0, False)
            front(3, 1, 1, False)
            back(2, 0, 1, False)
            with pe.Fori(2, NB // 2) as i:
                front(i * 2, 0, i, False)
                back(i * 2 - 1, 1, i - 1, False)
                front(i * 2 + 1, 1, i, False)
                back(i * 2, 0, i, False)
            back(NB - 1, 1, NB // 2 - 1, False)
            pe.wait_ge(S["evacuated"], NB)
            for n in range(NB):
                last = nc.tensor.transpose(ot[:, n, :], rows_out[:, n, :], ident)
            last.then_inc(S["out_turned"], 1)

        @block.vector
        def _(dve):
            dve.wait_ge(S["w_zeroed"], 1)
            dve.wait_ge(S["v_turned"], 1)
            nc.vector.tensor_copy(vnew[:].rearrange("p h c -> p (h c)"), vps[0:NS, :]).then_inc(S["v_kept"], 1)

            def front(n, b, first):
                dve.wait_ge(S["scored"], n + 1)
                nc.vector.tensor_reduce(small[:, b, 0:1], sc[:, 0:W], AX, ALU.max).then_inc(S["peaked"], 1)
                dve.wait_ge(S["peaked"], n + 1)
                nc.vector.tensor_scalar(small[:, b, 1:2], small[:, b, 0:1], -SCALE, None,
                                        ALU.mult).then_inc(S["biased"], 1)
                dve.wait_ge(S["exped"], n + 1)
                nc.vector.reciprocal(small[:, b, 3:4], small[:, b, 2:3]).then_inc(S["inverted"], 1)
                dve.wait_ge(S["inverted"], n + 1)
                nc.vector.tensor_scalar(small[:, b, 4:5], small[:, b, 3:4], neg_lam_rows, None,
                                        ALU.mult).then_inc(S["scaled"], 1)
                dve.wait_ge(S["scaled"], n + 1)
                if not first:
                    dve.wait_ge(S["turned"], n - 1)
                nc.vector.tensor_scalar(combs[:, b, :], comb[:, 0:16], small[:, b, 4:5], None,
                                        ALU.mult).then_inc(S["combined"], 1)

            def back(n, b, first):
                dve.wait_ge(S["turned"], n + 1)
                if not first:
                    dve.wait_ge(S["summed"], n - 1)
                tokens = lambda z, j: z.rearrange("p (j h t) -> p j h t", j=j, t=NT)
                nc.vector.tensor_copy(wT[:, b, 0:PAGES, :, 0:NT], tokens(tp[:, 0:PAGES * 16], PAGES))
                nc.vector.tensor_copy(wT[0:NS, b, PAGES:, :, 0:NT],
                                      tokens(tp[0:NS, PAGES * 16:(PAGES + 1) * 16], 1)).then_inc(S["kept"], 1)
                dve.wait_ge(S["summed"], n + 1)
                nc.vector.tensor_copy(rows_out[:, ds(n, 1)].rearrange("p a c -> p (a c)"), pv[:, 0:P])\
                    .then_inc(S["evacuated"], 1)
            front(0, 0, True)
            front(1, 1, True)
            back(0, 0, True)
            front(2, 0, False)
            back(1, 1, True)
            front(3, 1, False)
            back(2, 0, False)
            with dve.Fori(2, NB // 2) as i:
                front(i * 2, 0, False)
                back(i * 2 - 1, 1, False)
                front(i * 2 + 1, 1, False)
                back(i * 2, 0, False)
            back(NB - 1, 1, False)
            dve.wait_ge(S["out_turned"], 1)
            nc.vector.tensor_copy(out[:].rearrange("p h (n t) -> p n h t", t=NT),
                                  ot[:].rearrange("p n (h c) -> p n h c", c=32)[:, :, :, 0:NT])\
                .then_inc(S["out_kept"], 1)

        @block.scalar
        def _(act):
            def step(n, b, first):
                act.wait_ge(S["biased"], n + 1)
                if not first:
                    act.wait_ge(S["turned"], n - 1)
                nc.scalar.activation(pexp[:, b, :], sc[:, 0:W], ACT.Exp, bias=small[:, b, 1:2], scale=SCALE,
                                     accum_out=small[:, b, 2:3]).then_inc(S["exped"], 1)
            step(0, 0, True)
            step(1, 1, True)
            with act.Fori(1, NB // 2) as i:
                for b in range(2):
                    step(i * 2 + b, b, False)

NPAIR = 4
NSTEP = 6
NLEV = 6


def rwkv_mix(kit, ctx, a, proj, param, dsts):
    nc = kit.nc
    S = {n: kit.sem("mx_" + n) for n in ("state_in", "differed", "mixed")}
    cur_in = [kit.sem(f"mx_cur_in{b}") for b in range(2)]
    with ExitStack() as inner:
        cur = kit.sb(inner, "mx_cur", [P, 2, T])
        dif = kit.sb(inner, "mx_dif", [P, 2, T])
        st = kit.sb(inner, "mx_st", [P, 14, NB])
        block = inner.enter_context(nc.Block())

        @block.sync
        def _(sp):
            sp.dma_start(st[:], a["shiftT"]).then_inc(S["state_in"], 16)
            for j in range(14):
                if j >= 2:
                    sp.wait_ge(S["mixed"], j - 1)
                sp.dma_start(cur[:, j % 2], proj[12 + j]).then_inc(cur_in[j % 2], 16)

        @block.gpsimd
        def _(pool):
            pool.wait_ge(S["state_in"], 16)
            for j in range(14):
                b = j % 2
                pool.wait_ge(cur_in[b], 16 * (j // 2 + 1))
                if j >= 2:
                    pool.wait_ge(S["mixed"], j - 1)
                c, d = cur[:, b], dif[:, b]
                cs, dd = (z[:, SEQ:].rearrange("p (n t) -> p n t", t=NT) for z in (c, d))
                nc.gpsimd.tensor_tensor(d[:, 1:SEQ], c[:, 0:SEQ - 1], c[:, 1:SEQ], ALU.subtract).then_inc(S["differed"], 1)
                nc.gpsimd.tensor_scalar(d[:, 0:1], c[:, 0:1], -1.0, None, ALU.mult).then_inc(S["differed"], 1)
                nc.gpsimd.tensor_tensor(dd[:, :, 1:NT], cs[:, :, 0:NT - 1], cs[:, :, 1:NT],
                                        ALU.subtract).then_inc(S["differed"], 1)
                nc.gpsimd.tensor_tensor(dd[:, :, 0], st[:, j, :], cs[:, :, 0], ALU.subtract).then_inc(S["differed"], 1)

        @block.vector
        def _(dve):
            for j in range(14):
                dve.wait_ge(S["differed"], 4 * (j + 1))
                nc.vector.scalar_tensor_tensor(dsts[j], dif[:, j % 2], param("mu", 14)[:, j:j + 1], cur[:, j % 2],
                                               ALU.mult, ALU.add).then_inc(S["mixed"], 1)
            dve.wait_ge(S["mixed"], 14)


def rwkv_prepare(kit, ctx, a, param, Rm, Km, V, X12, XG, NR, Bc, Kc, BON, G, ELC, SD):
    nc = kit.nc
    names = ("w_in", "kaed", "tanhed", "z", "za", "g", "ss", "rks", "th", "ta", "g_kept", "rooted", "e_in",
             "e_ex", "e_neg", "lw", "av", "kk", "sq", "ssm", "inv", "kn", "bv", "fv", "kp", "rk", "rk2", "bonus",
             "lin", "lex", "nr0", "nr1", "bc", "kc", "elc", "sd", "sdw", "xg1", "xg2")
    S = {n: kit.sem("rp_" + n) for n in names}
    with ExitStack() as inner:
        w2 = kit.sb(inner, "rp_w2", [P, 512])
        g2 = kit.sb(inner, "rp_g2", [P, 512])
        blk = kit.sb(inner, "rp_blk", [P, P])
        reset = kit.sb(inner, "rp_reset", [P, SEQ], BF16)
        hc = kit.sb(inner, "rp_hc", [P, 12])
        tw = kit.sb(inner, "rp_tw", [P, T])
        tv = kit.sb(inner, "rp_tv", [P, T])
        ta = kit.sb(inner, "rp_ta", [P, T])
        tk = kit.sb(inner, "rp_tk", [P, T])
        tq = kit.sb(inner, "rp_tq", [P, T])
        tl = kit.sb(inner, "rp_tl", [P, 2, SEQ])
        te = kit.sb(inner, "rp_te", [P, 3, SEQ])
        pz = kit.ps(inner, "rp_pz", [P, 3, 512])
        pq = kit.ps(inner, "rp_pq", [P, 3, 512])
        block = inner.enter_context(nc.Block())
        part = lambda z: z.rearrange("p (n t) -> p n t", t=T3)

        @block.sync
        def _(sp):
            for dst, src in ((w2[0:64, :], a["w2"]), (w2[64:128, :], a["a2"]), (g2[:], a["g2"]),
                             (blk[:], a["blockones"]), (reset[:], a["reset"])):
                sp.dma_start(dst, src).then_inc(S["w_in"], 16)

        @block.tensor
        def _(pe):
            def product(psum, lhsT, rhs, sem):
                for n in range(3):
                    last = nc.tensor.matmul(psum[:, n, 0:T3], lhsT, rhs[:, n * T3:(n + 1) * T3], start=True, stop=True)
                last.then_inc(S[sem], 1)
            pe.wait_ge(S["w_in"], 80)
            for p in range(NPAIR):
                cs = slice(p * P, (p + 1) * P)
                pe.wait_ge(S["tanhed"], 1)
                if p:
                    pe.wait_ge(S["bonus"], p)
                product(pz, w2[0:64, cs], X12[0:64, :], "z")
                if p:
                    pe.wait_ge(S["ssm"], p)
                product(pq, w2[64:128, cs], X12[64:128, :], "za")
                pe.wait_ge(S["th"], p + 1)
                pe.wait_ge(S["xg2"], 1)
                product(pz, g2[:, cs], XG, "g")
                pe.wait_ge(S["ta"], p + 1)
                pe.wait_ge(S["sq"], p + 1)
                product(pq, blk[:], tq, "ss")
                pe.wait_ge(S["g_kept"], p + 1)
                pe.wait_ge(S["rk2"], p + 1)
                product(pz, blk[:], tq, "rks")

        @block.scalar
        def _(act):
            nc.scalar.activation(X12[0:64, :], X12[0:64, :], ACT.Tanh).then_inc(S["tanhed"], 1)
            nc.scalar.activation(XG, XG, ACT.Tanh, scale=0.5).then_inc(S["xg1"], 1)
            act.wait_ge(S["kaed"], 3)
            for p in range(NPAIR):
                act.wait_ge(S["z"], p + 1)
                if p:
                    act.wait_ge(S["lw"], p)
                nc.scalar.activation(part(tw[:]), pz[:, :, 0:T3], ACT.Tanh, bias=hc[:, p:p + 1],
                                     scale=0.5).then_inc(S["th"], 1)
                act.wait_ge(S["za"], p + 1)
                if p:
                    act.wait_ge(S["fv"], p)
                    act.wait_ge(S["bv"], p)
                    act.wait_ge(S["sd"], 5 * p)
                nc.scalar.activation(part(ta[:]), pq[:, :, 0:T3], ACT.Tanh, bias=hc[:, 4 + p:5 + p],
                                     scale=0.5).then_inc(S["ta"], 1)
                act.wait_ge(S["g"], p + 1)
                nc.scalar.activation(part(G[:, p]), pz[:, :, 0:T3], ACT.Copy).then_inc(S["g_kept"], 1)
                act.wait_ge(S["lin"], p + 1)
                if p:
                    act.wait_ge(S["nr1"], p)
                    act.wait_ge(S["nr0"], p)
                    act.wait_ge(S["bc"], p)
                    act.wait_ge(S["kc"], p)
                    act.wait_ge(S["elc"], p)
                nc.scalar.activation(te[:, 0], tl[:, 0], ACT.Exp).then_inc(S["e_in"], 1)
                nc.scalar.activation(te[:, 2], tl[:, 0], ACT.Exp, scale=-1.0).then_inc(S["e_neg"], 1)
                act.wait_ge(S["lex"], p + 1)
                nc.scalar.activation(te[:, 1], tl[:, 1], ACT.Exp).then_inc(S["e_ex"], 1)
                nc.scalar.activation(SD[:, p, 0, :], tv[:, SEQ:T], ACT.Exp).then_inc(S["sdw"], 1)
                act.wait_ge(S["ssm"], p + 1)
                nc.scalar.activation(tq[:], tq[:], ACT.Sqrt).then_inc(S["rooted"], 1)

        @block.vector
        def _(dve):
            kap = param("k_a", 4)
            nc.vector.tensor_scalar(hc[:, 0:4], param("w0", 4), 0.5, None, ALU.mult).then_inc(S["kaed"], 1)
            nc.vector.tensor_scalar(hc[:, 4:8], param("a0", 4), 0.5, None, ALU.mult).then_inc(S["kaed"], 1)
            nc.vector.tensor_scalar(hc[:, 8:12], kap, -1.0, 1.0, ALU.mult, ALU.add).then_inc(S["kaed"], 1)
            dve.wait_ge(S["kaed"], 3)
            dve.wait_ge(S["xg1"], 1)
            nc.vector.tensor_scalar(XG, XG, 1.0, 0.5, ALU.add, ALU.mult).then_inc(S["xg2"], 1)
            dve.wait_ge(S["w_in"], 80)
            for p in range(NPAIR):
                col = lambda name: param(name, 4)[:, p:p + 1]
                r, k, v = Rm[:, p], Km[:, p], V[:, p]
                if p:
                    dve.wait_ge(S["kn"], p)
                    dve.wait_ge(S["bv"], p)
                    dve.wait_ge(S["nr0"], p)
                    dve.wait_ge(S["sd"], 5 * p)
                nc.vector.tensor_scalar(tk[:], k, col("k_k"), None, ALU.mult).then_inc(S["kk"], 1)
                dve.wait_ge(S["kk"], p + 1)
                if p:
                    dve.wait_ge(S["rks"], p)
                nc.vector.tensor_tensor(tq[:], tk[:], tk[:], ALU.mult).then_inc(S["sq"], 1)
                dve.wait_ge(S["th"], p + 1)
                if p:
                    dve.wait_ge(S["sdw"], p)
                nc.vector.tensor_scalar(tv[:], tw[:], 1.0, -E05 / 2, ALU.add, ALU.mult).then_inc(S["lw"], 1)
                dve.wait_ge(S["lw"], p + 1)
                if p:
                    dve.wait_ge(S["e_ex"], p)
                    dve.wait_ge(S["e_neg"], p)
                nc.vector.tensor_tensor_scan(tl[:, 0], reset[:], tv[:, 0:SEQ], 0.0, ALU.mult,
                                             ALU.add).then_inc(S["lin"], 1)
                dve.wait_ge(S["ta"], p + 1)
                nc.vector.tensor_scalar(ta[:], ta[:], 0.5, 0.5, ALU.mult, ALU.add).then_inc(S["av"], 1)
                dve.wait_ge(S["ss"], p + 1)
                nc.vector.tensor_scalar(part(tq[:]), pq[:, :, 0:T3], 1e-24, None, ALU.max).then_inc(S["ssm"], 1)
                dve.wait_ge(S["rooted"], p + 1)
                nc.vector.reciprocal(tq[:], tq[:]).then_inc(S["inv"], 1)
                dve.wait_ge(S["inv"], p + 1)
                nc.vector.tensor_tensor(tk[:], tk[:], tq[:], ALU.mult).then_inc(S["kn"], 1)
                dve.wait_ge(S["av"], p + 1)
                dve.wait_ge(S["kn"], p + 1)
                nc.vector.tensor_scalar(tq[:], ta[:], col("k_a"), hc[:, 8 + p:9 + p], ALU.mult,
                                        ALU.add).then_inc(S["fv"], 1)
                dve.wait_ge(S["fv"], p + 1)
                nc.vector.tensor_tensor(k, k, tq[:], ALU.mult).then_inc(S["kp"], 1)
                nc.vector.tensor_tensor(ta[:], tk[:], ta[:], ALU.mult).then_inc(S["bv"], 1)
                dve.wait_ge(S["kp"], p + 1)
                nc.vector.tensor_scalar(tq[:], r, col("r_k"), None, ALU.mult).then_inc(S["rk"], 1)
                dve.wait_ge(S["rk"], p + 1)
                nc.vector.tensor_tensor(tq[:], tq[:], k, ALU.mult).then_inc(S["rk2"], 1)
                dve.wait_ge(S["e_ex"], p + 1)
                nc.vector.scalar_tensor_tensor(NR[:, p, 0, :], tk[:, 0:SEQ], -1.0, te[:, 1], ALU.mult,
                                               ALU.mult).then_inc(S["nr0"], 1)
                dve.wait_ge(S["e_in"], p + 1)
                nc.vector.tensor_copy(ELC[:, p, :], te[:, 0].rearrange("p (c t) -> p c t", t=C)[:, :, C - 1])\
                    .then_inc(S["elc"], 1)
                dve.wait_ge(S["rks"], p + 1)
                nc.vector.tensor_tensor(part(BON[:, p]), pz[:, :, 0:T3], part(v), ALU.mult).then_inc(S["bonus"], 1)

        @block.gpsimd
        def _(pool):
            for p in range(NPAIR):
                r, k, v = Rm[:, p], Km[:, p], V[:, p]
                pool.wait_ge(S["lin"], p + 1)
                if p:
                    pool.wait_ge(S["e_ex"], p)
                nc.gpsimd.tensor_tensor(tl[:, 1], tl[:, 0], tv[:, 0:SEQ], ALU.subtract).then_inc(S["lex"], 1)
                pool.wait_ge(S["e_in"], p + 1)
                nc.gpsimd.tensor_tensor(NR[:, p, 1, :], r[:, 0:SEQ], te[:, 0], ALU.mult).then_inc(S["nr1"], 1)
                pool.wait_ge(S["bv"], p + 1)
                pool.wait_ge(S["e_neg"], p + 1)
                nc.gpsimd.tensor_tensor(Bc[:, p], ta[:, 0:SEQ], te[:, 2], ALU.mult).then_inc(S["bc"], 1)
                pool.wait_ge(S["kp"], p + 1)
                nc.gpsimd.tensor_tensor(Kc[:, p], k[:, 0:SEQ], te[:, 2], ALU.mult).then_inc(S["kc"], 1)
                for q, src in ((1, tk[:]), (2, ta[:]), (3, k), (4, r), (5, v)):
                    nc.gpsimd.tensor_copy(SD[:, p, q, :], src[:, SEQ:T]).then_inc(S["sd"], 1)
            pool.wait_ge(S["sd"], 5 * NPAIR)


def rwkv_transitions(kit, a, NR, BK, V, Y):
    nc = kit.nc
    names = ("const_in", "zeroed", "placed", "p1", "p2", "adi0", "adi", "m3", "m2", "m4", "turn", "kept", "vs",
             "u", "ust", "ubd", "tt", "ww", "tst", "wst", "wbd0", "wbd", "a2v", "a2v_kept", "tn", "tn_kept", "x", "xst",
             "xbd0", "xbd", "phi", "phi_kept", "rz", "r_kept", "z_kept", "yl", "y_kept")
    S = {n: kit.sem("rt_" + n) for n in names}
    with ExitStack() as ctx:
        strict = kit.sb(ctx, "rt_strict", [P, 512])
        incl = kit.sb(ctx, "rt_incl", [P, 256])
        levst = kit.sb(ctx, "rt_levst", [P, NLEV, 256])
        pairbd = kit.sb(ctx, "rt_pairbd", [P, 512])
        eyebd = kit.sb(ctx, "rt_eyebd", [P, 512])
        eyest = kit.sb(ctx, "rt_eyest", [P, 256])
        ident = kit.sb(ctx, "rt_ident", [P, P])
        wide = lambda n, *k: kit.sb(ctx, "rt_" + n, [P, 2, *k, NPAIR, P])
        slim = lambda n: kit.sb(ctx, "rt_" + n, [P, 2, NPAIR, C])
        bd, turned = wide("bd", 4), wide("turned", 4)
        adi, m2, ubd, wbd, xbd, tn = (wide(n) for n in ("adi", "m2", "ubd", "wbd", "xbd", "tn"))
        m3, m4, ust, tst, wst, vs, a2v, xst = (slim(n) for n in ("m3", "m4", "ust", "tst", "wst", "vs", "a2v", "xst"))
        q0, q1, q2, q3 = ([kit.ps(ctx, f"rt_q{n}{b}", [P, NPAIR, P]) for b in range(2)] for n in range(4))
        block = ctx.enter_context(nc.Block())
        flat = lambda z: z.rearrange("p a b -> p (a b)")
        four = lambda z: z.rearrange("p (a h c) -> p a h c", a=NPAIR, h=2)
        slots = lambda z: z.rearrange("p (a c) -> p a c", c=C)
        spread = lambda z: z.unsqueeze(2).broadcast_to([P, NPAIR, 2, C])
        half = lambda h: slice(h * C, (h + 1) * C)
        consts = ((strict, "strict"), (incl, "incl"), (levst, "levst"), (pairbd, "pairbd"),
                  (eyebd, "eyebd"), (eyest, "eyest"), (ident, "ident"))

        def turns(eng, turn):
            turn(0, True)
            with eng.Fori(1, NCH // 2) as i:
                turn(i, False)

        @block.sync
        def _(sp):
            for dst, src in consts:
                sp.dma_start(dst[:], a[src]).then_inc(S["const_in"], 16)

        @block.gpsimd
        def _(pool):
            nc.gpsimd.memset(bd[:], 0.0).then_inc(S["zeroed"], 1)
            nc.gpsimd.memset(wbd[:], 0.0).then_inc(S["zeroed"], 1)
            nc.gpsimd.memset(xbd[:], 0.0).then_inc(S["zeroed"], 1)
            pool.wait_ge(S["zeroed"], 3)
            pool.wait_ge(S["const_in"], 16 * len(consts))

            def place(i, b, first):
                c = i * 2 + b
                if not first:
                    pool.wait_ge(S["vs"], i * 2)
                    pool.wait_ge(S["turn"], i * 8 - 2 + 2 * b)
                for q, src in enumerate((BK[:, 0], BK[:, 1], V, NR[:, :, 0, :])):
                    for h in range(2):
                        nc.gpsimd.tensor_copy(bd[half(h), b, q, :, half(h)],
                                              src[half(h), :, ds(c * C, C)]).then_inc(S["placed"], 1)

            def patch(i, b):
                c = i * 2 + b
                pool.wait_ge(S["adi0"], c + 1)
                nc.gpsimd.tensor_tensor(flat(adi[:, b]), flat(adi[:, b]), eyebd[:], ALU.add).then_inc(S["adi"], 1)

            def stack_v(i, b):
                pool.wait_ge(S["kept"], i * 8 + 5 + 2 * b)
                v = turned[:, b, 2]
                nc.gpsimd.tensor_tensor(vs[:, b], v[:, :, 0:C], v[:, :, C:P], ALU.add).then_inc(S["vs"], 1)

            place(0, 0, True)
            place(0, 1, True)

            def turn(i, first):
                pool.wait_ge(S["placed"], i * 16 + 16)
                for b in range(2):
                    patch(i, b)
                for b in range(2):
                    stack_v(i, b)

            turn(0, True)
            with pool.Fori(1, NCH // 2) as i:
                for b in range(2):
                    place(i, b, False)
                turn(i, False)

        @block.tensor
        def _(pe):
            pe.wait_ge(S["const_in"], 16 * len(consts))
            mm = nc.tensor.matmul

            def turn(i, first):
                for b in range(2):
                    c = i * 2 + b
                    pe.wait_ge(S["placed"], c * 8 + 8)
                    for q, dst, freed, sem in ((0, q0, "phi_kept", "p1"), (1, q1, "z_kept", "p2")):
                        if not first:
                            pe.wait_ge(S[freed], c - 1)
                        for p in range(NPAIR):
                            last = mm(dst[b][:, p, :], bd[:, b, q, p, :], NR[:, p, :, ds(c * C, C)],
                                      start=True, stop=True)
                        last.then_inc(S[sem], 1)
                for r, (qa, qb) in enumerate(((0, 1), (2, 3))):
                    for b in range(2):
                        for n, (q, dst) in enumerate(((qa, q2), (qb, q3))):
                            if r == 1:
                                pe.wait_ge(S["kept"], i * 8 + 2 * b + n + 1)
                            elif not first:
                                pe.wait_ge(S["y_kept" if n == 0 else "tn_kept"], i * 2 - 1 + b)
                            for p in range(NPAIR):
                                last = nc.tensor.transpose(dst[b][:, p, :], bd[:, b, q, p, :], ident[:])
                            last.then_inc(S["turn"], 1)
                for lev in range(NLEV):
                    for b in range(2):
                        n = (i * NLEV + lev) * 2 + b
                        if lev == 0:
                            pe.wait_ge(S["adi"], i * 2 + b + 1)
                            pe.wait_ge(S["m3"], i * 2 + b + 1)
                        else:
                            pe.wait_ge(S["tst"], (i * (NLEV - 1) + lev - 1) * 2 + b + 1)
                        for p in range(NPAIR):
                            t = tst[:, b, p, :] if lev else slots(eyest[:])[:, p, :]
                            last = mm(q0[b][:, p, 0:C], adi[:, b, p, :], t, start=True, stop=True)
                        last.then_inc(S["u"], 1)
                    for b in range(2):
                        n = (i * NLEV + lev) * 2 + b
                        pe.wait_ge(S["ust"], n + 1)
                        if lev < NLEV - 1:
                            if lev:
                                pe.wait_ge(S["wbd"], n - 1)
                            for p in range(NPAIR):
                                w = wbd[:, b, p, :] if lev else eyebd[:, p * P:(p + 1) * P]
                                last = mm(q0[b][:, p, C:P], w, ust[:, b, p, :], start=True, stop=True)
                            last.then_inc(S["tt"], 1)
                        pe.wait_ge(S["ubd"], n + 1)
                        if lev:
                            pe.wait_ge(S["wbd"], n - 1)
                        else:
                            pe.wait_ge(S["m4"], i * 2 + b + 1)
                        for p in range(NPAIR):
                            w = wst[:, b, p, :] if lev else slots(eyest[:])[:, p, :]
                            last = mm(q1[b][:, p, C:P], ubd[:, b, p, :], w, start=True, stop=True)
                        last.then_inc(S["ww"], 1)
                for b in range(2):
                    c = i * 2 + b
                    pe.wait_ge(S["m2"], c + 1)
                    pe.wait_ge(S["vs"], c + 1)
                    pe.wait_ge(S["kept"], i * 8 + 8)
                    for p in range(NPAIR):
                        last = mm(q2[b][:, p, 0:C], m2[:, b, p, :], vs[:, b, p, :], start=True, stop=True)
                    last.then_inc(S["a2v"], 1)
                for b in range(2):
                    c = i * 2 + b
                    pe.wait_ge(S["wbd"], ((i + 1) * NLEV - 1) * 2 + b + 1)
                    for p in range(NPAIR):
                        last = mm(q3[b][:, p, :], wbd[:, b, p, :], turned[:, b, 3, p, :], start=True, stop=True)
                    last.then_inc(S["tn"], 1)
                    pe.wait_ge(S["a2v_kept"], c + 1)
                    for p in range(NPAIR):
                        last = mm(q2[b][:, p, C:P], wbd[:, b, p, :], a2v[:, b, p, :], start=True, stop=True)
                    last.then_inc(S["x"], 1)
                for b in range(2):
                    c = i * 2 + b
                    pe.wait_ge(S["tn_kept"], c + 1)
                    for p in range(NPAIR):
                        last = mm(q0[b][:, p, :], tn[:, b, p, :], turned[:, b, 0, p, :], start=True, stop=True)
                    last.then_inc(S["phi"], 1)
                    pe.wait_ge(S["xst"], c + 1)
                    for p in range(NPAIR):
                        mm(q1[b][:, p, 0:C], tn[:, b, p, :], m3[:, b, p, :], start=True, stop=True)
                        mm(q1[b][:, p, C:P], turned[:, b, 0, p, :], xst[:, b, p, :], start=True, stop=False)
                        last = mm(q1[b][:, p, C:P], turned[:, b, 1, p, :], vs[:, b, p, :], start=False, stop=True)
                    last.then_inc(S["rz"], 1)
                    pe.wait_ge(S["xbd"], c + 1)
                    for p in range(NPAIR):
                        mm(q2[b][:, p, 0:C], xbd[:, b, p, :], m3[:, b, p, :], start=True, stop=False)
                        last = mm(q2[b][:, p, 0:C], turned[:, b, 2, p, :], m4[:, b, p, :], start=False, stop=True)
                    last.then_inc(S["yl"], 1)
            turns(pe, turn)

        @block.vector
        def _(dve):
            tt = nc.vector.tensor_tensor
            dve.wait_ge(S["const_in"], 16 * len(consts))

            def turn(i, first):
                for b in range(2):
                    c = i * 2 + b
                    dve.wait_ge(S["p1"], c + 1)
                    if not first:
                        dve.wait_ge(S["yl"], c - 1)
                    tt(four(flat(adi[:, b])), spread(q0[b][:, :, 0:C]), four(strict[:]), ALU.mult).then_inc(S["adi0"], 1)
                    tt(m3[:, b], q0[b][:, :, C:P], slots(incl[:]), ALU.mult).then_inc(S["m3"], 1)
                    dve.wait_ge(S["p2"], c + 1)
                    tt(four(flat(m2[:, b])), spread(q1[b][:, :, 0:C]), four(strict[:]), ALU.mult).then_inc(S["m2"], 1)
                    tt(m4[:, b], q1[b][:, :, C:P], slots(incl[:]), ALU.mult).then_inc(S["m4"], 1)
                for lev in range(NLEV):
                    for b in range(2):
                        n = (i * NLEV + lev) * 2 + b
                        dve.wait_ge(S["u"], n + 1)
                        if not (first and lev == 0):
                            dve.wait_ge(S["ww"], n - 1)
                        tt(ust[:, b], q0[b][:, :, 0:C], slots(levst[:, lev, :]), ALU.mult).then_inc(S["ust"], 1)
                        dve.wait_ge(S["ust"], n + 1)
                        tt(four(flat(ubd[:, b])), spread(ust[:, b]), four(pairbd[:]), ALU.mult).then_inc(S["ubd"], 1)
                for b in range(2):
                    c = i * 2 + b
                    dve.wait_ge(S["tn"], c + 1)
                    nc.vector.tensor_copy(tn[:, b], q3[b][:]).then_inc(S["tn_kept"], 1)
                for b in range(2):
                    c = i * 2 + b
                    here = ds(c * C, C)
                    dve.wait_ge(S["phi"], c + 1)
                    tt(BK[:, :, :, here].rearrange("p h a c -> p a h c"), four(flat(q0[b][:])), four(eyebd[:]),
                       ALU.add).then_inc(S["phi_kept"], 1)
                    dve.wait_ge(S["rz"], c + 1)
                    tt(NR[:, :, 1, here], q1[b][:, :, 0:C], NR[:, :, 1, here], ALU.add).then_inc(S["r_kept"], 1)
                    nc.vector.tensor_copy(NR[:, :, 0, here], q1[b][:, :, C:P]).then_inc(S["z_kept"], 1)
            turns(dve, turn)
            dve.wait_ge(S["z_kept"], NCH)

        @block.scalar
        def _(act):
            def copy(out, in_, sem):
                nc.scalar.activation(out, in_, ACT.Copy).then_inc(S[sem], 1)

            act.wait_ge(S["zeroed"], 3)

            def turn(i, first):
                for r, (qa, qb) in enumerate(((0, 1), (2, 3))):
                    for b in range(2):
                        for n, (q, src) in enumerate(((qa, q2), (qb, q3))):
                            act.wait_ge(S["turn"], i * 8 + r * 4 + b * 2 + n + 1)
                            if not first and r == 0:
                                act.wait_ge(S["yl"], i * 2 - 1 + b)
                            copy(turned[:, b, q], src[b][:], "kept")
                for lev in range(NLEV):
                    for b in range(2):
                        n = (i * NLEV + lev) * 2 + b
                        if lev < NLEV - 1:
                            act.wait_ge(S["tt"], (i * (NLEV - 1) + lev) * 2 + b + 1)
                            copy(tst[:, b], q0[b][:, :, C:P], "tst")
                        act.wait_ge(S["ww"], n + 1)
                        copy(wst[:, b], q1[b][:, :, C:P], "wst")
                        for h in range(2):
                            copy(wbd[half(h), b, :, half(h)], q1[b][half(h), :, C:P], ("wbd0", "wbd")[h])
                for b in range(2):
                    act.wait_ge(S["a2v"], i * 2 + b + 1)
                    copy(a2v[:, b], q2[b][:, :, 0:C], "a2v_kept")
                for b in range(2):
                    act.wait_ge(S["x"], i * 2 + b + 1)
                    copy(xst[:, b], q2[b][:, :, C:P], "xst")
                    for h in range(2):
                        copy(xbd[half(h), b, :, half(h)], q2[b][half(h), :, C:P], ("xbd0", "xbd")[h])
                for b in range(2):
                    c = i * 2 + b
                    act.wait_ge(S["yl"], c + 1)
                    copy(Y[:, :, ds(c * C, C)], q2[b][:, :, 0:C], "y_kept")
            turns(act, turn)
            act.wait_ge(S["y_kept"], NCH)


def rwkv_scan(kit, NR, BK, ELC, Y, state_out):
    nc = kit.nc
    names = ("zeroed", "phi_in", "next", "summed", "state", "placed", "y", "y_added", "state_out")
    S = {n: kit.sem("rn_" + n) for n in names}
    with ExitStack() as ctx:
        phi = kit.sb(ctx, "rn_phi", [P, 2, NPAIR, P])
        sbd = kit.sb(ctx, "rn_sbd", [P, 2, NPAIR, P])
        states = kit.sb(ctx, "rn_states", [P, NCH + 1, NPAIR, C])
        tsum = kit.sb(ctx, "rn_tsum", [P, NPAIR, C])
        ps = [kit.ps(ctx, f"rn_ps{b}", [P, NPAIR, P]) for b in range(2)]
        py = [kit.ps(ctx, f"rn_py{b}", [P, NPAIR, P]) for b in range(2)]
        block = ctx.enter_context(nc.Block())
        half = lambda h: slice(h * C, (h + 1) * C)
        at = lambda c: states[:, ds(c, 1)].rearrange("p s a c -> p (s a) c")

        def chunks(eng, step):
            for c in range(2):
                step(c, c, True)
            with eng.Fori(1, NCH // 2) as i:
                for b in range(2):
                    step(i * 2 + b, b, False)

        @block.sync
        def _(sp):
            sp.wait_ge(S["state"], NCH)
            sp.dma_start(state_out, states[:, NCH]).then_inc(S["state_out"], 16)
            sp.wait_ge(S["state_out"], 16)

        @block.scalar
        def _(act):
            def step(c, b, first):
                if not first:
                    act.wait_ge(S["next"], c - 1)
                nc.scalar.activation(phi[:, b].rearrange("p a (h c) -> p a h c", h=2),
                                     BK[:, :, :, ds(c * C, C)].rearrange("p h a c -> p a h c"),
                                     ACT.Copy).then_inc(S["phi_in"], 1)
            chunks(act, step)

        @block.gpsimd
        def _(pool):
            nc.gpsimd.memset(sbd[:], 0.0).then_inc(S["zeroed"], 1)
            pool.wait_ge(S["zeroed"], 2)

            def step(c, b, first):
                if not (isinstance(c, int) and c == 0):
                    pool.wait_ge(S["state"], c)
                if not first:
                    pool.wait_ge(S["y"], c - 1)
                for h in range(2):
                    nc.gpsimd.tensor_copy(sbd[half(h), b, :, half(h)], at(c)[half(h)]).then_inc(S["placed"], 1)
            chunks(pool, step)

        @block.tensor
        def _(pe):
            pe.wait_ge(S["zeroed"], 2)

            def values(c, b, first):
                pe.wait_ge(S["placed"], c * 2 + 2)
                if not first:
                    pe.wait_ge(S["y_added"], c - 1)
                for p in range(NPAIR):
                    last = nc.tensor.matmul(py[b][:, p, 0:C], sbd[:, b, p, :], NR[:, p, 1, ds(c * C, C)],
                                            start=True, stop=True)
                last.then_inc(S["y"], 1)

            def step(c, b, first):
                pe.wait_ge(S["phi_in"], c + 1)
                if not (isinstance(c, int) and c == 0):
                    pe.wait_ge(S["state"], c)
                for p in range(NPAIR):
                    last = nc.tensor.matmul(ps[b][:, p, 0:C], phi[:, b, p, :], at(c)[:, p, :], start=True, stop=True)
                last.then_inc(S["next"], 1)
                values(c, b, first)
            chunks(pe, step)

        @block.vector
        def _(dve):
            nc.vector.memset(states[:, 0], 0.0).then_inc(S["zeroed"], 1)
            dve.wait_ge(S["zeroed"], 2)

            def step(c, b, first):
                dve.wait_ge(S["next"], c + 1)
                if not (isinstance(c, int) and c == 0):
                    dve.wait_ge(S["state"], c)
                nc.vector.tensor_tensor(tsum[:], ps[b][:, :, 0:C], NR[:, :, 0, ds(c * C, C)], ALU.add)\
                    .then_inc(S["summed"], 1)
                dve.wait_ge(S["summed"], c + 1)
                nc.vector.tensor_tensor(at(c + 1), tsum[:], ELC[:, :, ds(c, 1)].broadcast_to([P, NPAIR, C]),
                                        ALU.mult).then_inc(S["state"], 1)
                if not (isinstance(c, int) and c == 0):
                    add(c - 1, 1 - b)

            def add(c, b):
                dve.wait_ge(S["y"], c + 1)
                y = Y[:, :, ds(c * C, C)]
                nc.vector.tensor_tensor(y, py[b][:, :, 0:C], y, ALU.add).then_inc(S["y_added"], 1)
            chunks(dve, step)
            add(NCH - 1, 1)
            dve.wait_ge(S["y_added"], NCH)


def rwkv_samples(kit, a, o, ident, SD, Y):
    nc = kit.nc
    names = ("turned", "kept", "out_sd", "vec_in", "state_in", "halved", "mul", "stored", "y_out", "y_in",
             "y_turned", "y_kept")
    S = {n: kit.sem("rs_" + n) for n in names}
    NV = NB * 8
    with ExitStack() as ctx:
        sdt = kit.sb(ctx, "rs_sdt", [NS, 8, NSTEP, 64])
        vec = kit.sb(ctx, "rs_vec", [P, NT, NSTEP, 64])
        v2 = kit.sb(ctx, "rs_v2", [P, NT, 32])
        st = kit.sb(ctx, "rs_st", [P, 32, 64])
        tmp = kit.sb(ctx, "rs_tmp", [P, 32, 64])
        sav = kit.sb(ctx, "rs_sa", [P, 32])
        ys = kit.sb(ctx, "rs_y", [P, NT, 32])
        yt = kit.sb(ctx, "rs_yt", [NS, 512])
        pt = kit.ps(ctx, "rs_pt", [NS, NSTEP, 512])
        py = kit.ps(ctx, "rs_py", [P, 512])
        block = ctx.enter_context(nc.Block())
        sd, ysd = o["sd"], o["ysd"]

        @block.sync
        def _(sp):
            for h in range(2):
                sp.dma_start(st[h * 64:(h + 1) * 64], a["wkv"][:, h]).then_inc(S["state_in"], 16)
            sp.wait_ge(S["kept"], 1)
            sp.dma_start(sd, sdt[:]).then_inc(S["out_sd"], 16)
            sp.wait_ge(S["out_sd"], 16)
            for h in range(2):
                for n in range(NB):
                    at = h * 64 + n * 8
                    sp.dma_start(vec[at:at + 8], sd[n * NT:(n + 1) * NT].rearrange("t h q k -> h t (q k)"))\
                        .then_inc(S["vec_in"], 16)
            sp.wait_ge(S["stored"], NT)
            for h in range(2):
                sp.dma_start(o["wkv_sample"][:, h], st[h * 64:(h + 1) * 64]).then_inc(S["y_out"], 16)
                for n in range(NB):
                    at = h * 64 + n * 8
                    sp.dma_start(ysd[n * NT:(n + 1) * NT, :, h].rearrange("t h v -> h t v"), ys[at:at + 8])\
                        .then_inc(S["y_out"], 16)
            sp.wait_ge(S["y_out"], 16 * (2 + 2 * NB))
            sp.dma_start(yt[:], ysd.rearrange("t h a v -> t (h a v)")).then_inc(S["y_in"], 16)

        @block.tensor
        def _(pe):
            for q in range(NSTEP):
                for p in range(NPAIR):
                    last = nc.tensor.transpose(pt[:, q, p * P:(p + 1) * P], SD[:, p, q, :], ident)
            last.then_inc(S["turned"], 1)
            pe.wait_ge(S["y_in"], 16)
            for p in range(NPAIR):
                last = nc.tensor.transpose(py[:, p * NS:(p + 1) * NS], yt[:, p * P:(p + 1) * P], ident[0:NS, 0:NS])
            last.then_inc(S["y_turned"], 1)

        @block.vector
        def _(dve):
            dve.wait_ge(S["turned"], 1)
            nc.vector.tensor_copy(sdt[:].rearrange("t h q k -> t q h k"),
                                  pt[:].rearrange("t q (h k) -> t q h k", k=64)).then_inc(S["kept"], 1)
            dve.wait_ge(S["vec_in"], 16 * 2 * NB)
            dve.wait_ge(S["state_in"], 32)
            for h in range(2):
                rows = slice(h * 64, (h + 1) * 64)
                nc.vector.tensor_copy(v2[rows], vec[rows, :, 5, h * 32:(h + 1) * 32]).then_inc(S["halved"], 1)
            dve.wait_ge(S["halved"], 2)
            count = 0
            for t in range(NT):
                along_v = lambda q: vec[:, t, q, :].unsqueeze(1).broadcast_to([P, 32, 64])
                along_k = lambda z: z.unsqueeze(2).broadcast_to([P, 32, 64])
                steps = (
                    (tmp[:], st[:], along_v(1), ALU.mult), (sav[:], tmp[:], None, ALU.add),
                    (st[:], st[:], along_v(0), ALU.mult),
                    (tmp[:], along_k(sav[:]), along_v(2), ALU.mult), (st[:], st[:], tmp[:], ALU.subtract),
                    (tmp[:], along_k(v2[:, t, :]), along_v(3), ALU.mult), (st[:], st[:], tmp[:], ALU.add),
                    (tmp[:], st[:], along_v(4), ALU.mult), (ys[:, t, :], tmp[:], None, ALU.add))
                for n, (out, x, y, op) in enumerate(steps):
                    if y is None:
                        ins = nc.vector.tensor_reduce(out, x, AX, op)
                    else:
                        ins = nc.vector.tensor_tensor(out, x, y, op)
                    ins.then_inc(S["mul"], 1)
                    count += 1
                    dve.wait_ge(S["mul"], count)
                dve.sem_inc(S["stored"], 1)
            dve.wait_ge(S["y_turned"], 1)
            nc.vector.tensor_copy(Y[:, :, SEQ:T], py[:, 0:NPAIR * NS].rearrange("p (a t) -> p a t", t=NS))\
                .then_inc(S["y_kept"], 1)
            dve.wait_ge(S["y_kept"], 1)


def rwkv_finish(kit, blk64, epsg, param, Y, BON, G, mix_out):
    nc = kit.nc
    names = ("mean", "centred", "squared", "var", "rooted", "inverted", "normed", "affine", "bonused", "gated", "stored")
    S = {n: kit.sem("rf_" + n) for n in names}
    with ExitStack() as ctx:
        dev = kit.sb(ctx, "rf_dev", [P, 2, T])
        sq = kit.sb(ctx, "rf_sq", [P, 2, T])
        rs = kit.sb(ctx, "rf_rs", [P, 2, T])
        pm = kit.ps(ctx, "rf_pm", [P, 3, 512])
        pvv = kit.ps(ctx, "rf_pv", [P, 3, 512])
        block = ctx.enter_context(nc.Block())
        part = lambda z: z.rearrange("p (n t) -> p n t", t=T3)

        @block.tensor
        def _(pe):
            for p in range(NPAIR):
                if p:
                    pe.wait_ge(S["centred"], p)
                for n in range(3):
                    last = nc.tensor.matmul(pm[:, n, 0:T3], blk64, Y[:, p, n * T3:(n + 1) * T3], start=True, stop=True)
                last.then_inc(S["mean"], 1)
                pe.wait_ge(S["squared"], p + 1)
                if p:
                    pe.wait_ge(S["rooted"], p)
                for n in range(3):
                    last = nc.tensor.matmul(pvv[:, n, 0:T3], blk64, sq[:, p % 2, n * T3:(n + 1) * T3],
                                            start=True, stop=True)
                last.then_inc(S["var"], 1)

        @block.scalar
        def _(act):
            for p in range(NPAIR):
                act.wait_ge(S["centred"], p + 1)
                if p >= 2:
                    act.wait_ge(S["inverted"], p - 1)
                nc.scalar.activation(sq[:, p % 2], dev[:, p % 2], ACT.Square).then_inc(S["squared"], 1)
                act.wait_ge(S["var"], p + 1)
                if p >= 2:
                    act.wait_ge(S["normed"], p - 1)
                nc.scalar.activation(part(rs[:, p % 2]), pvv[:, :, 0:T3], ACT.Sqrt, bias=epsg).then_inc(S["rooted"], 1)

        @block.vector
        def _(dve):
            for p in range(NPAIR):
                b = p % 2
                dve.wait_ge(S["mean"], p + 1)
                if p >= 2:
                    dve.wait_ge(S["affine"], p - 1)
                nc.vector.tensor_tensor(part(dev[:, b]), part(Y[:, p]), pm[:, :, 0:T3], ALU.subtract)\
                    .then_inc(S["centred"], 1)
                dve.wait_ge(S["rooted"], p + 1)
                nc.vector.reciprocal(rs[:, b], rs[:, b]).then_inc(S["inverted"], 1)
                dve.wait_ge(S["inverted"], p + 1)
                nc.vector.tensor_tensor(dev[:, b], dev[:, b], rs[:, b], ALU.mult).then_inc(S["normed"], 1)
                dve.wait_ge(S["normed"], p + 1)
                nc.vector.tensor_scalar(Y[:, p], dev[:, b], param("ln_w", 4)[:, p:p + 1], param("ln_b", 4)[:, p:p + 1],
                                        ALU.mult, ALU.add).then_inc(S["affine"], 1)

        @block.gpsimd
        def _(pool):
            for p in range(NPAIR):
                pool.wait_ge(S["affine"], p + 1)
                nc.gpsimd.tensor_tensor(Y[:, p], Y[:, p], BON[:, p], ALU.add).then_inc(S["bonused"], 1)
                pool.wait_ge(S["bonused"], p + 1)
                nc.gpsimd.tensor_tensor(Y[:, p], Y[:, p], G[:, p], ALU.mult).then_inc(S["gated"], 1)

        @block.sync
        def _(sp):
            for p in range(NPAIR):
                sp.wait_ge(S["gated"], p + 1)
                sp.dma_start(mix_out[p], Y[:, p]).then_inc(S["stored"], 16)
            sp.wait_ge(S["stored"], 16 * NPAIR)


def build(nc, a, o):
    with ExitStack() as top:
        kit = Kit(nc, top)
        par = kit.sb(top, "par", [P, NPARAM])
        ones = kit.sb(top, "ones", [P, P])
        epsc = kit.sb(top, "epsc", [P, 2])
        param = lambda name, n: par[:, PCOL[name]:PCOL[name] + n]

        ident = kit.sb(top, "ident", [P, P])
        identb = kit.sb(top, "identb", [P, P], BF16)
        causal = kit.sb(top, "causal", [P, P], BF16)
        lam = kit.sb(top, "lam", [P, 8])
        oR = o["oR"].rearrange("(h p) t -> h p t", p=P)
        oT = o["oT"].rearrange("(h p) t -> h p t", p=P)

        gain = lambda name: lambda k: param(name, KD)[:, k:k + 1]

        load_phase(kit, "ld_c", [(ident[:], a["ident"]), (identb[:], a["identb"]), (causal[:], a["causal"]),
                                 (par[:], a["par"])])
        made, chain = kit.sem("made"), kit.sem("lam_chain")
        with ExitStack() as ctx:
            lq = kit.sb(ctx, "lq", [P, 4, DH])
            prod = kit.sb(ctx, "lprod", [P, 2, DH])
            comb1 = kit.sb(ctx, "lcomb", [P, 17])
            load_phase(kit, "ld_l", [(lq[:], a["lams"]), (comb1[:], a["comb"])])
            block = ctx.enter_context(nc.Block())

            @block.scalar
            def _(act):
                act.wait_ge(chain, 3)
                nc.scalar.activation(lam[:, 2:4], lam[:, 0:2], ACT.Exp).then_inc(chain, 1)

            @block.vector
            def _(dve):
                nc.vector.memset(ones[:], 1.0 / D).then_inc(made, 1)
                nc.vector.memset(epsc[:, 0:1], EPS).then_inc(made, 1)
                nc.vector.memset(epsc[:, 1:2], GN_EPS).then_inc(made, 1)
                nc.vector.tensor_tensor(prod[:], lq[:, 0:2], lq[:, 2:4], ALU.mult).then_inc(chain, 1)
                dve.wait_ge(chain, 1)
                nc.vector.tensor_reduce(lam[:, 0:2], prod[:], AX, ALU.add).then_inc(chain, 2)
                dve.wait_ge(chain, 4)
                nc.vector.tensor_tensor(lam[:, 4:5], lam[:, 3:4], lam[:, 2:3], ALU.subtract).then_inc(chain, 1)
                dve.wait_ge(chain, 5)
                nc.vector.tensor_scalar(lam[:, 4:5], lam[:, 4:5], -LAM_INIT, None, ALU.add).then_inc(chain, 1)
                dve.wait_ge(chain, 6)
                nc.vector.tensor_scalar(lam[:, 5:6], lam[:, 4:5], -1.0, comb1[:, 16:17], ALU.add,
                                        ALU.mult).then_inc(chain, 1)
                dve.wait_ge(chain, 7)
                nc.vector.tensor_scalar(lam[:, 5:6], lam[:, 5:6], 1.0, None, ALU.add).then_inc(chain, 1)
                dve.wait_ge(chain, 8)
                dve.wait_ge(made, 3)

        x_view = a["xT"].rearrange("(k p) t -> p k t", p=P)

        proj = o["projT"].rearrange("(m p) t -> m p t", p=P)

        with ExitStack() as ctx:
            Hh = kit.sb(ctx, "Hh", [P, KD, T], F32R)
            Hl = kit.sb(ctx, "Hl", [P, KD, T], F32R)
            with ExitStack() as inner:
                X = kit.sb(inner, "X", [P, KD, T])
                R = kit.sb(inner, "R", [P, T])
                load_phase(kit, "ld_x", [(X[:, k], x_view[:, k]) for k in range(KD)])
                rms_rows(kit, "rms_x", X, R[:], KD, T, ones[:], epsc[:, 0:1])
                scale_split(kit, "split_x", X, KD, T, Hh, Hl, gain("g_mix_pre"), lambda k: R[:])
            parts = [(n * T3, T3) for n in range(3)]
            project(kit, "in", MT_IN, KD, 1, a["w_in"], Hh, Hl, parts,
                    lambda c: ToDram(kit, c, "in", parts, lambda m: proj[m] if isinstance(m, int) else
                                     proj[ds(m, 1)].rearrange("a p t -> (a p) t")))

        attend_prompt(kit, proj, oT, ident[:], identb[:], causal[:], lam[:, 4:5])
        attend_sample(kit, a, proj, oT, ident[:], identb[:], lam[:, 5:6])

        kit.retire()

        with ExitStack() as ctx:
            V = kit.sb(ctx, "V", [P, NPAIR, T])
            NR = kit.sb(ctx, "NR", [P, NPAIR, 2, SEQ])
            BK = kit.sb(ctx, "BK", [P, 2, NPAIR, SEQ])
            spill = [o[n].rearrange("(a p) t -> p a t", p=P) for n in ("bonus", "gate")]
            ELC = kit.sb(ctx, "ELC", [P, NPAIR, NCH])
            SD = kit.sb(ctx, "SD", [P, NPAIR, NSTEP, NS])
            with ExitStack() as inner:
                BON = kit.sb(inner, "BON", [P, NPAIR, T])
                G = kit.sb(inner, "G", [P, NPAIR, T])
                Rm = kit.sb(inner, "Rm", [P, NPAIR, T])
                Km = kit.sb(inner, "Km", [P, NPAIR, T])
                X12 = kit.sb(inner, "X12", [P, T])
                XG = kit.sb(inner, "XG", [P, T])
                dsts = [z[:, p] for z in (Rm, Km, V) for p in range(NPAIR)] + [X12[:], XG[:]]
                rwkv_mix(kit, ctx, a, proj, param, dsts)
                rwkv_prepare(kit, ctx, a, param, Rm, Km, V, X12, XG[:], NR, BK[:, 0], BK[:, 1], BON, G, ELC, SD)
                load_phase(kit, "st_bg", [(spill[0], BON[:]), (spill[1], G[:])])
            with ExitStack() as inner:
                Y = kit.sb(inner, "Y", [P, NPAIR, T])
                kit.retire()
                rwkv_transitions(kit, a, NR, BK, V, Y)
                kit.retire()
                rwkv_scan(kit, NR, BK, ELC, Y, o["wkv_prompt"])
                rwkv_samples(kit, a, o, ident[:], SD, Y)
                blk64 = kit.sb(inner, "blk64", [P, P])
                BON = kit.sb(inner, "BON2", [P, NPAIR, T])
                G = kit.sb(inner, "G2", [P, NPAIR, T])
                load_phase(kit, "ld_b", [(blk64[:], a["blockmean"]), (BON[:], spill[0]), (G[:], spill[1])])
                rwkv_finish(kit, blk64[:], epsc[:, 1:2], param, Y, BON, G, oR)


        kit.retire()
        third = [(n * T3, T3) for n in range(3)]
        quarter = [(0, TH // 2), (TH // 2, TH // 2)]
        x1 = o["x1T"].rearrange("(k p) t -> p k t", p=P)
        h2 = o["h2T"].rearrange("(k p) t -> p k t", p=P)
        fT = o["fT"].rearrange("(k p) t -> p k t", p=P)

        with ExitStack() as ctx:
            Y = kit.sb(ctx, "mixed", [P, KD, T])
            with ExitStack() as inner:
                Hh = kit.sb(inner, "Mh", [P, KD, T], F32R)
                Hl = kit.sb(inner, "Ml", [P, KD, T], F32R)
                with ExitStack() as pre:
                    ones_head = kit.sb(pre, "ones_head", [P, P])
                    R4 = kit.sb(pre, "R4", [P, HEADS, T])
                    gs = kit.sb(pre, "gs", [P, 1])
                    load_phase(kit, "ld_m", [(ones_head[:], a["headmean"])]
                               + [(Y[:, h], oT[h]) for h in range(4)] + [(Y[:, 4 + h], oR[h]) for h in range(4)])
                    subln = kit.sem("subln")
                    with nc.Block() as block:
                        @block.vector
                        def _(dve):
                            nc.vector.tensor_scalar(gs[:], param("g_subln", 1), 1.0 - LAM_INIT, None,
                                                    ALU.mult).then_inc(subln, 1)
                            dve.wait_ge(subln, 1)
                    for n in range(2):
                        rms_rows(kit, f"rms_o{n}", Y[:, 2 * n:2 * n + 2, :].rearrange("p (o k) t -> p o (k t)", o=1),
                                 R4[:, 2 * n:2 * n + 2, :].rearrange("p k t -> p (k t)"), 1, 2 * T, ones_head[:],
                                 epsc[:, 0:1])
                    scale_split(kit, "split_o", Y, 4, T, Hh, Hl, lambda k: gs[:], lambda k: R4[:, k, :])
                    scale_split(kit, "split_r", Y[:, 4:8], 4, T, Hh[:, 4:8], Hl[:, 4:8])
                project(kit, "wo", KD, KD, 1, a["w_o"], Hh, Hl, third, lambda c: ToSbuf(kit, c, "wo", third, Y))
            X = kit.sb(ctx, "X1", [P, KD, T])
            R = kit.sb(ctx, "R1", [P, T])
            load_phase(kit, "ld_x1", [(X[:, k], x_view[:, k]) for k in range(KD)])
            rms_rows(kit, "rms_m", Y, R[:], KD, T, ones[:], epsc[:, 0:1])
            add_scaled(kit, "add_m", Y, param("g_mix_post", KD), R[:], X)
            rms_rows(kit, "rms_f", X, R[:], KD, T, ones[:], epsc[:, 0:1])
            scale_split(kit, "store_h2", X, KD, T, None, None, gain("g_ffn_pre"), lambda k: R[:], store=h2)
            load_phase(kit, "st_x1", [(x1[:, k], X[:, k]) for k in range(KD)])
        kit.retire()

        with ExitStack() as ctx:
            carry = kit.sb(ctx, "carry", [P, 2 * FT, 2])
            states = kit.sb(ctx, "states", [P, 2 * FT, 2 * NB])
            conv_out = kit.sb(ctx, "conv_out", [P, 2 * FT, 2 + 2 * NB])
            cleared = kit.sem("carry_cleared")
            load_phase(kit, "ld_st", [(states[:], a["convT"])])
            with nc.Block() as block:
                @block.vector
                def _(dve):
                    nc.vector.memset(carry[:], 0.0).then_inc(cleared, 1)
                    dve.wait_ge(cleared, 1)
            for half in range(2):
                with ExitStack() as inner:
                    Gh = kit.sb(inner, f"Gh{half}", [P, FT, TH], F32R)
                    Gl = kit.sb(inner, f"Gl{half}", [P, FT, TH], F32R)
                    with ExitStack() as up:
                        Hh = kit.sb(up, f"Uh{half}", [P, KD, TH], F32R)
                        Hl = kit.sb(up, f"Ul{half}", [P, KD, TH], F32R)
                        with ExitStack() as pre:
                            H = kit.sb(pre, f"H2{half}", [P, KD, TH])
                            load_phase(kit, f"ld_h{half}", [(H[:, k], h2[:, k, half * TH:(half + 1) * TH])
                                                            for k in range(KD)])
                            scale_split(kit, f"split_h{half}", H, KD, TH, Hh, Hl)
                        project(kit, f"up{half}", 2 * FT, KD, 1, a["w_up"], Hh, Hl, quarter,
                                lambda c: ConvGate(kit, c, f"cg{half}", quarter, par, carry, states, conv_out, Gh, Gl,
                                                   half == 1))
                    down = o["fT"].rearrange("(m p) t -> m p t", p=P)[:, :, half * TH:(half + 1) * TH]
                    project(kit, f"dn{half}", KD, FT // 2, 2, a["w_down"], Gh, Gl, quarter,
                            lambda c: ToDram(kit, c, f"dn{half}", quarter, lambda m: down[m] if isinstance(m, int) else
                                             down[ds(m, 1)].rearrange("a p t -> (a p) t")))
                kit.retire()
            load_phase(kit, "st_cv", [(o["conv_out"], conv_out[:])])

        with ExitStack() as ctx:
            X = kit.sb(ctx, "X2", [P, KD, T])
            R = kit.sb(ctx, "R2", [P, T])
            Y = kit.sb(ctx, "Y2", [P, KD, T])
            load_phase(kit, "ld_f", [(X[:, k], x1[:, k]) for k in range(KD)] + [(Y[:, k], fT[:, k]) for k in range(KD)])
            rms_rows(kit, "rms_d", Y, R[:], KD, T, ones[:], epsc[:, 0:1])
            add_scaled(kit, "add_d", Y, param("g_ffn_post", KD), R[:], X)
            with ExitStack() as inner:
                Eh = kit.sb(inner, "Eh", [P, PLE // P, T], F32R)
                El = kit.sb(inner, "El", [P, PLE // P, T], F32R)
                with ExitStack() as pre:
                    E = kit.sb(pre, "E", [P, PLE // P, T])
                    load_phase(kit, "ld_p", [(E[:], a["pT"].rearrange("(k p) t -> p k t", p=P))])
                    scale_split(kit, "split_p", E, PLE // P, T, Eh, El)
                project(kit, "ple", KD, PLE // P, 1, a["w_ple"], Eh, El, third,
                        lambda c: ToSbuf(kit, c, "ple", third, Y, 0.5))
            with ExitStack() as inner:
                Hh = kit.sb(inner, "X2h", [P, KD, T], F32R)
                Hl = kit.sb(inner, "X2l", [P, KD, T], F32R)
                scale_split(kit, "split_x2", X, KD, T, Hh, Hl)
                project(kit, "pg", KD, KD, 1, a["w_gate"], Hh, Hl, third, lambda c: Gate(kit, c, "pg", third, Y))
            rms_rows(kit, "rms_p", Y, R[:], KD, T, ones[:], epsc[:, 0:1])
            add_scaled(kit, "add_p", Y, param("g_ple", KD), R[:], X)
            load_phase(kit, "st_y", [(o["yT"].rearrange("(k p) t -> p k t", p=P)[:, k], X[:, k]) for k in range(KD)])

OUTS = {"yT": (D, T), "projT": (N_IN, T), "wkv_prompt": (P, NPAIR, C), "wkv_sample": (NB * 8, 2, 32, 64),
        "conv_out": (P, 2 * FT, 2 + 2 * NB)}
SCRATCH = {"oT": (512, T), "oR": (512, T), "x1T": (D, T), "h2T": (D, T), "fT": (D, T), "bonus": (512, T), "gate": (512, T),
           "sd": (NS, 8, NSTEP, 64), "ysd": (NS, 8, 2, 32)}


def kernel(**inputs):
    import numpy as np
    import concourse.bacc as bacc
    from concourse import mybir as mb
    from concourse.bass_utils import run_bass_kernel_spmd

    bf16 = mb.dt.np(mb.dt.bfloat16)
    v = {n: np.asarray(x) for n, x in inputs.items()}

    def cols(x, n):
        x = np.ascontiguousarray(x, dtype=x.dtype).reshape(-1)
        return np.pad(x, (0, n * P - x.size)).reshape(n, P).T

    def halves(x):
        g, u = cols(x[:FF], FT), cols(x[FF:], FT)
        return np.stack([g, u], axis=2).reshape(P, 2 * FT)

    def tiles(w, kt, units):
        k, m = units * kt * P, -(-w.shape[1] // P) * P
        w = np.pad(w, ((0, k - w.shape[0]), (0, m - w.shape[1])))
        w = w.reshape(units, kt, P, m // P, P).transpose(3, 0, 2, 1, 4)
        return np.ascontiguousarray(w).reshape(m // P * units, P, kt * P)

    def tokens(p, s):
        return np.ascontiguousarray(np.concatenate([p.reshape(SEQ, -1), s.reshape(NS, -1)]).T)

    par = np.ascontiguousarray(np.concatenate(
        [cols(v[n][0], 8) for n in ("g_mix_pre", "g_mix_post", "g_ffn_pre", "g_ffn_post", "g_ple")]
        + [cols(v["g_subln"][0], 1), cols(v["mu_shift"][0], 14)]
        + [cols(v[n][0], 4) for n in ("w0", "a0", "k_k", "k_a", "r_k", "ln_x_w", "ln_x_b")]
        + [halves(v["conv_w"][0, j]) for j in range(3)] + [halves(v["conv_b"][0])], axis=1))
    comb = np.zeros((P, 17), np.float32)
    new_mask = np.full((P, NB, NS), NEG, np.float32)
    for h in range(HEADS):
        for c in range(2):
            for t in range(NT):
                row = 32 * h + NT * c + t
                comb[row, NT * h + t] = 1.0
                comb[row, 16] = c
                for n in range(NB):
                    new_mask[row, n, NT * n:NT * n + t + 1] = 0.0
    j, h2 = np.arange(P) % C, np.arange(P) // C
    i = np.arange(C)
    same = h2[:, None] == np.arange(2)[None, :]

    def bd4(m):
        return np.tile((m[:, None, :] * same[:, :, None]).reshape(P, P), (1, NPAIR)).astype(np.float32)

    def st4(m):
        return np.tile(m, (1, NPAIR)).astype(np.float32)

    lev = [(j[:, None] == i[None, :]) | ((j[:, None] >> (n + 1) == i[None, :] >> (n + 1))
                                         & (j[:, None] >> n > i[None, :] >> n)) for n in range(NLEV)]
    new_mask = new_mask.reshape(P, NB * NS).astype(bf16)
    wu = v["w_up"][0]
    sc = v["state_conv"][0].reshape(NB * 2, 2 * FF)
    convT = np.ascontiguousarray(np.stack([halves(row) for row in sc], axis=2))
    gate, val = tiles(wu[:, :FF], KD, 1), tiles(wu[:, FF:], KD, 1)
    arrays = {
        "xT": tokens(v["x_prompt"], v["x_sample"]),
        "pT": tokens(v["p_prompt"], v["p_sample"]),
        "par": par,
        "w_in": tiles(v["w_in"][0], KD, 1),
        "w_o": tiles(v["w_o"][0], KD, 1),
        "w_up": np.ascontiguousarray(np.stack([gate, val], axis=1)).reshape(2 * FT, P, KD * P),
        "w_down": tiles(v["w_down"][0], FT // 2, 2),
        "w_ple": tiles(v["w_ple"][0], PLE // P, 1),
        "w_gate": tiles(v["w_ple_gate"][0], KD, 1),
        "headmean": np.full((P, P), 1 / P, np.float32),
        "convT": convT,
        "ident": np.eye(P, dtype=np.float32),
        "identb": np.eye(P, dtype=bf16),
        "causal": np.where(np.arange(P)[None, :] > np.arange(P)[:, None], NEG, 0.0).astype(bf16),
        "lams": np.tile(np.stack([v[n][0] for n in ("lam_q1", "lam_q2", "lam_k1", "lam_k2")])[None], (P, 1, 1)),
        "comb": comb,
        "w2": v["w2"][0], "a2": v["a2"][0], "g2": v["g2"][0],
        "blockones": np.kron(np.eye(2), np.ones((C, C))).astype(np.float32),
        "blockmean": np.kron(np.eye(2), np.full((C, C), 1 / C)).astype(np.float32),
        "reset": np.tile((np.arange(SEQ) % C != 0)[None], (P, 1)).astype(bf16),
        "strict": bd4(j[:, None] < i[None, :]), "incl": st4(j[:, None] <= i[None, :]),
        "levst": np.stack([st4(m) for m in lev], axis=1),
        "pairbd": bd4(np.ones((P, C))), "eyebd": bd4(j[:, None] == i[None, :]), "eyest": st4(j[:, None] == i[None, :]),
        "shiftT": np.ascontiguousarray(v["state_shift"][0].reshape(NB, 14, P).transpose(2, 1, 0)),
        "wkv": v["state_wkv"][0].reshape(NB * 8, 2, 32, 64),
        "new_mask": new_mask,
        "table": v["page_table"].reshape(1, -1),
        "k_pool": np.ascontiguousarray(v["cache_k"][0].transpose(0, 3, 2, 1)).reshape(POOL, P, HEADS * PAGE),
        "v_pool": v["cache_v"][0].reshape(POOL, PAGE, HEADS * P),
    }

    nc = bacc.Bacc("TRN2", target_bir_lowering=False, num_devices=1)
    a = {n: nc.dram_tensor("dram_" + n, x.shape, mb.dt.from_np(x.dtype), kind="ExternalInput").ap()
         for n, x in arrays.items()}
    o = {n: nc.dram_tensor("dram_" + n, s, mb.dt.float32, kind="ExternalOutput").ap() for n, s in OUTS.items()}
    o.update({n: nc.dram_tensor("dram_" + n, s, mb.dt.float32).ap() for n, s in SCRATCH.items()})
    build(nc, a, o)
    r = run_bass_kernel_spmd(nc, [{"dram_" + n: x for n, x in arrays.items()}], core_ids=[0]).results[0]
    y, proj, wp, ws, cv = (r["dram_" + n] for n in OUTS)
    kT, vT, sh = proj[512:1024], proj[1024:1536], proj[1536:]
    last = [SEQ + n * NT + NT - 1 for n in range(NB)]

    def split(z, shape):
        z = np.ascontiguousarray(z.T)
        return z[:SEQ].reshape(1, 1, SEQ, *shape), z[SEQ:].reshape(1, NB, NT, *shape)

    y_prompt, y_sample = (z[0] for z in split(y, (D,)))
    (kp, ks), (vp, vs) = split(kT, (HEADS, P)), split(vT, (HEADS, P))
    wp = wp.reshape(2, C, NPAIR, C).transpose(2, 0, 3, 1).reshape(1, 1, 8, C, C)
    cv = cv.reshape(P, FT, 2, 18).transpose(3, 2, 1, 0).reshape(18, 2, FT * P)[:, :, :FF].reshape(18, 2 * FF)
    return (y_prompt, y_sample, kp, vp, ks, vs, sh[:, SEQ - 1].reshape(1, 1, -1), np.ascontiguousarray(wp),
            cv[0:2].reshape(1, 1, 2, -1), np.ascontiguousarray(sh[:, last].T)[None], ws.reshape(1, NB, 8, C, C),
            cv[2:].reshape(1, NB, 2, -1))
```

```python
import math
from contextlib import ExitStack

import concourse.bass as bass
from concourse import mybir

F32 = mybir.dt.float32
F32R = mybir.dt.float32r
BF16 = mybir.dt.bfloat16
I32 = mybir.dt.int32
ALU = mybir.AluOpType
ACT = mybir.ActivationFunctionType
AX = mybir.AxisListType.X
ds = bass.ds

P = 128
D = 1024
KD = D // P
SEQ = 1024
NB, NT = 8, 4
NS = NB * NT
T = SEQ + NS
T3 = T // 3
HEADS, DH = 4, 64
PAGES, PAGE = 8, 128
POOL = 80
N_IN = 3328
MT_IN = N_IN // P
FF = 2752
FT = (FF + P - 1) // P
TH = T // 2
PLE = 256
EPS = 1e-6
GN_EPS = 64e-5
LAM_INIT = 0.8 - 0.6 * math.exp(0.0)
C = 64
NCH = SEQ // C
NEG = -1e30
E05 = math.exp(-0.5)

PCOL = {}
_n = 0
for _name, _w in (("g_mix_pre", 8), ("g_mix_post", 8), ("g_ffn_pre", 8), ("g_ffn_post", 8), ("g_ple", 8),
                  ("g_subln", 1), ("mu", 14), ("w0", 4), ("a0", 4), ("k_k", 4), ("k_a", 4), ("r_k", 4),
                  ("ln_w", 4), ("ln_b", 4), ("cw0", 2 * FT), ("cw1", 2 * FT), ("cw2", 2 * FT), ("cb", 2 * FT)):
    PCOL[_name] = _n
    _n += _w
NPARAM = _n


class Kit:

    def __init__(self, nc):
        self.nc, self.live = nc, []

    def sb(self, ctx, name, shape, dt=F32):
        return ctx.enter_context(self.nc.sbuf_tensor(name, shape, dt))

    def ps(self, ctx, name, shape, dt=F32):
        return ctx.enter_context(self.nc.psum_tensor(name, shape, dt))

    def sem(self, name):
        self.live.append(self.nc.alloc_semaphore(name=name))
        return self.live[-1]

    def retire(self):
        self.nc.clear_and_free_semaphores(self.live)
        self.nc.all_engine_barrier()
        self.live = []


def load_phase(kit, name, pairs):
    nc = kit.nc
    loaded_sp, loaded_act = kit.sem(name + "_loaded_sp"), kit.sem(name + "_loaded_act")
    with nc.Block() as block:
        @block.sync
        def _(sp):
            for dst, src in pairs[0::2]:
                sp.dma_start(dst, src).then_inc(loaded_sp, 16)
            sp.wait_ge(loaded_sp, 16 * len(pairs[0::2]))

        @block.scalar
        def _(act):
            for dst, src in pairs[1::2]:
                act.dma_start(dst, src).then_inc(loaded_act, 16)
            if len(pairs) > 1:
                act.wait_ge(loaded_act, 16 * len(pairs[1::2]))


def rms_rows(kit, name, X, R, tiles, ones, eps, ident, per_tile=False, loads=(), also=(), sums=None):
    nc = kit.nc
    S = {n: kit.sem(f"{name}_{n}") for n in ("squared", "summed", "totals", "rooted", "inverted", "spread", "kept")}
    loaded = [kit.sem(f"{name}_loaded{k}") for k in range(len(loads))]
    also_loaded = kit.sem(name + "_also_loaded")
    groups = tiles if per_tile else 1
    nblk = -(-T // P)
    with ExitStack() as ctx:
        if sums is None:
            sq = kit.sb(ctx, name + "_sq", [P, tiles if per_tile else 2, T])
            acc = sq if per_tile else kit.sb(ctx, name + "_acc", [P, 1, T])
        else:
            acc, tiles = sums.unsqueeze(1), 0
        col = kit.sb(ctx, name + "_col", [P, groups, nblk])
        tot = kit.ps(ctx, name + "_tot", [P, groups, nblk])
        wide = kit.ps(ctx, name + "_wide", [P, 2, 3 * 512])
        block = ctx.enter_context(nc.Block())
        last = T - (nblk - 1) * P
        parts = ((slice(0, P), slice(0, nblk - 1)), (slice(0, last), slice(nblk - 1, nblk)))

        @block.sync
        def _(sp):
            for k in range(0, len(loads), 2):
                sp.dma_start(X[:, k, :], loads[k]).then_inc(loaded[k], 16)
            for dst, src in also:
                sp.dma_start(dst, src).then_inc(also_loaded, 16)
            if also:
                sp.wait_ge(also_loaded, 16 * len(also))

        @block.scalar
        def _(act):
            for k in range(1, len(loads), 2):
                act.dma_start(X[:, k, :], loads[k]).then_inc(loaded[k], 16)
            for k in range(tiles):
                if loads:
                    act.wait_ge(loaded[k], 16)
                if not per_tile and k >= 2:
                    act.wait_ge(S["summed"], k - 1)
                nc.scalar.activation(sq[:, k if per_tile else k % 2, :], X[:, k, :], ACT.Square)\
                    .then_inc(S["squared"], 1)
            act.wait_ge(S["totals"], 1)
            for rows, cols in parts:
                nc.scalar.activation(col[rows, :, cols], tot[rows, :, cols], ACT.Sqrt, bias=eps[rows])\
                    .then_inc(S["rooted"], 1)
            for g in range(groups):
                act.wait_ge(S["spread"], g + 1)
                nc.scalar.activation(R[:, g] if per_tile else R, wide[:, g % 2, 0:T], ACT.Copy).then_inc(S["kept"], 1)
            act.wait_ge(S["kept"], groups)

        @block.vector
        def _(dve):
            for k in range(0 if per_tile else tiles):
                dve.wait_ge(S["squared"], k + 1)
                if k == 0:
                    nc.vector.tensor_copy(acc[:, 0], sq[:, 0, :]).then_inc(S["summed"], 1)
                else:
                    dve.wait_ge(S["summed"], k)
                    nc.vector.tensor_tensor(acc[:, 0], acc[:, 0], sq[:, k % 2, :], ALU.add).then_inc(S["summed"], 1)
            dve.wait_ge(S["rooted"], 2)
            for rows, cols in parts:
                nc.vector.reciprocal(col[rows, :, cols], col[rows, :, cols]).then_inc(S["inverted"], 1)
            dve.wait_ge(S["inverted"], 2)

        @block.tensor
        def _(pe):
            for g in range(groups):
                if tiles:
                    pe.wait_ge(S["squared" if per_tile else "summed"], g + 1 if per_tile else tiles)
                for n in range(nblk):
                    w = min(P, T - n * P)
                    ins = nc.tensor.matmul(tot[0:w, g, n:n + 1], acc[:, g, n * P:n * P + w], ones,
                                           start=True, stop=True)
            ins.then_inc(S["totals"], 1)
            pe.wait_ge(S["inverted"], 2)
            for g in range(groups):
                if g >= 2:
                    pe.wait_ge(S["kept"], g - 1)
                for n in range(nblk):
                    w = min(P, T - n * P)
                    ins = nc.tensor.matmul(wide[:, g % 2, n * P:n * P + w],
                                           col[0:w, g, n:n + 1].broadcast_to([w, P]), ident[0:w, 0:w],
                                           start=True, stop=True)
                ins.then_inc(S["spread"], 1)


NBLK = -(-T // P)
TOKEN_PARTS = ((slice(0, P), slice(0, NBLK - 1)), (slice(0, T - (NBLK - 1) * P), slice(NBLK - 1, NBLK)))


def sum_heads(nc, out, x, blockcol):
    for n in range(NBLK):
        w = min(P, T - n * P)
        last = nc.tensor.matmul(out[0:w, n, :], x[:, n * P:n * P + w], blockcol, start=True, stop=True)
    return last


def spread_heads(nc, out, col, ident):
    for n in range(NBLK):
        w = min(P, T - n * P)
        for h in range(2):
            last = nc.tensor.matmul(out[h * C:(h + 1) * C, n * P:n * P + w], col[0:w, n, h:h + 1].broadcast_to([w, C]),
                                    ident[0:w, 0:w], start=True, stop=True)
    return last


def scale_split(kit, name, X, tiles, width, Hh, Hl, gain=None, R=None, store=None,
                loads=(), ahead=()):
    nc = kit.nc
    scaled, high, low = (kit.sem(f"{name}_{s}") for s in ("scaled", "high", "low"))
    stored = [kit.sem(f"{name}_stored{b}") for b in range(2)] if store is not None else None
    with ExitStack() as ctx:
        tmp = kit.sb(ctx, name + "_tmp", [P, 2, width]) if gain is not None else None
        block = ctx.enter_context(nc.Block())

        @block.vector
        def _(dve):
            def scale(k):
                if k >= 2 and store is not None:
                    dve.wait_ge(stored[k % 2], 16 * (k // 2))
                elif k >= 2:
                    dve.wait_ge(low, k - 1)
                nc.vector.scalar_tensor_tensor(tmp[:, k % 2, :], X[:, k, :], gain(k), R(k),
                                               ALU.mult, ALU.mult).then_inc(scaled, 1)

            if gain is not None:
                scale(0)
            for k in range(tiles):
                if gain is not None and k + 1 < tiles:
                    scale(k + 1)
                if store is None:
                    src = tmp[:, k % 2, :] if gain is not None else X[:, k, :]
                    dve.wait_ge(high, k + 1)
                    nc.vector.tensor_tensor(Hl[:, k, :], src, Hh[:, k, :].bitcast(F32),
                                            ALU.subtract).then_inc(low, 1)
            if store is None:
                dve.wait_ge(low, tiles)

        if store is None:
            loaded = [kit.sem(f"{name}_loaded{k}") for k in range(len(loads))]
            loaded_ahead = kit.sem(name + "_loaded_ahead")

            @block.sync
            def _(sp):
                for k, src in enumerate(loads):
                    sp.dma_start(X[:, k, :], src).then_inc(loaded[k], 16)
                for dst, src in ahead:
                    sp.dma_start(dst, src).then_inc(loaded_ahead, 16)
                if ahead:
                    sp.wait_ge(loaded_ahead, 16 * len(ahead))

            @block.scalar
            def _(act):
                for k in range(tiles):
                    if loads:
                        act.wait_ge(loaded[k], 16)
                    if gain is not None:
                        act.wait_ge(scaled, k + 1)
                    src = tmp[:, k % 2, :] if gain is not None else X[:, k, :]
                    nc.scalar.activation(Hh[:, k, :], src, ACT.Copy).then_inc(high, 1)
        else:
            @block.sync
            def _(sp):
                for k in range(tiles):
                    sp.wait_ge(scaled, k + 1)
                    sp.dma_start(store[:, k, :], tmp[:, k % 2, :]).then_inc(stored[k % 2], 16)
                for b in range(2):
                    sp.wait_ge(stored[b], 16 * (tiles // 2))


def add_scaled(kit, name, Y, gain, R, X, store=None, sums=None):
    nc = kit.nc
    scaled, added, added_dve = (kit.sem(f"{name}_{n}") for n in ("scaled", "added", "added_dve"))
    stored = kit.sem(name + "_stored")
    mine = [k for k in range(KD) if k % 3 == 2 or k == KD - 1]
    others = [k for k in range(KD) if k not in mine]
    squared, summed = kit.sem(name + "_squared"), kit.sem(name + "_summed")

    def wait_added(eng, k):
        if k in mine:
            eng.wait_ge(added_dve, mine.index(k) + 1)
        else:
            eng.wait_ge(added, others.index(k) + 1)

    with ExitStack() as ctx:
        if sums is not None:
            sq = kit.sb(ctx, name + "_sq", [P, 3, T])
        block = ctx.enter_context(nc.Block())

        @block.vector
        def _(dve):
            def add_square(k):
                dve.wait_ge(squared, k + 1)
                if k == 0:
                    nc.vector.tensor_copy(sums, sq[:, 0]).then_inc(summed, 1)
                else:
                    dve.wait_ge(summed, k)
                    nc.vector.tensor_tensor(sums, sums, sq[:, k % 3], ALU.add).then_inc(summed, 1)

            for k in range(KD):
                nc.vector.scalar_tensor_tensor(Y[:, k, :], Y[:, k, :], gain[:, k:k + 1], R,
                                               ALU.mult, ALU.mult).then_inc(scaled, 1)
                if k in mine:
                    dve.wait_ge(scaled, k + 1)
                    nc.vector.tensor_tensor(X[:, k, :], X[:, k, :], Y[:, k, :], ALU.add).then_inc(added_dve, 1)
                if sums is not None and k >= 3:
                    add_square(k - 3)
            dve.wait_ge(added_dve, len(mine))
            if sums is not None:
                for k in range(KD - 3, KD):
                    add_square(k)
                dve.wait_ge(summed, KD)

        if sums is not None:
            @block.scalar
            def _(act):
                for k in range(KD):
                    wait_added(act, k)
                    if k >= 3:
                        act.wait_ge(summed, k - 2)
                    nc.scalar.activation(sq[:, k % 3], X[:, k, :], ACT.Square).then_inc(squared, 1)

        @block.gpsimd
        def _(pool):
            for k in others:
                pool.wait_ge(scaled, k + 1)
                nc.gpsimd.tensor_tensor(X[:, k, :], X[:, k, :], Y[:, k, :], ALU.add).then_inc(added, 1)
            pool.wait_ge(added, len(others))

        if store is not None:
            @block.sync
            def _(sp):
                for k in range(KD):
                    wait_added(sp, k)
                    sp.dma_start(store[:, k], X[:, k]).then_inc(stored, 16)
                sp.wait_ge(stored, 16 * KD)


class ToDram:

    def __init__(self, kit, ctx, name, parts, dst):
        self.nc, self.parts, self.dst = kit.nc, parts, dst
        self.out = kit.sb(ctx, name + "_out", [P, 2, len(parts), parts[0][1]])
        self.stored = [kit.sem(f"{name}_stored{b}") for b in range(2)]

    def act(self, act, m, b, turn, first):
        act.wait_ge(self.multiplied, (m + 1) * self.units)
        if not first:
            act.wait_ge(self.stored[b], turn * 16)
        self.nc.scalar.activation(self.out[:, b], self.acc[:, b, :, 0:self.parts[0][1]],
                                  ACT.Copy).then_inc(self.drained, 1)

    def pool(self, pool, m, b, turn, first):
        pool.wait_ge(self.drained, m + 1)
        pool.dma_start(self.dst(m), self.out[:, b].rearrange("p n t -> p (n t)")).then_inc(self.stored[b], 16)

    def pool_end(self, pool, ntiles):
        for b in range(2):
            pool.wait_ge(self.stored[b], 16 * (ntiles // 2))


class SquareSum:

    def __init__(self, kit, ctx, name, acc):
        self.nc, self.acc = kit.nc, acc
        self.sq = kit.sb(ctx, name + "_sq", [P, T])
        self.step = kit.sem(name + "_step")

    def add(self, dve, m, y):
        if isinstance(m, int) and m == 0:
            self.nc.vector.tensor_tensor(self.acc, y, y, ALU.mult).then_inc(self.step, 1)
            return
        dve.wait_ge(self.step, m * 2 - 1)
        self.nc.vector.tensor_tensor(self.sq[:], y, y, ALU.mult).then_inc(self.step, 1)
        dve.wait_ge(self.step, m * 2)
        self.nc.vector.tensor_tensor(self.acc, self.acc, self.sq[:], ALU.add).then_inc(self.step, 1)

    def end(self, dve, ntiles):
        dve.wait_ge(self.step, ntiles * 2 - 1)


class ToSbuf:

    def __init__(self, kit, ctx, name, parts, Y, scale=1.0):
        self.nc, self.parts, self.Y, self.scale = kit.nc, parts, Y, scale

    def act(self, act, m, b, turn, first):
        act.wait_ge(self.multiplied, (m + 1) * self.units)
        w = self.parts[0][1]
        out = self.Y[:, ds(m, 1), :].rearrange("p a (n t) -> p (a n) t", t=w)
        self.nc.scalar.activation(out, self.acc[:, b, :, 0:w], ACT.Copy,
                                  scale=self.scale).then_inc(self.drained, 1)


class ToSbufSquared(ToSbuf):

    def __init__(self, kit, ctx, name, parts, Y, acc):
        super().__init__(kit, ctx, name, parts, Y)
        self.squares = SquareSum(kit, ctx, name, acc)

    def dve(self, dve, m, b, turn, first):
        dve.wait_ge(self.drained, m + 1)
        self.squares.add(dve, m, self.Y[:, ds(m, 1), :].rearrange("p a t -> p (a t)"))

    def dve_end(self, dve, ntiles):
        self.squares.end(dve, ntiles)


class Gate:

    def __init__(self, kit, ctx, name, parts, Y, acc):
        self.nc, self.parts, self.Y = kit.nc, parts, Y
        self.squares = SquareSum(kit, ctx, name, acc)
        self.th = kit.sb(ctx, name + "_th", [P, 2, T])
        self.gated = kit.sem(name + "_gated")

    def act(self, act, m, b, turn, first):
        act.wait_ge(self.multiplied, (m + 1) * self.units)
        if not first:
            act.wait_ge(self.gated, m - 1)
        w = self.parts[0][1]
        self.nc.scalar.activation(self.th[:, b].rearrange("p (n t) -> p n t", t=w), self.acc[:, b, :, 0:w],
                                  ACT.Tanh, scale=0.5).then_inc(self.drained, 1)

    def dve(self, dve, m, b, turn, first):
        dve.wait_ge(self.drained, m + 1)
        y = self.Y[:, ds(m, 1), :].rearrange("p a t -> p (a t)")
        self.nc.vector.scalar_tensor_tensor(y, self.th[:, b], 1.0, y, ALU.add, ALU.mult).then_inc(self.gated, 1)
        dve.wait_ge(self.gated, m + 1)
        self.squares.add(dve, m, y)

    def dve_end(self, dve, ntiles):
        self.squares.end(dve, ntiles)


class ConvGate:

    def __init__(self, kit, ctx, name, parts, par, carry, states, conv_out, Gh, Gl, last):
        self.nc, self.parts, self.par, self.last = kit.nc, parts, par, last
        self.carry, self.states, self.conv_out, self.Gh, self.Gl = carry, states, conv_out, Gh, Gl
        self.prompt = TH - NS if last else TH
        self.wide = 2 + self.prompt + (NB * (2 + NT) if last else 0)
        self.u = kit.sb(ctx, name + "_u", [P, 2, self.wide])
        self.c = kit.sb(ctx, name + "_c", [P, 2, self.wide - 2])
        self.ge = kit.sb(ctx, name + "_ge", [P, self.wide - 2])
        self.g = kit.sb(ctx, name + "_g", [P, TH])
        self.S = {n: kit.sem(f"{name}_{n}") for n in ("led", "tap0", "tap1", "tap2", "saved", "gelued", "gated",
                                                      "g_high", "g_low")}

    def samples(self, z):
        return z[:, 2 + self.prompt:].rearrange("p (n t) -> p n t", t=2 + NT)

    def tap(self, name, m):
        return self.par[:, ds(m + PCOL[name], 1)]

    def act(self, act, m, b, turn, first):
        S, nc = self.S, self.nc
        w = self.parts[0][1]
        act.wait_ge(self.multiplied, m + 1)
        if not first:
            act.wait_ge(S["tap2"], m - 1)
            act.wait_ge(S["saved"], m - 1)
        u, acc = self.u[:, b], self.acc[:, b]
        if self.last:
            nc.scalar.activation(u[:, 2:2 + w], acc[:, 0, 0:w], ACT.Copy)
            nc.scalar.activation(u[:, 2 + w:2 + self.prompt], acc[:, 1, 0:self.prompt - w], ACT.Copy)
            ins = nc.scalar.activation(self.samples(u)[:, :, 2:],
                                       acc[:, 1, self.prompt - w:w].rearrange("p (n t) -> p n t", t=NT), ACT.Copy)
        else:
            ins = nc.scalar.activation(u[:, 2:].rearrange("p (n t) -> p n t", t=w), acc[:, :, 0:w], ACT.Copy)
        ins.then_inc(self.drained, 1)
        if b == 0 and not first:
            self.high(act, turn - 1)
        act.wait_ge(self.drained, m + 1)
        act.wait_ge(S["led"], m + 1)
        if not first:
            act.wait_ge(S["gated"], turn)
        n = self.wide - 2
        nc.scalar.activation(self.c[:, b], u[:, 0:n], ACT.Identity, bias=self.tap("cb", m),
                             scale=self.tap("cw0", m)).then_inc(S["tap0"], 1)
        if b == 1:
            act.wait_ge(S["tap2"], m)
            nc.scalar.activation(self.ge[:], self.c[:, 0], ACT.Gelu_apprx_tanh).then_inc(S["gelued"], 1)

    def high(self, act, turn):
        act.wait_ge(self.S["gated"], turn + 1)
        if not isinstance(turn, int) or turn > 0:
            act.wait_ge(self.S["g_low"], turn)
        self.nc.scalar.activation(self.Gh[:, ds(turn, 1), :].rearrange("p a t -> p (a t)"), self.g[:],
                                  ACT.Copy).then_inc(self.S["g_high"], 1)

    def act_end(self, act, ntiles):
        self.high(act, ntiles // 2 - 1)

    def low(self, dve, turn):
        dve.wait_ge(self.S["g_high"], turn + 1)
        gh, gl = (z[:, ds(turn, 1), :].rearrange("p a t -> p (a t)") for z in (self.Gh, self.Gl))
        self.nc.vector.tensor_tensor(gl, self.g[:], gh.bitcast(F32), ALU.subtract).then_inc(self.S["g_low"], 1)

    def dve(self, dve, m, b, turn, first):
        S, nc, n = self.S, self.nc, self.wide - 2
        if b == 0 and not first:
            self.low(dve, turn - 1)
        c, u = self.c[:, b], self.u[:, b]
        for k in (1, 2):
            dve.wait_ge(S[f"tap{k - 1}"], m + 1)
            nc.vector.scalar_tensor_tensor(c, u[:, k:k + n], self.tap(f"cw{k}", m), c, ALU.mult,
                                           ALU.add).then_inc(S[f"tap{k}"], 1)
        one = lambda z: z[:, ds(m, 1)].rearrange("p a t -> p (a t)")
        end = u[:, self.prompt:self.prompt + 2]
        if self.last:
            nc.vector.tensor_scalar(one(self.conv_out)[:, 0:2], end, 1.0, None, ALU.mult)
            nc.vector.tensor_scalar(one(self.conv_out)[:, 2:].rearrange("p (n t) -> p n t", t=2),
                                    self.samples(u)[:, :, NT:NT + 2], 1.0, None, ALU.mult).then_inc(S["saved"], 1)
        else:
            nc.vector.tensor_scalar(one(self.carry), end, 1.0, None, ALU.mult).then_inc(S["saved"], 1)
        if b == 1:
            dve.wait_ge(S["gelued"], turn + 1)
            dve.wait_ge(S["tap2"], m + 1)
            if not first:
                dve.wait_ge(S["g_low"], turn)
            g, ge, v = self.g, self.ge, self.c[:, 1]
            q = self.prompt
            if self.last:
                nc.vector.tensor_tensor(g[:, 0:q], ge[:, 0:q], v[:, 0:q], ALU.mult)
                at = lambda z: z[:, 2 + q:2 + q + (NB - 1) * (2 + NT)].rearrange("p (n t) -> p n t", t=2 + NT)
                nc.vector.tensor_tensor(g[:, q:TH - NT].rearrange("p (n t) -> p n t", t=NT), at(ge)[:, :, 0:NT],
                                        at(v)[:, :, 0:NT], ALU.mult)
                end = 2 + q + (NB - 1) * (2 + NT)
                ins = nc.vector.tensor_tensor(g[:, TH - NT:TH], ge[:, end:end + NT], v[:, end:end + NT], ALU.mult)
            else:
                ins = nc.vector.tensor_tensor(g[:], ge[:], v, ALU.mult)
            ins.then_inc(S["gated"], 1)

    def dve_end(self, dve, ntiles):
        self.low(dve, ntiles // 2 - 1)
        dve.wait_ge(self.S["g_low"], ntiles // 2)
        dve.wait_ge(self.S["saved"], ntiles)

    def pool(self, pool, m, b, turn, first):
        S, nc = self.S, self.nc
        if not first:
            pool.wait_ge(S["tap2"], m - 1)
            pool.wait_ge(S["saved"], m - 1)
        u = self.u[:, b]
        one = lambda z: z[:, ds(m, 1)]
        ins = nc.gpsimd.tensor_copy(u[:, 0:2], one(self.carry).rearrange("p a t -> p (a t)"))
        if self.last:
            ins = nc.gpsimd.tensor_copy(self.samples(u)[:, :, 0:2],
                                        one(self.states).rearrange("p a (n t) -> p (a n) t", t=2))
        ins.then_inc(S["led"], 1)


def run_tiles(eng, ntiles, step, trail=None):
    peeled = min(2 if trail else 1, ntiles // 2)
    for m in range(2 * peeled):
        step(m, m % 2, m // 2, m < 2)
        if trail and m >= 1:
            trail(m - 1, (m - 1) % 2, (m - 1) // 2, m - 1 < 2)
    if ntiles > 2 * peeled:
        with eng.Fori(peeled, ntiles // 2) as i:
            step(i * 2, 0, i, False)
            if trail:
                trail(i * 2 - 1, 1, i - 1, False)
            step(i * 2 + 1, 1, i, False)
            if trail:
                trail(i * 2, 0, i, False)
    if trail:
        trail(ntiles - 1, 1, ntiles // 2 - 1, ntiles == 2)


def weight_buffer(kit, ctx, name, kt):
    return kit.sb(ctx, name + "_raw", [P, 2, kt, P])


def first_units(raw, w_dram):
    return [(raw[:, j].rearrange("p k m -> p (k m)"), w_dram[j]) for j in range(2)]


def project(kit, name, ntiles, kt, units, w_dram, Xh, Xl, parts, make_evac, raw, prefetch=()):
    nc = kit.nc
    rounded, residued, multiplied, drained = (kit.sem(f"{name}_{s}") for s in
                                              ("rounded", "residued", "multiplied", "drained"))
    fetched = [kit.sem(f"{name}_fetched{b}") for b in range(2)]
    passes = 3
    with ExitStack() as ctx:
        wh = kit.sb(ctx, name + "_wh", [P, 2, kt, P], F32R)
        wl = kit.sb(ctx, name + "_wl", [P, 2, kt, P], F32R)
        acc = kit.ps(ctx, name + "_acc", [P, 2, len(parts), 512])
        ev = make_evac(ctx)
        ev.multiplied, ev.drained, ev.acc, ev.units = multiplied, drained, acc, units
        ev.name = name
        block = ctx.enter_context(nc.Block())

        def each_unit(m, b, turn):
            for u in range(units):
                local = b * units + u
                yield m * units + u, local % 2, turn * units + local // 2, u

        @block.sync
        def _(sp):
            def fetch(m, b, turn, first):
                for j, buf, use, u in each_unit(m, b, turn):
                    if isinstance(j, int) and j < 2:
                        continue
                    sp.wait_ge(residued, j - 1)
                    src = w_dram[j] if isinstance(j, int) else w_dram[ds(j, 1)].rearrange("a p n -> (a p) n")
                    sp.dma_start(raw[:, buf].rearrange("p k m -> p (k m)"), src).then_inc(fetched[buf], 16)
            run_tiles(sp, ntiles, fetch)

        @block.scalar
        def _(act):
            def round_up(m, b, turn, first):
                for j, buf, use, u in each_unit(m, b, turn):
                    if not (isinstance(j, int) and j < 2):
                        act.wait_ge(fetched[buf], use * 16)
                        act.wait_ge(multiplied, j - 1)
                    nc.scalar.activation(wh[:, buf], raw[:, buf], ACT.Copy).then_inc(rounded, 1)

            run_tiles(act, ntiles, round_up,
                      lambda m, b, turn, first: ev.act(act, m, b, turn, first))
            if hasattr(ev, "act_end"):
                ev.act_end(act, ntiles)

        @block.vector
        def _(dve):
            def residue(m, b, turn, first):
                for j, buf, use, u in each_unit(m, b, turn):
                    dve.wait_ge(rounded, j + 1)
                    nc.vector.tensor_tensor(wl[:, buf], raw[:, buf], wh[:, buf].bitcast(F32),
                                            ALU.subtract).then_inc(residued, 1)
            trail = (lambda m, b, turn, first: ev.dve(dve, m, b, turn, first)) if hasattr(ev, "dve") else None
            run_tiles(dve, ntiles, residue, trail)
            if hasattr(ev, "dve_end"):
                ev.dve_end(dve, ntiles)

        @block.tensor
        def _(pe):
            def multiply(m, b, turn, first):
                for j, buf, use, u in each_unit(m, b, turn):
                    pe.wait_ge(residued, j + 1)
                    if u == 0 and not first:
                        pe.wait_ge(drained, m - 1)
                    for n, (at, size) in enumerate(parts):
                        for k in range(kt):
                            for q, (w, x) in enumerate(((wh, Xh), (wh, Xl), (wl, Xh))):
                                last = nc.tensor.matmul(acc[:, b, n, 0:size], w[:, buf, k, :],
                                                        x[:, u * kt + k, at:at + size],
                                                        start=(u == 0 and k == 0 and q == 0),
                                                        stop=(u == units - 1 and k == kt - 1 and q == passes - 1))
                    last.then_inc(multiplied, 1)
            run_tiles(pe, ntiles, multiply)

        prefetched = kit.sem(name + "_prefetched")

        @block.gpsimd
        def _(pool):
            for dst, src in prefetch:
                pool.dma_start(dst, src).then_inc(prefetched, 16)
            if hasattr(ev, "pool"):
                run_tiles(pool, ntiles, lambda m, b, turn, first: ev.pool(pool, m, b, turn, first))
            if hasattr(ev, "pool_end"):
                ev.pool_end(pool, ntiles)
            if prefetch:
                pool.wait_ge(prefetched, 16 * len(prefetch))


def run_units(eng, stages):
    per = 2 * SEQ // P

    def step(j, u):
        for stage, lag in stages:
            if isinstance(j, int) and not 0 <= per * j + u - lag < HEADS // 2 * per:
                continue
            if u >= lag:
                stage(j, u - lag)
            else:
                stage(j - 1, u - lag + per)

    for u in range(per):
        step(0, u)
    with eng.Fori(1, HEADS // 2) as j:
        for u in range(per):
            step(j, u)
    for u in range(max(lag for _, lag in stages)):
        step(HEADS // 2, u)


def attend_prompt(kit, proj, oT, ident, identb, causal, neg_lam, beside):
    nc = kit.nc
    NQ = SEQ // P
    names = ("qk_in", "v_in", "v_turned", "v_kept", "scored", "peaked", "biased", "exped", "inverted", "coefd",
             "w_first", "weighted", "turned", "kept", "summed", "evacuated", "high", "low")
    S = {n: kit.sem("ap_" + n) for n in names}
    head_out = [kit.sem(f"ap_head_out{b}") for b in range(2)]
    beside_done = kit.sem("ap_beside_done")
    SCALE = DH ** -0.5
    with ExitStack() as ctx:
        dup = kit.sb(ctx, "ap_dup", [P, 2, 2, SEQ])
        qs = kit.sb(ctx, "ap_qs", [P, 2, 2, SEQ], F32R)
        kh = kit.sb(ctx, "ap_kh", [P, 2, 2, SEQ], F32R)
        kl = kit.sb(ctx, "ap_kl", [P, 2, 2, SEQ], F32R)
        vin = kit.sb(ctx, "ap_vin", [P, SEQ])
        vt = kit.sb(ctx, "ap_vt", [P, 2, NQ, P])
        pexp = kit.sb(ctx, "ap_pexp", [P, 2, 2, SEQ])
        wgt = kit.sb(ctx, "ap_wgt", [P, 2, SEQ])
        wT = kit.sb(ctx, "ap_wT", [P, 2, NQ, P])
        small = kit.sb(ctx, "ap_small", [P, 2, 10])
        out = kit.sb(ctx, "ap_out", [P, 2, SEQ])
        sc = kit.ps(ctx, "ap_sc", [P, 2, SEQ])
        tp = kit.ps(ctx, "ap_tp", [P, NQ, P])
        pv = kit.ps(ctx, "ap_pv", [P, 2, 512])
        block = ctx.enter_context(nc.Block())
        unit = lambda j, u: j * (2 * NQ) + u
        head_of = lambda j, u: j * 2 + u // NQ
        early = lambda j, u, n: isinstance(j, int) and j * 2 * NQ + u < n

        @block.gpsimd
        def _(pool):
            beside(pool, beside_done)

        @block.sync
        def _(sp):
            def load(h, first):
                if not first:
                    sp.wait_ge(S["low"], h * 4)
                tile = lambda n: proj[n] if isinstance(n, int) else proj[ds(n, 1)].rearrange("a p t -> (a p) t")
                for n in range(2):
                    src = tile(h + n * HEADS)[:, 0:SEQ].rearrange("(c r) t -> r c t", c=2)
                    for rows in (slice(0, DH), slice(DH, P)):
                        sp.dma_start(dup[rows, n], src).then_inc(S["qk_in"], 16)
                if not first:
                    sp.wait_ge(S["v_turned"], h)
                sp.dma_start(vin[:], tile(h + 2 * HEADS)[:, 0:SEQ]).then_inc(S["v_in"], 16)

            def head(h, b):
                load(h + 1, False)
                sp.wait_ge(S["evacuated"], (h + 1) * NQ)
                dst = oT[h] if isinstance(h, int) else oT[ds(h, 1)].rearrange("a p t -> (a p) t")
                sp.dma_start(dst[:, 0:SEQ], out[:, b]).then_inc(head_out[b], 16)

            load(0, True)
            for b in range(2):
                head(b, b)
            with sp.Fori(1, HEADS // 2) as j:
                for b in range(2):
                    head(j * 2 + b, b)
            for b in range(2):
                sp.wait_ge(head_out[b], 16 * (HEADS // 2))
            sp.wait_ge(S["v_in"], 16 * (HEADS + 1))

        @block.tensor
        def _(pe):
            def score(j, u):
                s, h, hb, i = unit(j, u), head_of(j, u), u // NQ, u % NQ
                if i == 0:
                    pe.wait_ge(S["high"], (h + 1) * 4)
                    pe.wait_ge(S["low"], (h + 1) * 4)
                keys = (i + 1) * P
                for c in range(2):
                    if not early(j, u, 1):
                        pe.wait_ge(S["exped"], s * 2 - 1 + c)
                    for at in range(0, keys, 512):
                        n = min(512, keys - at)
                        diag = at + n == keys
                        for k in (kh, kl):
                            last = nc.tensor.matmul(sc[:, c, at:at + n], qs[:, hb, c, i * P:(i + 1) * P],
                                                    k[:, hb, c, at:at + n], start=(k is kh),
                                                    stop=(k is kl and not diag))
                        if diag:
                            last = nc.tensor.matmul(sc[:, c, i * P:keys], identb, causal, start=False, stop=True)
                    last.then_inc(S["scored"], 1)

            def turn_v(j, u):
                s, h, i = unit(j, u), head_of(j, u), u % NQ
                if i != 1:
                    return
                pe.wait_ge(S["v_in"], (h + 1) * 16)
                if not early(j, u, NQ):
                    pe.wait_ge(S["kept"], s - 2)
                for n in range(NQ):
                    last = nc.tensor.transpose(tp[:, n, :], vin[:, n * P:(n + 1) * P], ident)
                last.then_inc(S["v_turned"], 1)

            def turn(j, u):
                s, h, i = unit(j, u), head_of(j, u), u % NQ
                pe.wait_ge(S["weighted"], s + 1)
                if not early(j, u, 1):
                    pe.wait_ge(S["kept"], s)
                if early(j, u, 1):
                    pe.wait_ge(S["v_kept"], 1)
                elif i == NQ - 1 and not (isinstance(j, int) and h == HEADS - 1):
                    pe.wait_ge(S["v_kept"], h + 2)
                for n in range(i + 1):
                    last = nc.tensor.transpose(tp[:, n, :], wgt[:, u % 2, n * P:(n + 1) * P], ident)
                last.then_inc(S["turned"], 1)

            def values(j, u):
                s, h, hb, i = unit(j, u), head_of(j, u), u // NQ, u % NQ
                if i == 0:
                    pe.wait_ge(S["v_kept"], h + 1)
                pe.wait_ge(S["kept"], s + 1)
                if not early(j, u, 2):
                    pe.wait_ge(S["evacuated"], s - 1)
                for n in range(i + 1):
                    last = nc.tensor.matmul(pv[:, u % 2, 0:P], vt[:, hb, n, :], wT[:, u % 2, n, :],
                                            start=(n == 0), stop=(n == i))
                last.then_inc(S["summed"], 1)

            run_units(pe, ((score, 0), (turn_v, 0), (turn, 2), (values, 3)))

        @block.vector
        def _(dve):
            def low(h, hb, part):
                n, c = part // 2, part % 2
                dve.wait_ge(S["high"], h * 4 + part + 1)
                if n == 0:
                    nc.vector.tensor_tensor(qs[DH:P, hb, c], dup[DH:P, 0, c], qs[DH:P, hb, c].bitcast(F32),
                                            ALU.subtract).then_inc(S["low"], 1)
                else:
                    nc.vector.tensor_tensor(kl[:, hb, c], dup[:, 1, c], kh[:, hb, c].bitcast(F32),
                                            ALU.subtract).then_inc(S["low"], 1)

            def peak(j, u):
                s, b, keys = unit(j, u), u % 2, (u % NQ + 1) * P
                for c in range(2):
                    dve.wait_ge(S["scored"], s * 2 + c + 1)
                    nc.vector.tensor_reduce(small[:, b, c:c + 1], sc[:, c, 0:keys], AX, ALU.max)\
                        .then_inc(S["peaked"], 1)
                    dve.wait_ge(S["peaked"], s * 2 + c + 1)
                    nc.vector.tensor_scalar(small[:, b, 2 + c:3 + c], small[:, b, c:c + 1], -SCALE, None,
                                            ALU.mult).then_inc(S["biased"], 1)

            def weight(j, u):
                s, b, keys = unit(j, u), u % 2, (u % NQ + 1) * P
                dve.wait_ge(S["exped"], s * 2 + 2)
                nc.vector.reciprocal(small[:, b, 6:8], small[:, b, 4:6]).then_inc(S["inverted"], 1)
                dve.wait_ge(S["inverted"], s + 1)
                nc.vector.tensor_scalar(small[:, b, 8:9], small[:, b, 7:8], neg_lam, None,
                                        ALU.mult).then_inc(S["coefd"], 1)
                if not early(j, u, 2):
                    dve.wait_ge(S["turned"], s - 1)
                nc.vector.tensor_scalar(wgt[:, b, 0:keys], pexp[:, b, 0, 0:keys], small[:, b, 6:7], None,
                                        ALU.mult).then_inc(S["w_first"], 1)
                dve.wait_ge(S["coefd"], s + 1)
                dve.wait_ge(S["w_first"], s + 1)
                nc.vector.scalar_tensor_tensor(wgt[:, b, 0:keys], pexp[:, b, 1, 0:keys], small[:, b, 8:9],
                                               wgt[:, b, 0:keys], ALU.mult, ALU.add).then_inc(S["weighted"], 1)

            def split(j, u):
                if u % NQ >= NQ - 4:
                    low(head_of(j, u) + 1, 1 - u // NQ, u % NQ - (NQ - 4))

            for part in range(4):
                low(0, 0, part)
            run_units(dve, ((peak, 0), (weight, 1), (split, 0)))

        @block.scalar
        def _(act):
            def high(h, hb, part):
                n, c = part // 2, part % 2
                nc.scalar.activation((qs, kh)[n][:, hb, c], dup[:, n, c], ACT.Copy).then_inc(S["high"], 1)

            def split(j, u):
                i, h = u % NQ, head_of(j, u) + 1
                if i >= NQ - 5 and i < NQ - 1:
                    if i == NQ - 5:
                        act.wait_ge(S["qk_in"], h * 64 + 64)
                        if not early(j, u, NQ):
                            act.wait_ge(S["scored"], (h - 1) * (2 * NQ))
                    high(h, 1 - u // NQ, i - (NQ - 5))

            def keep_v(j, u):
                h, hb = head_of(j, u), u // NQ
                if u % NQ != 1:
                    return
                act.wait_ge(S["v_turned"], h + 1)
                if not early(j, u, 2 * NQ):
                    act.wait_ge(S["summed"], (h - 1) * NQ)
                nc.scalar.activation(vt[:, hb], tp[:], ACT.Copy).then_inc(S["v_kept"], 1)

            def exponential(j, u):
                s, b, keys = unit(j, u), u % 2, (u % NQ + 1) * P
                if not early(j, u, 2):
                    act.wait_ge(S["weighted"], s - 1)
                for c in range(2):
                    act.wait_ge(S["biased"], s * 2 + c + 1)
                    nc.scalar.activation(pexp[:, b, c, 0:keys], sc[:, c, 0:keys], ACT.Exp,
                                         bias=small[:, b, 2 + c:3 + c], scale=SCALE,
                                         accum_out=small[:, b, 4 + c:5 + c]).then_inc(S["exped"], 1)

            def keep(j, u):
                s, b, i = unit(j, u), u % 2, u % NQ
                act.wait_ge(S["turned"], s + 1)
                if not early(j, u, 2):
                    act.wait_ge(S["summed"], s - 1)
                nc.scalar.activation(wT[:, b, 0:i + 1, :], tp[:, 0:i + 1, :], ACT.Copy).then_inc(S["kept"], 1)

            def leave(j, u):
                s, h, hb, i = unit(j, u), head_of(j, u), u // NQ, u % NQ
                act.wait_ge(S["summed"], s + 1)
                if i == 0 and not early(j, u, 2 * NQ):
                    act.wait_ge(head_out[hb], j * 16)
                nc.scalar.activation(out[:, hb, i * P:(i + 1) * P], pv[:, u % 2, 0:P],
                                     ACT.Copy).then_inc(S["evacuated"], 1)

            act.wait_ge(S["qk_in"], 64)
            for part in range(4):
                high(0, 0, part)
            run_units(act, ((keep_v, 0), (exponential, 0), (keep, 2), (leave, 3), (split, 0)))


def attend_sample(kit, a, proj, oT, ident, identb, neg_lam_rows):
    nc = kit.nc
    SCALE = DH ** -0.5
    W = PAGES * PAGE + NS
    names = ("table_in", "small_in", "q_zeroed", "q_placed", "v_turned", "v_kept", "scored", "peaked", "biased",
             "exped", "inverted", "scaled", "combined", "turned", "kept", "summed", "evacuated", "stored", "q_picked",
             "w_zeroed", "out_turned", "out_kept")
    S = {n: kit.sem("as_" + n) for n in names}
    k_in = [kit.sem(f"as_k_in{b}") for b in range(2)]
    v_in = [kit.sem(f"as_v_in{b}") for b in range(2)]
    with ExitStack() as ctx:
        table = kit.sb(ctx, "as_table", [1, NB * PAGES], I32)
        qkv = kit.sb(ctx, "as_qkv", [P, 3, HEADS, NS])
        qd = kit.sb(ctx, "as_qd", [P, NB, HEADS, 32])
        qb = kit.sb(ctx, "as_qb", [P, 2, HEADS, 32])
        vnew = kit.sb(ctx, "as_vnew", [NS, HEADS, P])
        mask = kit.sb(ctx, "as_mask", [P, NB * NS], BF16)
        comb = kit.sb(ctx, "as_comb", [P, 18])
        kT = kit.sb(ctx, "as_kT", [P, 2, PAGES, HEADS, PAGE])
        vp = kit.sb(ctx, "as_vp", [P, 2, PAGES, HEADS * P])
        pexp = kit.sb(ctx, "as_pexp", [P, 2, W])
        small = kit.sb(ctx, "as_small", [P, 2, 6])
        combs = kit.sb(ctx, "as_combs", [P, 2, 16])
        wT = kit.sb(ctx, "as_wT", [P, 2, PAGES + 1, HEADS, 32])
        rows_out = kit.sb(ctx, "as_rows_out", [P, NB, P])
        out = kit.sb(ctx, "as_out", [P, HEADS, NS])
        sc = kit.ps(ctx, "as_sc", [P, 3 * 512])
        tp = kit.ps(ctx, "as_tp", [P, 512])
        pv = kit.ps(ctx, "as_pv", [P, 512])
        vps = kit.ps(ctx, "as_vps", [P, 512])
        ot = kit.ps(ctx, "as_ot", [P, NB, P])
        block = ctx.enter_context(nc.Block())

        def pages(eng, n, b, dst, pool_dram, arrived):
            for j in range(PAGES):
                page = eng.value_load(table[0:1, ds(n * PAGES + j, 1)], min_val=0, max_val=POOL - 1)
                eng.dma_start(dst[:, b, j].rearrange("p h c -> p (h c)") if len(dst.shape) == 5 else dst[:, b, j],
                              pool_dram[ds(page, 1)].rearrange("a p n -> (a p) n")).then_inc(arrived[b], 16)

        @block.sync
        def _(sp):
            sp.dma_start(table[:], a["table"]).then_inc(S["table_in"], 16)
            for j in range(3):
                sp.dma_start(qkv[:, j], proj[j * HEADS:(j + 1) * HEADS, :, SEQ:T].rearrange("h p t -> p h t"))\
                    .then_inc(S["small_in"], 16)
            sp.dma_start(mask[:], a["new_mask"]).then_inc(S["small_in"], 16)
            sp.dma_start(comb[:, 0:17], a["comb"]).then_inc(S["small_in"], 16)
            sp.wait_ge(S["table_in"], 16)
            pages(sp, 0, 0, kT, a["k_pool"], k_in)
            pages(sp, 1, 1, kT, a["k_pool"], k_in)
            with sp.Fori(1, NB // 2) as i:
                for b in range(2):
                    sp.wait_ge(S["scored"], i * 2 + b - 1)
                    pages(sp, i * 2 + b, b, kT, a["k_pool"], k_in)
            sp.wait_ge(S["out_kept"], 1)
            sp.dma_start(oT.rearrange("h p t -> p h t")[:, :, SEQ:T], out[:]).then_inc(S["stored"], 16)
            sp.wait_ge(S["stored"], 16)

        @block.gpsimd
        def _(pool):
            nc.gpsimd.memset(qd[:], 0.0).then_inc(S["q_zeroed"], 1)
            nc.gpsimd.memset(wT[:], 0.0).then_inc(S["w_zeroed"], 1)
            pool.wait_ge(S["small_in"], 16 * 5)
            pool.wait_ge(S["q_zeroed"], 1)
            pool.wait_ge(S["w_zeroed"], 1)
            for c in range(2):
                rows = slice(c * DH, (c + 1) * DH)
                for h in range(HEADS):
                    nc.gpsimd.tensor_copy(qd[rows, :, h, c * NT:(c + 1) * NT],
                                          qkv[rows, 0, h, :].rearrange("p (n t) -> p n t", t=NT))\
                        .then_inc(S["q_placed"], 1)
            pool.wait_ge(S["q_placed"], 2 * HEADS)

            def pick(n, b, first):
                if not first:
                    pool.wait_ge(S["scored"], n - 1)
                nc.gpsimd.tensor_copy(qb[:, b], qd[:, ds(n, 1)].rearrange("p a h c -> p (a h) c"))\
                    .then_inc(S["q_picked"], 1)
            pick(0, 0, True)
            pick(1, 1, True)
            pool.wait_ge(S["table_in"], 16)
            pages(pool, 0, 0, vp, a["v_pool"], v_in)
            pages(pool, 1, 1, vp, a["v_pool"], v_in)
            with pool.Fori(1, NB // 2) as i:
                for b in range(2):
                    pick(i * 2 + b, b, False)
                    pool.wait_ge(S["summed"], i * 2 + b - 1)
                    pages(pool, i * 2 + b, b, vp, a["v_pool"], v_in)

        @block.tensor
        def _(pe):
            pe.wait_ge(S["small_in"], 16 * 5)
            for h in range(HEADS):
                last = nc.tensor.transpose(vps[0:NS, h * P:(h + 1) * P], qkv[:, 2, h, :], ident)
            last.then_inc(S["v_turned"], 1)
            pe.wait_ge(S["v_kept"], 1)

            def back(n, b, turn, first):
                pe.wait_ge(S["combined"], n + 1)
                if not first:
                    pe.wait_ge(S["kept"], n)
                for j in range(PAGES + 1):
                    keys = PAGE if j < PAGES else NS
                    last = nc.tensor.matmul(tp[0:keys, j * 16:(j + 1) * 16],
                                            pexp[:, b, j * PAGE:j * PAGE + keys], combs[:, b, :],
                                            start=True, stop=True)
                last.then_inc(S["turned"], 1)
                pe.wait_ge(v_in[b], (turn + 1) * 16 * PAGES)
                pe.wait_ge(S["kept"], n + 1)
                if not first:
                    pe.wait_ge(S["evacuated"], n)
                for h in range(HEADS):
                    for j in range(PAGES + 1):
                        if j < PAGES:
                            v, w = vp[:, b, j, h * P:(h + 1) * P], wT[:, b, j, h, :]
                        else:
                            v, w = vnew[:, h, :], wT[0:NS, b, j, h, :]
                        last = nc.tensor.matmul(pv[32 * h:32 * h + 32, 0:P], w, v, start=(j == 0), stop=(j == PAGES))
                last.then_inc(S["summed"], 1)

            def front(n, b, turn, first):
                pe.wait_ge(k_in[b], (turn + 1) * 16 * PAGES)
                pe.wait_ge(S["q_picked"], n + 1)
                if not (isinstance(n, int) and n == 0):
                    pe.wait_ge(S["exped"], n)
                for h in range(HEADS):
                    rows = slice(32 * h, 32 * h + 32)
                    for half in range(2):
                        last = nc.tensor.matmul(sc[rows, half * 512:(half + 1) * 512], qb[:, b, h, :],
                                                kT[:, b, half * 4:half * 4 + 4, h, :], start=True, stop=True)
                    last = nc.tensor.matmul(sc[rows, 1024:W], qb[:, b, h, :], qkv[:, 1, h, :],
                                            start=True, stop=False, skip_group_check=True)
                nc.tensor.matmul(sc[:, 1024:W], identb, mask[:, ds(n * NS, NS)], start=False, stop=True,
                                 skip_group_check=True).then_inc(S["scored"], 1)

            front(0, 0, 0, True)
            front(1, 1, 0, True)
            back(0, 0, 0, True)
            front(2, 0, 1, False)
            back(1, 1, 0, False)
            front(3, 1, 1, False)
            back(2, 0, 1, False)
            with pe.Fori(2, NB // 2) as i:
                front(i * 2, 0, i, False)
                back(i * 2 - 1, 1, i - 1, False)
                front(i * 2 + 1, 1, i, False)
                back(i * 2, 0, i, False)
            back(NB - 1, 1, NB // 2 - 1, False)
            pe.wait_ge(S["evacuated"], NB)
            for n in range(NB):
                last = nc.tensor.transpose(ot[:, n, :], rows_out[:, n, :], ident)
            last.then_inc(S["out_turned"], 1)

        @block.vector
        def _(dve):
            dve.wait_ge(S["w_zeroed"], 1)
            dve.wait_ge(S["v_turned"], 1)
            nc.vector.tensor_copy(vnew[:].rearrange("p h c -> p (h c)"), vps[0:NS, :]).then_inc(S["v_kept"], 1)

            def front(n, b, first):
                dve.wait_ge(S["scored"], n + 1)
                nc.vector.tensor_reduce(small[:, b, 0:1], sc[:, 0:W], AX, ALU.max).then_inc(S["peaked"], 1)
                dve.wait_ge(S["peaked"], n + 1)
                nc.vector.tensor_scalar(small[:, b, 1:2], small[:, b, 0:1], -SCALE, None,
                                        ALU.mult).then_inc(S["biased"], 1)
                dve.wait_ge(S["exped"], n + 1)
                nc.vector.reciprocal(small[:, b, 3:4], small[:, b, 2:3]).then_inc(S["inverted"], 1)
                dve.wait_ge(S["inverted"], n + 1)
                nc.vector.tensor_scalar(small[:, b, 4:5], small[:, b, 3:4], neg_lam_rows, None,
                                        ALU.mult).then_inc(S["scaled"], 1)
                dve.wait_ge(S["scaled"], n + 1)
                if not first:
                    dve.wait_ge(S["turned"], n - 1)
                nc.vector.tensor_scalar(combs[:, b, :], comb[:, 0:16], small[:, b, 4:5], None,
                                        ALU.mult).then_inc(S["combined"], 1)

            def back(n, b, first):
                dve.wait_ge(S["turned"], n + 1)
                if not first:
                    dve.wait_ge(S["summed"], n - 1)
                tokens = lambda z, j: z.rearrange("p (j h t) -> p j h t", j=j, t=NT)
                nc.vector.tensor_copy(wT[:, b, 0:PAGES, :, 0:NT], tokens(tp[:, 0:PAGES * 16], PAGES))
                nc.vector.tensor_copy(wT[0:NS, b, PAGES:, :, 0:NT],
                                      tokens(tp[0:NS, PAGES * 16:(PAGES + 1) * 16], 1)).then_inc(S["kept"], 1)
                dve.wait_ge(S["summed"], n + 1)
                nc.vector.tensor_copy(rows_out[:, ds(n, 1)].rearrange("p a c -> p (a c)"), pv[:, 0:P])\
                    .then_inc(S["evacuated"], 1)
            front(0, 0, True)
            front(1, 1, True)
            back(0, 0, True)
            front(2, 0, False)
            back(1, 1, True)
            front(3, 1, False)
            back(2, 0, False)
            with dve.Fori(2, NB // 2) as i:
                front(i * 2, 0, False)
                back(i * 2 - 1, 1, False)
                front(i * 2 + 1, 1, False)
                back(i * 2, 0, False)
            back(NB - 1, 1, False)
            dve.wait_ge(S["out_turned"], 1)
            nc.vector.tensor_copy(out[:].rearrange("p h (n t) -> p n h t", t=NT),
                                  ot[:].rearrange("p n (h c) -> p n h c", c=32)[:, :, :, 0:NT])\
                .then_inc(S["out_kept"], 1)

        @block.scalar
        def _(act):
            def step(n, b, first):
                act.wait_ge(S["biased"], n + 1)
                if not first:
                    act.wait_ge(S["turned"], n - 1)
                nc.scalar.activation(pexp[:, b, :], sc[:, 0:W], ACT.Exp, bias=small[:, b, 1:2], scale=SCALE,
                                     accum_out=small[:, b, 2:3]).then_inc(S["exped"], 1)
            step(0, 0, True)
            step(1, 1, True)
            with act.Fori(1, NB // 2) as i:
                for b in range(2):
                    step(i * 2 + b, b, False)

NPAIR = 4
NSTEP = 6
NLEV = 6


def rwkv_mix(kit, ctx, a, proj, param, dsts):
    nc = kit.nc
    NBUF = 4
    S = {n: kit.sem("mx_" + n) for n in ("state_in", "omu", "scaled", "mixed")}
    cur_in = [kit.sem(f"mx_cur_in{b}") for b in range(NBUF)]
    with ExitStack() as inner:
        cur = kit.sb(inner, "mx_cur", [P, NBUF, T])
        st = kit.sb(inner, "mx_st", [P, 14, NB])
        omu = kit.sb(inner, "mx_omu", [P, 14])
        block = inner.enter_context(nc.Block())

        @block.sync
        def _(sp):
            sp.dma_start(st[:], a["shiftT"]).then_inc(S["state_in"], 16)
            for j in range(14):
                if j >= NBUF:
                    sp.wait_ge(S["mixed"], 3 * (j - NBUF + 1))
                sp.dma_start(cur[:, j % NBUF], proj[12 + j]).then_inc(cur_in[j % NBUF], 16)

        @block.scalar
        def _(act):
            act.wait_ge(S["omu"], 1)
            for j in range(14):
                b = j % NBUF
                act.wait_ge(cur_in[b], 16 * (j // NBUF + 1))
                nc.scalar.activation(dsts[j], cur[:, b], ACT.Copy, scale=omu[:, j:j + 1]).then_inc(S["scaled"], 1)

        @block.vector
        def _(dve):
            mu = param("mu", 14)
            nc.vector.tensor_scalar(omu[:], mu, -1.0, 1.0, ALU.mult, ALU.add).then_inc(S["omu"], 1)
            dve.wait_ge(S["state_in"], 16)
            for j in range(14):
                c, d, m = cur[:, j % NBUF], dsts[j], mu[:, j:j + 1]
                cs, dd = (z[:, SEQ:].rearrange("p (n t) -> p n t", t=NT) for z in (c, d))
                dve.wait_ge(S["scaled"], j + 1)
                for out, before in ((d[:, 1:SEQ], c[:, 0:SEQ - 1]), (dd[:, :, 1:NT], cs[:, :, 0:NT - 1]),
                                    (dd[:, :, 0], st[:, j, :])):
                    nc.vector.scalar_tensor_tensor(out, before, m, out, ALU.mult, ALU.add).then_inc(S["mixed"], 1)
            dve.wait_ge(S["mixed"], 3 * 14)


def rwkv_prepare(kit, ctx, a, param, Rm, Km, V, X12, XG, NR, Bc, Kc, BON, G, ELC, SD, spill,
                 ident, blockcol):
    nc = kit.nc
    names = ("w_in", "kaed", "tanhed", "z", "za", "g", "ss", "rks", "th", "ta", "g_kept", "rooted", "e_in",
             "e_ex", "e_neg", "lw", "av", "kk", "sq", "ssm", "inv", "kn", "bv", "fv", "kp", "rk", "rk2", "bonus",
             "lin", "lex", "norm", "nr0", "nr1", "bc", "kc", "elc", "sd", "sdw", "xg1", "xg2", "spilled")
    S = {n: kit.sem("rp_" + n) for n in names}
    with ExitStack() as inner:
        w2 = kit.sb(inner, "rp_w2", [P, 512])
        g2 = kit.sb(inner, "rp_g2", [P, 512])
        blk = kit.sb(inner, "rp_blk", [P, P])
        reset = kit.sb(inner, "rp_reset", [P, SEQ], BF16)
        hc = kit.sb(inner, "rp_hc", [P, 12])
        tw = kit.sb(inner, "rp_tw", [P, T])
        tv = kit.sb(inner, "rp_tv", [P, T])
        ta = kit.sb(inner, "rp_ta", [P, T])
        tk = kit.sb(inner, "rp_tk", [P, T])
        tq = kit.sb(inner, "rp_tq", [P, T])
        tl = kit.sb(inner, "rp_tl", [P, 2, SEQ])
        te = kit.sb(inner, "rp_te", [P, 3, SEQ])
        pz = kit.ps(inner, "rp_pz", [P, 3, 512])
        pq = kit.ps(inner, "rp_pq", [P, 3, 512])
        pc = kit.ps(inner, "rp_pc", [P, NBLK, 2])
        norms = kit.sb(inner, "rp_norms", [P, NBLK, 2])
        block = inner.enter_context(nc.Block())
        part = lambda z: z.rearrange("p (n t) -> p n t", t=T3)

        @block.sync
        def _(sp):
            for dst, src in ((w2[0:64, :], a["w2"]), (w2[64:128, :], a["a2"]), (g2[:], a["g2"]),
                             (blk[:], a["blockones"]), (reset[:], a["reset"])):
                sp.dma_start(dst, src).then_inc(S["w_in"], 16)
            for p in range(NPAIR):
                sp.wait_ge(S["g_kept"], p + 1)
                sp.dma_start(spill[1][:, p], G[:, p]).then_inc(S["spilled"], 16)
                sp.wait_ge(S["bonus"], p + 1)
                sp.dma_start(spill[0][:, p], BON[:, p]).then_inc(S["spilled"], 16)
            sp.wait_ge(S["spilled"], 2 * 16 * NPAIR)

        @block.tensor
        def _(pe):
            def product(psum, lhsT, rhs, sem):
                for n in range(3):
                    last = nc.tensor.matmul(psum[:, n, 0:T3], lhsT, rhs[:, n * T3:(n + 1) * T3], start=True, stop=True)
                last.then_inc(S[sem], 1)
            pe.wait_ge(S["w_in"], 80)
            for p in range(NPAIR):
                cs = slice(p * P, (p + 1) * P)
                pe.wait_ge(S["tanhed"], 1)
                if p:
                    pe.wait_ge(S["bonus"], p)
                product(pz, w2[0:64, cs], X12[0:64, :], "z")
                if p:
                    pe.wait_ge(S["kn"], p)
                product(pq, w2[64:128, cs], X12[64:128, :], "za")
                pe.wait_ge(S["th"], p + 1)
                pe.wait_ge(S["xg2"], 1)
                product(pz, g2[:, cs], XG, "g")
                pe.wait_ge(S["sq"], p + 1)
                if p:
                    pe.wait_ge(S["rooted"], 2 * p)
                sum_heads(nc, pc, tq, blockcol).then_inc(S["ss"], 1)
                pe.wait_ge(S["ta"], p + 1)
                pe.wait_ge(S["inv"], 2 * p + 2)
                spread_heads(nc, pq[:].rearrange("p n t -> p (n t)"), norms, ident).then_inc(S["norm"], 1)
                pe.wait_ge(S["g_kept"], p + 1)
                pe.wait_ge(S["rk2"], p + 1)
                product(pz, blk[:], tq, "rks")

        @block.scalar
        def _(act):
            nc.scalar.activation(X12[0:64, :], X12[0:64, :], ACT.Tanh).then_inc(S["tanhed"], 1)
            nc.scalar.activation(XG, XG, ACT.Tanh, scale=0.5).then_inc(S["xg1"], 1)
            act.wait_ge(S["kaed"], 3)
            for p in range(NPAIR):
                act.wait_ge(S["z"], p + 1)
                if p:
                    act.wait_ge(S["lw"], p)
                nc.scalar.activation(part(tw[:]), pz[:, :, 0:T3], ACT.Tanh, bias=hc[:, p:p + 1],
                                     scale=0.5).then_inc(S["th"], 1)
                act.wait_ge(S["za"], p + 1)
                if p:
                    act.wait_ge(S["fv"], p)
                    act.wait_ge(S["bv"], p)
                    act.wait_ge(S["sd"], 5 * p)
                nc.scalar.activation(part(ta[:]), pq[:, :, 0:T3], ACT.Tanh, bias=hc[:, 4 + p:5 + p],
                                     scale=0.5).then_inc(S["ta"], 1)
                act.wait_ge(S["g"], p + 1)
                nc.scalar.activation(part(G[:, p]), pz[:, :, 0:T3], ACT.Copy).then_inc(S["g_kept"], 1)
                act.wait_ge(S["lin"], p + 1)
                if p:
                    act.wait_ge(S["nr1"], p)
                    act.wait_ge(S["nr0"], p)
                    act.wait_ge(S["bc"], p)
                    act.wait_ge(S["kc"], p)
                    act.wait_ge(S["elc"], p)
                nc.scalar.activation(te[:, 0], tl[:, 0], ACT.Exp).then_inc(S["e_in"], 1)
                nc.scalar.activation(te[:, 2], tl[:, 0], ACT.Exp, scale=-1.0).then_inc(S["e_neg"], 1)
                act.wait_ge(S["lex"], p + 1)
                nc.scalar.activation(te[:, 1], tl[:, 1], ACT.Exp).then_inc(S["e_ex"], 1)
                nc.scalar.activation(SD[:, p, 0, :], tv[:, SEQ:T], ACT.Exp).then_inc(S["sdw"], 1)
                act.wait_ge(S["ss"], p + 1)
                if p:
                    act.wait_ge(S["norm"], p)
                for rows, cols in TOKEN_PARTS:
                    nc.scalar.activation(norms[rows, cols], pc[rows, cols], ACT.Sqrt).then_inc(S["rooted"], 1)

        @block.vector
        def _(dve):
            kap = param("k_a", 4)
            nc.vector.tensor_scalar(hc[:, 0:4], param("w0", 4), 0.5, None, ALU.mult).then_inc(S["kaed"], 1)
            nc.vector.tensor_scalar(hc[:, 4:8], param("a0", 4), 0.5, None, ALU.mult).then_inc(S["kaed"], 1)
            nc.vector.tensor_scalar(hc[:, 8:12], kap, -1.0, 1.0, ALU.mult, ALU.add).then_inc(S["kaed"], 1)
            dve.wait_ge(S["kaed"], 3)
            dve.wait_ge(S["xg1"], 1)
            nc.vector.tensor_scalar(XG, XG, 1.0, 0.5, ALU.add, ALU.mult).then_inc(S["xg2"], 1)
            dve.wait_ge(S["w_in"], 80)
            for p in range(NPAIR):
                col = lambda name: param(name, 4)[:, p:p + 1]
                r, k, v = Rm[:, p], Km[:, p], V[:, p]
                if p:
                    dve.wait_ge(S["kn"], p)
                    dve.wait_ge(S["bv"], p)
                    dve.wait_ge(S["nr0"], p)
                    dve.wait_ge(S["sd"], 5 * p)
                nc.vector.tensor_scalar(tk[:], k, col("k_k"), None, ALU.mult).then_inc(S["kk"], 1)
                dve.wait_ge(S["kk"], p + 1)
                if p:
                    dve.wait_ge(S["rks"], p)
                nc.vector.tensor_tensor(tq[:], tk[:], tk[:], ALU.mult).then_inc(S["sq"], 1)
                dve.wait_ge(S["th"], p + 1)
                if p:
                    dve.wait_ge(S["sdw"], p)
                nc.vector.tensor_scalar(tv[:], tw[:], 1.0, -E05 / 2, ALU.add, ALU.mult).then_inc(S["lw"], 1)
                dve.wait_ge(S["lw"], p + 1)
                if p:
                    dve.wait_ge(S["e_ex"], p)
                    dve.wait_ge(S["e_neg"], p)
                nc.vector.tensor_tensor_scan(tl[:, 0], reset[:], tv[:, 0:SEQ], 0.0, ALU.mult,
                                             ALU.add).then_inc(S["lin"], 1)
                dve.wait_ge(S["ta"], p + 1)
                nc.vector.tensor_scalar(ta[:], ta[:], 0.5, 0.5, ALU.mult, ALU.add).then_inc(S["av"], 1)
                dve.wait_ge(S["rooted"], 2 * p + 2)
                for n, (rows, cols) in enumerate(TOKEN_PARTS):
                    nc.vector.tensor_scalar(norms[rows, cols], norms[rows, cols], 1e-12, None, ALU.max)\
                        .then_inc(S["ssm"], 1)
                    dve.wait_ge(S["ssm"], 2 * p + n + 1)
                    nc.vector.reciprocal(norms[rows, cols], norms[rows, cols]).then_inc(S["inv"], 1)
                dve.wait_ge(S["norm"], p + 1)
                nc.vector.tensor_tensor(tk[:], tk[:], pq[:].rearrange("p n t -> p (n t)")[:, 0:T], ALU.mult)\
                    .then_inc(S["kn"], 1)
                dve.wait_ge(S["av"], p + 1)
                dve.wait_ge(S["kn"], p + 1)
                nc.vector.tensor_scalar(tq[:], ta[:], col("k_a"), hc[:, 8 + p:9 + p], ALU.mult,
                                        ALU.add).then_inc(S["fv"], 1)
                dve.wait_ge(S["fv"], p + 1)
                nc.vector.tensor_tensor(k, k, tq[:], ALU.mult).then_inc(S["kp"], 1)
                nc.vector.tensor_tensor(ta[:], tk[:], ta[:], ALU.mult).then_inc(S["bv"], 1)
                dve.wait_ge(S["kp"], p + 1)
                nc.vector.tensor_scalar(tq[:], r, col("r_k"), None, ALU.mult).then_inc(S["rk"], 1)
                dve.wait_ge(S["rk"], p + 1)
                nc.vector.tensor_tensor(tq[:], tq[:], k, ALU.mult).then_inc(S["rk2"], 1)
                dve.wait_ge(S["e_ex"], p + 1)
                nc.vector.scalar_tensor_tensor(NR[:, p, 0, :], tk[:, 0:SEQ], -1.0, te[:, 1], ALU.mult,
                                               ALU.mult).then_inc(S["nr0"], 1)
                dve.wait_ge(S["e_in"], p + 1)
                nc.vector.tensor_copy(ELC[:, p, :], te[:, 0].rearrange("p (c t) -> p c t", t=C)[:, :, C - 1])\
                    .then_inc(S["elc"], 1)
                dve.wait_ge(S["rks"], p + 1)
                nc.vector.tensor_tensor(part(BON[:, p]), pz[:, :, 0:T3], part(v), ALU.mult).then_inc(S["bonus"], 1)

        @block.gpsimd
        def _(pool):
            for p in range(NPAIR):
                r, k, v = Rm[:, p], Km[:, p], V[:, p]
                pool.wait_ge(S["lin"], p + 1)
                if p:
                    pool.wait_ge(S["e_ex"], p)
                nc.gpsimd.tensor_tensor(tl[:, 1], tl[:, 0], tv[:, 0:SEQ], ALU.subtract).then_inc(S["lex"], 1)
                pool.wait_ge(S["e_in"], p + 1)
                nc.gpsimd.tensor_tensor(NR[:, p, 1, :], r[:, 0:SEQ], te[:, 0], ALU.mult).then_inc(S["nr1"], 1)
                pool.wait_ge(S["bv"], p + 1)
                pool.wait_ge(S["e_neg"], p + 1)
                nc.gpsimd.tensor_tensor(Bc[:, p], ta[:, 0:SEQ], te[:, 2], ALU.mult).then_inc(S["bc"], 1)
                pool.wait_ge(S["kp"], p + 1)
                nc.gpsimd.tensor_tensor(Kc[:, p], k[:, 0:SEQ], te[:, 2], ALU.mult).then_inc(S["kc"], 1)
                for q, src in ((1, tk[:]), (2, ta[:]), (3, k), (4, r), (5, v)):
                    nc.gpsimd.tensor_copy(SD[:, p, q, :], src[:, SEQ:T]).then_inc(S["sd"], 1)
            pool.wait_ge(S["sd"], 5 * NPAIR)


def rwkv_transitions(kit, a, NR, BK, V, Y):
    nc = kit.nc
    names = ("const_in", "zeroed", "eye_set", "placed", "p1", "p2", "adi0", "adi", "m3", "m2", "m4", "turn", "kept",
             "stacked", "ut", "uturn", "ubd", "made", "wz", "wbd0", "wbd", "a2v", "a2v_kept", "tx", "tn_kept",
             "xst", "xbd0", "xbd", "pr", "phi_kept", "r_kept", "zy", "z_kept", "y_kept")
    S = {n: kit.sem("rt_" + n) for n in names}
    with ExitStack() as ctx:
        strict = kit.sb(ctx, "rt_strict", [P, 2, C])
        pairbd = kit.sb(ctx, "rt_pairbd", [P, 2, C])
        levbd = kit.sb(ctx, "rt_levbd", [P, NLEV, 2, C])
        below = kit.sb(ctx, "rt_below", [P, C])
        incl = kit.sb(ctx, "rt_incl", [P, C])
        eye = kit.sb(ctx, "rt_eye", [P, C])
        ident = kit.sb(ctx, "rt_ident", [P, P])
        wide = lambda n, *k: kit.sb(ctx, "rt_" + n, [P, 2, *k, NPAIR, P])
        duo = lambda n: kit.sb(ctx, "rt_" + n, [P, 2, NPAIR, 2, C])
        slim = lambda n: kit.sb(ctx, "rt_" + n, [P, 2, NPAIR, C])
        bd, turned = wide("bd", 4), wide("turned", 4)
        m2, ut, ubd, wbd, tn, xbd = (wide(n) for n in ("m2", "ut", "ubd", "wbd", "tn", "xbd"))
        za, wz, bm, na = (duo(n) for n in ("za", "wz", "bm", "na"))
        m4, vs, xst = (slim(n) for n in ("m4", "vs", "xst"))
        q0, q1, q2, q3 = ([kit.ps(ctx, f"rt_q{n}{b}", [P, NPAIR, P]) for b in range(2)] for n in range(4))
        block = ctx.enter_context(nc.Block())
        half = lambda h: slice(h * C, (h + 1) * C)
        blocks = lambda z: z.rearrange("p a (h c) -> p a h c", h=2)
        side = lambda z: z.rearrange("p s c -> p (s c)")
        spread = lambda z: z.unsqueeze(2).broadcast_to([P, NPAIR, 2, C])
        pairs = lambda z: z.unsqueeze(1).broadcast_to([P, NPAIR, *z.shape[1:]])
        consts = ((strict, "strict"), (below, "below"), (incl, "incl"), (levbd, "levbd"), (pairbd, "pairbd"), (eye, "eye"),
                  (ident, "ident"))

        def turns(eng, turn):
            turn(0, True)
            with eng.Fori(1, NCH // 2) as i:
                turn(i, False)

        @block.sync
        def _(sp):
            for dst, src in consts:
                sp.dma_start(dst[:], a[src]).then_inc(S["const_in"], 16)

        @block.gpsimd
        def _(pool):
            for z in (bd, wbd, xbd):
                nc.gpsimd.memset(z[:], 0.0).then_inc(S["zeroed"], 1)
            pool.wait_ge(S["zeroed"], 3)
            pool.wait_ge(S["const_in"], 16 * len(consts))
            for b in range(2):
                nc.gpsimd.tensor_copy(za[:, b, :, 0], pairs(eye[:])).then_inc(S["eye_set"], 1)
            pool.wait_ge(S["eye_set"], 2)

            def place(i, b, first):
                c = i * 2 + b
                if not first:
                    pool.wait_ge(S["stacked"], i * 6)
                    pool.wait_ge(S["turn"], i * 8 - 2 + 2 * b)
                for q, src in enumerate((BK[:, 0], BK[:, 1], V, NR[:, :, 0, :])):
                    for h in range(2):
                        nc.gpsimd.tensor_copy(bd[half(h), b, q, :, half(h)],
                                              src[half(h), :, ds(c * C, C)]).then_inc(S["placed"], 1)

            def patch(i, b):
                pool.wait_ge(S["adi0"], i * 2 + b + 1)
                nc.gpsimd.tensor_tensor(za[:, b, :, 1], za[:, b, :, 1], pairs(eye[:]), ALU.add).then_inc(S["adi"], 1)

            def stack(i, b, first):
                if not first:
                    pool.wait_ge(S["zy"], i * 2 - 1 + b)
                for q, dst, count in ((0, bm[:, b, :, 0], 2 * b + 1), (2, vs[:, b], 2 * b + 5), (3, na[:, b, :, 0], 2 * b + 6)):
                    pool.wait_ge(S["kept"], i * 8 + count)
                    z = turned[:, b, q]
                    nc.gpsimd.tensor_tensor(dst, z[:, :, 0:C], z[:, :, C:P], ALU.add).then_inc(S["stacked"], 1)

            place(0, 0, True)
            place(0, 1, True)

            def turn(i, first):
                pool.wait_ge(S["placed"], i * 16 + 16)
                for b in range(2):
                    patch(i, b)
                for b in range(2):
                    stack(i, b, first)

            turn(0, True)
            with pool.Fori(1, NCH // 2) as i:
                for b in range(2):
                    place(i, b, False)
                turn(i, False)

        @block.tensor
        def _(pe):
            pe.wait_ge(S["const_in"], 16 * len(consts))
            mm = nc.tensor.matmul

            def turn(i, first):
                for b in range(2):
                    c = i * 2 + b
                    pe.wait_ge(S["placed"], c * 8 + 8)
                    for q, dst, freed, sem in ((0, q0, ("phi_kept", "r_kept"), "p1"), (1, q1, ("z_kept", "y_kept"), "p2")):
                        if not first:
                            for name in freed:
                                pe.wait_ge(S[name], c - 1)
                        for p in range(NPAIR):
                            last = mm(dst[b][:, p, :], bd[:, b, q, p, :], NR[:, p, :, ds(c * C, C)],
                                      start=True, stop=True)
                        last.then_inc(S[sem], 1)
                for r, (qa, qb) in enumerate(((0, 1), (2, 3))):
                    for b in range(2):
                        for n, (q, dst) in enumerate(((qa, q2), (qb, q3))):
                            if r == 1:
                                pe.wait_ge(S["kept"], i * 8 + 2 * b + n + 1)
                            elif not first:
                                pe.wait_ge(S["a2v_kept" if n == 0 else "xbd"], i * 2 - 1 + b)
                            for p in range(NPAIR):
                                last = nc.tensor.transpose(dst[b][:, p, :], bd[:, b, q, p, :], ident[:])
                            last.then_inc(S["turn"], 1)
                for lev in range(NLEV):
                    for b in range(2):
                        n = (i * NLEV + lev) * 2 + b
                        pe.wait_ge(S["ut"], n + 1)
                        if lev == 0:
                            pe.wait_ge(S["m4"], i * 2 + b + 1)
                        for p in range(NPAIR):
                            last = nc.tensor.transpose(q1[b][:, p, :], ut[:, b, p, :], ident[:])
                        last.then_inc(S["uturn"], 1)
                    for b in range(2):
                        n = (i * NLEV + lev) * 2 + b
                        pe.wait_ge(S["ubd"], n + 1)
                        if lev == 0:
                            pe.wait_ge(S["m3"], i * 2 + b + 1)
                            pe.wait_ge(S["adi"], i * 2 + b + 1)
                        else:
                            pe.wait_ge(S["wz"], (i * (NLEV - 1) + lev - 1) * 2 + b + 1)
                        src, w = za if lev == 0 else wz, C if lev == NLEV - 1 else 2 * C
                        for p in range(NPAIR):
                            last = mm(q0[b][:, p, 0:w], ubd[:, b, p, :], side(src[:, b, p])[:, 0:w], start=True, stop=True)
                        last.then_inc(S["made"], 1)
                    if lev == 0:
                        for b in range(2):
                            pe.wait_ge(S["m2"], i * 2 + b + 1)
                            pe.wait_ge(S["stacked"], i * 6 + b * 3 + 2)
                            pe.wait_ge(S["kept"], i * 8 + 8)
                            for p in range(NPAIR):
                                last = mm(q2[b][:, p, 0:C], m2[:, b, p, :], vs[:, b, p, :], start=True, stop=True)
                            last.then_inc(S["a2v"], 1)
                for b in range(2):
                    c = i * 2 + b
                    pe.wait_ge(S["wbd"], c + 1)
                    pe.wait_ge(S["a2v_kept"], c + 1)
                    pe.wait_ge(S["stacked"], i * 6 + b * 3 + 3)
                    for p in range(NPAIR):
                        last = mm(q3[b][:, p, :], wbd[:, b, p, :], side(na[:, b, p]), start=True, stop=True)
                    last.then_inc(S["tx"], 1)
                for b in range(2):
                    c = i * 2 + b
                    pe.wait_ge(S["tn_kept"], c + 1)
                    for p in range(NPAIR):
                        last = mm(q0[b][:, p, :], tn[:, b, p, :], side(bm[:, b, p]), start=True, stop=True)
                    last.then_inc(S["pr"], 1)
                    pe.wait_ge(S["xst"], c + 1)
                    pe.wait_ge(S["xbd"], c + 1)
                    for p in range(NPAIR):
                        mm(q1[b][:, p, 0:C], turned[:, b, 0, p, :], xst[:, b, p, :], start=True, stop=False)
                        mm(q1[b][:, p, 0:C], turned[:, b, 1, p, :], vs[:, b, p, :], start=False, stop=True)
                        mm(q1[b][:, p, C:P], xbd[:, b, p, :], bm[:, b, p, 1, :], start=True, stop=False)
                        last = mm(q1[b][:, p, C:P], turned[:, b, 2, p, :], m4[:, b, p, :], start=False, stop=True)
                    last.then_inc(S["zy"], 1)
            turns(pe, turn)

        @block.vector
        def _(dve):
            tt = nc.vector.tensor_tensor
            dve.wait_ge(S["const_in"], 16 * len(consts))

            def turn(i, first):
                for b in range(2):
                    c = i * 2 + b
                    dve.wait_ge(S["p1"], c + 1)
                    if not first:
                        dve.wait_ge(S["zy"], c - 1)
                    tt(za[:, b, :, 1], q0[b][:, :, 0:C], pairs(below[:]), ALU.mult)\
                        .then_inc(S["adi0"], 1)
                    tt(bm[:, b, :, 1], q0[b][:, :, C:P], pairs(incl[:]), ALU.mult).then_inc(S["m3"], 1)
                for b in range(2):
                    c = i * 2 + b
                    dve.wait_ge(S["p2"], c + 1)
                    tt(blocks(m2[:, b]), spread(q1[b][:, :, 0:C]), pairs(strict[:]), ALU.mult).then_inc(S["m2"], 1)
                    tt(m4[:, b], q1[b][:, :, C:P], pairs(incl[:]), ALU.mult).then_inc(S["m4"], 1)
                for lev in range(NLEV):
                    for b in range(2):
                        n = (i * NLEV + lev) * 2 + b
                        if lev == 0:
                            dve.wait_ge(S["adi"], i * 2 + b + 1)
                        else:
                            dve.wait_ge(S["made"], n - 1)
                        if not (first and lev == 0):
                            dve.wait_ge(S["uturn"], n - 1)
                        z = za[:, b, :, 1] if lev == 0 else q0[b][:, :, C:P]
                        tt(blocks(ut[:, b]), spread(z), pairs(levbd[:, lev]), ALU.mult).then_inc(S["ut"], 1)
                    for b in range(2):
                        n = (i * NLEV + lev) * 2 + b
                        dve.wait_ge(S["uturn"], n + 1)
                        if not (first and lev == 0):
                            dve.wait_ge(S["made"], n - 1)
                        nc.vector.tensor_copy(ubd[:, b], q1[b][:]).then_inc(S["ubd"], 1)
                for b in range(2):
                    c = i * 2 + b
                    dve.wait_ge(S["tx"], c + 1)
                    tt(blocks(tn[:, b]), spread(q3[b][:, :, 0:C]), pairs(pairbd[:]), ALU.mult).then_inc(S["tn_kept"], 1)
                for b in range(2):
                    c = i * 2 + b
                    here = ds(c * C, C)
                    dve.wait_ge(S["pr"], c + 1)
                    tt(BK[:, 0, :, here], q0[b][:, :, 0:C], pairs(eye[:]), ALU.add).then_inc(S["phi_kept"], 1)
                    tt(NR[:, :, 1, here], q0[b][:, :, C:P], NR[:, :, 1, here], ALU.add).then_inc(S["r_kept"], 1)
            turns(dve, turn)
            dve.wait_ge(S["phi_kept"], NCH)
            dve.wait_ge(S["r_kept"], NCH)

        @block.scalar
        def _(act):
            def copy(out, in_, sem):
                nc.scalar.activation(out, in_, ACT.Copy).then_inc(S[sem], 1)

            act.wait_ge(S["zeroed"], 3)

            def turn(i, first):
                for r, (qa, qb) in enumerate(((0, 1), (2, 3))):
                    for b in range(2):
                        for n, (q, src) in enumerate(((qa, q2), (qb, q3))):
                            act.wait_ge(S["turn"], i * 8 + r * 4 + b * 2 + n + 1)
                            if not first and r == 0:
                                act.wait_ge(S["zy"], i * 2 - 1 + b)
                            copy(turned[:, b, q], src[b][:], "kept")
                for lev in range(NLEV):
                    if lev == 1:
                        for b in range(2):
                            act.wait_ge(S["a2v"], i * 2 + b + 1)
                            copy(na[:, b, :, 1], q2[b][:, :, 0:C], "a2v_kept")
                    for b in range(2):
                        n = (i * NLEV + lev) * 2 + b
                        act.wait_ge(S["made"], n + 1)
                        if lev < NLEV - 1:
                            act.wait_ge(S["ut"], n + 3)
                            copy(wz[:, b].rearrange("p a s c -> p a (s c)"), q0[b][:], "wz")
                        else:
                            for h in range(2):
                                copy(wbd[half(h), b, :, half(h)], q0[b][half(h), :, 0:C], ("wbd0", "wbd")[h])
                for b in range(2):
                    act.wait_ge(S["tn_kept"], i * 2 + b + 1)
                    for h in range(2):
                        copy(xbd[half(h), b, :, half(h)], q3[b][half(h), :, C:P], ("xbd0", "xbd")[h])
                    copy(xst[:, b], q3[b][:, :, C:P], "xst")
                for b in range(2):
                    c = i * 2 + b
                    here = ds(c * C, C)
                    act.wait_ge(S["zy"], c + 1)
                    copy(NR[:, :, 0, here], q1[b][:, :, 0:C], "z_kept")
                    copy(Y[:, :, here], q1[b][:, :, C:P], "y_kept")
            turns(act, turn)
            act.wait_ge(S["z_kept"], NCH)
            act.wait_ge(S["y_kept"], NCH)


def rwkv_scan(kit, NR, BK, ELC, Y, state_out):
    nc = kit.nc
    names = ("zeroed", "phi_in", "next", "summed", "state", "placed", "y", "y_added", "state_out")
    S = {n: kit.sem("rn_" + n) for n in names}
    with ExitStack() as ctx:
        phi = kit.sb(ctx, "rn_phi", [P, 2, NPAIR, P])
        sbd = kit.sb(ctx, "rn_sbd", [P, 2, NPAIR, P])
        states = kit.sb(ctx, "rn_states", [P, NCH + 1, NPAIR, C])
        tsum = kit.sb(ctx, "rn_tsum", [P, NPAIR, C])
        ps = [kit.ps(ctx, f"rn_ps{b}", [P, NPAIR, P]) for b in range(2)]
        py = [kit.ps(ctx, f"rn_py{b}", [P, NPAIR, P]) for b in range(2)]
        block = ctx.enter_context(nc.Block())
        half = lambda h: slice(h * C, (h + 1) * C)
        at = lambda c: states[:, ds(c, 1)].rearrange("p s a c -> p (s a) c")

        def chunks(eng, step):
            for c in range(2):
                step(c, c, True)
            with eng.Fori(1, NCH // 2) as i:
                for b in range(2):
                    step(i * 2 + b, b, False)

        @block.sync
        def _(sp):
            sp.wait_ge(S["state"], NCH)
            sp.dma_start(state_out, states[:, NCH]).then_inc(S["state_out"], 16)
            sp.wait_ge(S["state_out"], 16)

        @block.scalar
        def _(act):
            def step(c, b, first):
                if not first:
                    act.wait_ge(S["next"], c - 1)
                for h in range(2):
                    nc.scalar.activation(phi[half(h), b, :, half(h)], BK[half(h), 0, :, ds(c * C, C)],
                                         ACT.Copy).then_inc(S["phi_in"], 1)
            act.wait_ge(S["zeroed"], 3)
            chunks(act, step)

        @block.gpsimd
        def _(pool):
            nc.gpsimd.memset(sbd[:], 0.0).then_inc(S["zeroed"], 1)
            nc.gpsimd.memset(phi[:], 0.0).then_inc(S["zeroed"], 1)
            pool.wait_ge(S["zeroed"], 3)

            def step(c, b, first):
                if not (isinstance(c, int) and c == 0):
                    pool.wait_ge(S["state"], c)
                if not first:
                    pool.wait_ge(S["y"], c - 1)
                for h in range(2):
                    nc.gpsimd.tensor_copy(sbd[half(h), b, :, half(h)], at(c)[half(h)]).then_inc(S["placed"], 1)
            chunks(pool, step)

        @block.tensor
        def _(pe):
            pe.wait_ge(S["zeroed"], 3)

            def values(c, b, first):
                pe.wait_ge(S["placed"], c * 2 + 2)
                if not first:
                    pe.wait_ge(S["y_added"], c - 1)
                for p in range(NPAIR):
                    last = nc.tensor.matmul(py[b][:, p, 0:C], sbd[:, b, p, :], NR[:, p, 1, ds(c * C, C)],
                                            start=True, stop=True)
                last.then_inc(S["y"], 1)

            def step(c, b, first):
                pe.wait_ge(S["phi_in"], c * 2 + 2)
                if not (isinstance(c, int) and c == 0):
                    pe.wait_ge(S["state"], c)
                for p in range(NPAIR):
                    last = nc.tensor.matmul(ps[b][:, p, 0:C], phi[:, b, p, :], at(c)[:, p, :], start=True, stop=True)
                last.then_inc(S["next"], 1)
                values(c, b, first)
            chunks(pe, step)

        @block.vector
        def _(dve):
            nc.vector.memset(states[:, 0], 0.0).then_inc(S["zeroed"], 1)
            dve.wait_ge(S["zeroed"], 3)

            def step(c, b, first):
                dve.wait_ge(S["next"], c + 1)
                if not (isinstance(c, int) and c == 0):
                    dve.wait_ge(S["state"], c)
                nc.vector.tensor_tensor(tsum[:], ps[b][:, :, 0:C], NR[:, :, 0, ds(c * C, C)], ALU.add)\
                    .then_inc(S["summed"], 1)
                dve.wait_ge(S["summed"], c + 1)
                nc.vector.tensor_tensor(at(c + 1), tsum[:], ELC[:, :, ds(c, 1)].broadcast_to([P, NPAIR, C]),
                                        ALU.mult).then_inc(S["state"], 1)
                if not (isinstance(c, int) and c == 0):
                    add(c - 1, 1 - b)

            def add(c, b):
                dve.wait_ge(S["y"], c + 1)
                y = Y[:, :, ds(c * C, C)]
                nc.vector.tensor_tensor(y, py[b][:, :, 0:C], y, ALU.add).then_inc(S["y_added"], 1)
            chunks(dve, step)
            add(NCH - 1, 1)
            dve.wait_ge(S["y_added"], NCH)


class SampleStates:

    def __init__(self, kit, ctx):
        self.nc = kit.nc
        self.vec = kit.sb(ctx, "rs_vec", [P, NT, NSTEP, 64])
        self.v2 = kit.sb(ctx, "rs_v2", [P, NT, 32])
        self.st = kit.sb(ctx, "rs_st", [P, 32, 64])
        self.tmp = kit.sb(ctx, "rs_tmp", [P, 32, 64])
        self.sav = kit.sb(ctx, "rs_sa", [P, 32])
        self.ys = kit.sb(ctx, "rs_y", [P, NT, 32])

    @staticmethod
    def dump(kit, sd, ident, SD):
        nc = kit.nc
        S = {n: kit.sem("rs_" + n) for n in ("turned", "kept", "out_sd")}
        with ExitStack() as ctx:
            sdt = kit.sb(ctx, "rs_sdt", [NS, 8, NSTEP, 64])
            pt = kit.ps(ctx, "rs_pt", [NS, NSTEP, 512])
            block = ctx.enter_context(nc.Block())

            @block.sync
            def _(sp):
                sp.wait_ge(S["kept"], 1)
                sp.dma_start(sd, sdt[:]).then_inc(S["out_sd"], 16)
                sp.wait_ge(S["out_sd"], 16)

            @block.tensor
            def _(pe):
                for q in range(NSTEP):
                    for p in range(NPAIR):
                        last = nc.tensor.transpose(pt[:, q, p * P:(p + 1) * P], SD[:, p, q, :], ident)
                last.then_inc(S["turned"], 1)

            @block.vector
            def _(dve):
                dve.wait_ge(S["turned"], 1)
                nc.vector.tensor_copy(sdt[:].rearrange("t h q k -> t q h k"),
                                      pt[:].rearrange("t q (h k) -> t q h k", k=64)).then_inc(S["kept"], 1)

    def load(self, kit, wkv, sd):
        nc, vec, st = self.nc, self.vec, self.st
        S = {n: kit.sem("rs_" + n) for n in ("vec_in", "vec_in_act", "state_in", "halved")}
        with ExitStack() as ctx:
            block = ctx.enter_context(nc.Block())

            def spread_vectors(eng, h, sem):
                for n in range(NB):
                    at = h * 64 + n * 8
                    eng.dma_start(vec[at:at + 8], sd[n * NT:(n + 1) * NT].rearrange("t h q k -> h t (q k)"))\
                        .then_inc(S[sem], 16)

            @block.sync
            def _(sp):
                spread_vectors(sp, 0, "vec_in")
                sp.dma_start(st[0:64], wkv[:, 0]).then_inc(S["state_in"], 16)

            @block.scalar
            def _(act):
                spread_vectors(act, 1, "vec_in_act")
                act.dma_start(st[64:128], wkv[:, 1]).then_inc(S["state_in"], 16)

            @block.vector
            def _(dve):
                dve.wait_ge(S["vec_in"], 16 * NB)
                dve.wait_ge(S["vec_in_act"], 16 * NB)
                for h in range(2):
                    rows = slice(h * 64, (h + 1) * 64)
                    nc.vector.tensor_copy(self.v2[rows], vec[rows, :, 5, h * 32:(h + 1) * 32]).then_inc(S["halved"], 1)
                dve.wait_ge(S["halved"], 2)
                dve.wait_ge(S["state_in"], 32)

    def recur(self, pool, done):
        vec, v2, st, tmp, sav, ys = self.vec, self.v2, self.st, self.tmp, self.sav, self.ys
        along_v = lambda t, q: vec[:, t, q, :].unsqueeze(1).broadcast_to([P, 32, 64])
        along_k = lambda z: z.unsqueeze(2).broadcast_to([P, 32, 64])

        def summed(out):
            n = 32
            while n > 1:
                yield tmp[:, :, 0:n], tmp[:, :, 0:n], tmp[:, :, n:2 * n], ALU.add
                n //= 2
            yield out, tmp[:, :, 0], tmp[:, :, 1], ALU.add

        count = 0
        for t in range(NT):
            steps = (
                (tmp[:], st[:], along_v(t, 1), ALU.mult), *summed(sav[:]),
                (st[:], st[:], along_v(t, 0), ALU.mult),
                (tmp[:], along_k(sav[:]), along_v(t, 2), ALU.mult), (st[:], st[:], tmp[:], ALU.subtract),
                (tmp[:], along_k(v2[:, t, :]), along_v(t, 3), ALU.mult), (st[:], st[:], tmp[:], ALU.add),
                (tmp[:], st[:], along_v(t, 4), ALU.mult), *summed(ys[:, t, :]))
            for out, x, y, op in steps:
                self.nc.gpsimd.tensor_tensor(out, x, y, op).then_inc(done, 1)
                count += 1
                pool.wait_ge(done, count)

    def unload(self, kit, o, ident, Y):
        nc, ys, st, ysd = self.nc, self.ys, self.st, o["ysd"]
        S = {n: kit.sem("rs_" + n) for n in ("y_out", "y_out_act", "state_out", "y_in", "y_turned", "y_kept")}
        with ExitStack() as ctx:
            yt = kit.sb(ctx, "rs_yt", [NS, 512])
            py = kit.ps(ctx, "rs_py", [P, 512])
            block = ctx.enter_context(nc.Block())

            def gather(eng, h, sem):
                for n in range(NB):
                    at = h * 64 + n * 8
                    eng.dma_start(ysd[n * NT:(n + 1) * NT, :, h].rearrange("t h v -> h t v"), ys[at:at + 8])\
                        .then_inc(S[sem], 16)

            @block.sync
            def _(sp):
                gather(sp, 0, "y_out")
                sp.wait_ge(S["y_out"], 16 * NB)
                sp.wait_ge(S["y_out_act"], 16 * NB)
                sp.dma_start(yt[:], ysd.rearrange("t h a v -> t (h a v)")).then_inc(S["y_in"], 16)
                sp.wait_ge(S["state_out"], 32)

            @block.scalar
            def _(act):
                gather(act, 1, "y_out_act")
                for h in range(2):
                    act.dma_start(o["wkv_sample"][:, h], st[h * 64:(h + 1) * 64]).then_inc(S["state_out"], 16)

            @block.tensor
            def _(pe):
                pe.wait_ge(S["y_in"], 16)
                for p in range(NPAIR):
                    last = nc.tensor.transpose(py[:, p * NS:(p + 1) * NS], yt[:, p * P:(p + 1) * P], ident[0:NS, 0:NS])
                last.then_inc(S["y_turned"], 1)

            @block.vector
            def _(dve):
                dve.wait_ge(S["y_turned"], 1)
                nc.vector.tensor_copy(Y[:, :, SEQ:T], py[:, 0:NPAIR * NS].rearrange("p (a t) -> p a t", t=NS))\
                    .then_inc(S["y_kept"], 1)
                dve.wait_ge(S["y_kept"], 1)


def rwkv_finish(kit, a, spill, epsg, param, Y, ident, blockcol):
    nc = kit.nc
    names = ("blk_in", "bon_in", "g_in", "mean", "centred", "squared", "var", "rooted", "inverted", "spread",
             "normed", "affine", "bonused", "gated")
    S = {n: kit.sem("rf_" + n) for n in names}
    with ExitStack() as ctx:
        blk64 = kit.sb(ctx, "rf_blk64", [P, P])
        BON = kit.sb(ctx, "rf_BON", [P, NPAIR, T])
        G = kit.sb(ctx, "rf_G", [P, NPAIR, T])
        dev = kit.sb(ctx, "rf_dev", [P, NPAIR, T])
        sq = kit.sb(ctx, "rf_sq", [P, 2, T])
        col = kit.sb(ctx, "rf_col", [P, 2, NBLK, 2])
        pm = kit.ps(ctx, "rf_pm", [P, 3, 512])
        wide = kit.ps(ctx, "rf_wide", [P, 3 * 512])
        pc = [kit.ps(ctx, f"rf_pc{b}", [P, NBLK, 2]) for b in range(2)]
        block = ctx.enter_context(nc.Block())
        part = lambda z: z.rearrange("p (n t) -> p n t", t=T3)

        @block.sync
        def _(sp):
            sp.dma_start(blk64[:], a["blockmean"]).then_inc(S["blk_in"], 16)
            sp.dma_start(BON[:], spill[0]).then_inc(S["bon_in"], 16)
            sp.dma_start(G[:], spill[1]).then_inc(S["g_in"], 16)

        @block.tensor
        def _(pe):
            def mean(p):
                if p:
                    pe.wait_ge(S["centred"], p)
                for n in range(3):
                    last = nc.tensor.matmul(pm[:, n, 0:T3], blk64[:], Y[:, p, n * T3:(n + 1) * T3], start=True, stop=True)
                last.then_inc(S["mean"], 1)

            def spread(p):
                pe.wait_ge(S["inverted"], 2 * p + 2)
                if p:
                    pe.wait_ge(S["normed"], p)
                spread_heads(nc, wide, col[:, p % 2], ident).then_inc(S["spread"], 1)

            pe.wait_ge(S["blk_in"], 16)
            mean(0)
            for p in range(NPAIR):
                if p + 1 < NPAIR:
                    mean(p + 1)
                pe.wait_ge(S["squared"], p + 1)
                if p >= 2:
                    pe.wait_ge(S["rooted"], 2 * p - 2)
                sum_heads(nc, pc[p % 2], sq[:, p % 2], blockcol).then_inc(S["var"], 1)
                if p:
                    spread(p - 1)
            spread(NPAIR - 1)

        @block.scalar
        def _(act):
            def root(p):
                act.wait_ge(S["var"], p + 1)
                if p >= 2:
                    act.wait_ge(S["spread"], p - 1)
                for rows, cols in TOKEN_PARTS:
                    nc.scalar.activation(col[rows, p % 2, cols], pc[p % 2][rows, cols], ACT.Sqrt, bias=epsg[rows],
                                         scale=1.0 / C).then_inc(S["rooted"], 1)

            for p in range(NPAIR):
                act.wait_ge(S["centred"], p + 1)
                if p >= 2:
                    act.wait_ge(S["var"], p - 1)
                nc.scalar.activation(sq[:, p % 2], dev[:, p], ACT.Square).then_inc(S["squared"], 1)
                root(p)

        @block.vector
        def _(dve):
            def centre(p):
                dve.wait_ge(S["mean"], p + 1)
                nc.vector.tensor_tensor(part(dev[:, p]), part(Y[:, p]), pm[:, :, 0:T3], ALU.subtract)\
                    .then_inc(S["centred"], 1)

            centre(0)
            for p in range(NPAIR):
                if p + 1 < NPAIR:
                    centre(p + 1)
                dve.wait_ge(S["rooted"], 2 * p + 2)
                for rows, cols in TOKEN_PARTS:
                    nc.vector.reciprocal(col[rows, p % 2, cols], col[rows, p % 2, cols]).then_inc(S["inverted"], 1)
                dve.wait_ge(S["spread"], p + 1)
                nc.vector.tensor_tensor(dev[:, p], dev[:, p], wide[:, 0:T], ALU.mult).then_inc(S["normed"], 1)
                dve.wait_ge(S["normed"], p + 1)
                nc.vector.tensor_scalar(Y[:, p], dev[:, p], param("ln_w", 4)[:, p:p + 1], param("ln_b", 4)[:, p:p + 1],
                                        ALU.mult, ALU.add).then_inc(S["affine"], 1)

        @block.gpsimd
        def _(pool):
            pool.wait_ge(S["bon_in"], 16)
            pool.wait_ge(S["g_in"], 16)
            for p in range(NPAIR):
                pool.wait_ge(S["affine"], p + 1)
                nc.gpsimd.tensor_tensor(Y[:, p], Y[:, p], BON[:, p], ALU.add).then_inc(S["bonused"], 1)
                pool.wait_ge(S["bonused"], p + 1)
                nc.gpsimd.tensor_tensor(Y[:, p], Y[:, p], G[:, p], ALU.mult).then_inc(S["gated"], 1)
            pool.wait_ge(S["gated"], NPAIR)


def build(nc, a, o):
    with ExitStack() as top:
        kit = Kit(nc)
        par = kit.sb(top, "par", [P, NPARAM])
        ones = kit.sb(top, "ones", [P, 1])
        epsc = kit.sb(top, "epsc", [P, 2])
        param = lambda name, n: par[:, PCOL[name]:PCOL[name] + n]

        ident = kit.sb(top, "ident", [P, P])
        identb = kit.sb(top, "identb", [P, P], BF16)
        causal = kit.sb(top, "causal", [P, P], BF16)
        blockcol = kit.sb(top, "blockcol", [P, 2])
        lam = kit.sb(top, "lam", [P, 8])
        oT = o["oT"].rearrange("(h p) t -> h p t", p=P)

        gain = lambda name: lambda k: param(name, KD)[:, k:k + 1]

        load_phase(kit, "ld_c", [(ident[:], a["ident"]), (identb[:], a["identb"]), (causal[:], a["causal"]),
                                 (par[:], a["par"]), (blockcol[:], a["blockcol"])])
        made, chain = kit.sem("made"), kit.sem("lam_chain")
        with ExitStack() as ctx:
            lq = kit.sb(ctx, "lq", [P, 4, DH])
            prod = kit.sb(ctx, "lprod", [P, 2, DH])
            comb1 = kit.sb(ctx, "lcomb", [P, 17])
            load_phase(kit, "ld_l", [(lq[:], a["lams"]), (comb1[:], a["comb"])])
            block = ctx.enter_context(nc.Block())

            @block.scalar
            def _(act):
                act.wait_ge(chain, 3)
                nc.scalar.activation(lam[:, 2:4], lam[:, 0:2], ACT.Exp).then_inc(chain, 1)

            @block.vector
            def _(dve):
                nc.vector.memset(ones[:], 1.0 / D).then_inc(made, 1)
                nc.vector.memset(epsc[:, 0:1], EPS).then_inc(made, 1)
                nc.vector.memset(epsc[:, 1:2], GN_EPS).then_inc(made, 1)
                nc.vector.tensor_tensor(prod[:], lq[:, 0:2], lq[:, 2:4], ALU.mult).then_inc(chain, 1)
                dve.wait_ge(chain, 1)
                nc.vector.tensor_reduce(lam[:, 0:2], prod[:], AX, ALU.add).then_inc(chain, 2)
                dve.wait_ge(chain, 4)
                nc.vector.tensor_tensor(lam[:, 4:5], lam[:, 3:4], lam[:, 2:3], ALU.subtract).then_inc(chain, 1)
                dve.wait_ge(chain, 5)
                nc.vector.tensor_scalar(lam[:, 4:5], lam[:, 4:5], -LAM_INIT, None, ALU.add).then_inc(chain, 1)
                dve.wait_ge(chain, 6)
                nc.vector.tensor_scalar(lam[:, 5:6], lam[:, 4:5], -1.0, comb1[:, 16:17], ALU.add,
                                        ALU.mult).then_inc(chain, 1)
                dve.wait_ge(chain, 7)
                nc.vector.tensor_scalar(lam[:, 5:6], lam[:, 5:6], 1.0, None, ALU.add).then_inc(chain, 1)
                dve.wait_ge(chain, 8)
                dve.wait_ge(made, 3)

        x_view = a["xT"].rearrange("(k p) t -> p k t", p=P)

        proj = o["projT"].rearrange("(m p) t -> m p t", p=P)

        with ExitStack() as ctx:
            Hh = kit.sb(ctx, "Hh", [P, KD, T], F32R)
            Hl = kit.sb(ctx, "Hl", [P, KD, T], F32R)
            raw = weight_buffer(kit, ctx, "in", KD)
            with ExitStack() as inner:
                X = kit.sb(inner, "X", [P, KD, T])
                R = kit.sb(inner, "R", [P, T])
                rms_rows(kit, "rms_x", X, R[:], KD, ones[:], epsc[:, 0:1], ident[:],
                         loads=[x_view[:, k] for k in range(KD)])
                scale_split(kit, "split_x", X, KD, T, Hh, Hl, gain("g_mix_pre"), lambda k: R[:],
                            ahead=first_units(raw, a["w_in"]))
            parts = [(n * T3, T3) for n in range(3)]
            project(kit, "in", MT_IN, KD, 1, a["w_in"], Hh, Hl, parts,
                    lambda c: ToDram(kit, c, "in", parts, lambda m: proj[m] if isinstance(m, int) else
                                     proj[ds(m, 1)].rearrange("a p t -> (a p) t")), raw)

        kit.retire()

        mix = ExitStack()
        MIX = kit.sb(mix, "mixed", [P, KD, T])
        Y = MIX[:, HEADS:]
        with ExitStack() as ctx:
            with ExitStack() as rwkv:
                NR = kit.sb(rwkv, "NR", [P, NPAIR, 2, SEQ])
                BK = kit.sb(rwkv, "BK", [P, 2, NPAIR, SEQ])
                spill = [o[n].rearrange("(a p) t -> p a t", p=P) for n in ("bonus", "gate")]
                ELC = kit.sb(rwkv, "ELC", [P, NPAIR, NCH])
                with ExitStack() as values:
                    V = kit.sb(values, "V", [P, NPAIR, T])
                    with ExitStack() as inner:
                        SD = kit.sb(inner, "SD", [P, NPAIR, NSTEP, NS])
                        with ExitStack() as prep:
                            BON, G = MIX[:, 0:HEADS], Y
                            Rm = kit.sb(prep, "Rm", [P, NPAIR, T])
                            Km = kit.sb(prep, "Km", [P, NPAIR, T])
                            X12 = kit.sb(prep, "X12", [P, T])
                            XG = kit.sb(prep, "XG", [P, T])
                            dsts = [z[:, p] for z in (Rm, Km, V) for p in range(NPAIR)] + [X12[:], XG[:]]
                            rwkv_mix(kit, prep, a, proj, param, dsts)
                            rwkv_prepare(kit, prep, a, param, Rm, Km, V, X12, XG[:], NR, BK[:, 0], BK[:, 1], BON, G,
                                         ELC, SD, spill, ident[:], blockcol[:])
                        SampleStates.dump(kit, o["sd"], ident[:], SD)
                    kit.retire()
                    rwkv_transitions(kit, a, NR, BK, V, Y)
                kit.retire()
                rwkv_scan(kit, NR, BK, ELC, Y, o["wkv_prompt"])
            states = SampleStates(kit, ctx)
            states.load(kit, a["wkv"], o["sd"])
            attend_prompt(kit, proj, oT, ident[:], identb[:], causal[:], lam[:, 4:5], states.recur)
            kit.retire()
            attend_sample(kit, a, proj, oT, ident[:], identb[:], lam[:, 5:6])
            states.unload(kit, o, ident[:], Y)
            kit.retire()
            rwkv_finish(kit, a, spill, epsc[:, 1:2], param, Y, ident[:], blockcol[:])

        kit.retire()
        third = [(n * T3, T3) for n in range(3)]
        quarter = [(0, TH // 2), (TH // 2, TH // 2)]
        x1 = o["x1T"].rearrange("(k p) t -> p k t", p=P)
        h2 = o["h2T"].rearrange("(k p) t -> p k t", p=P)
        fT = o["fT"].rearrange("(k p) t -> p k t", p=P)

        with mix as ctx:
            Y = MIX
            X = kit.sb(ctx, "X1", [P, KD, T])
            SQ = kit.sb(ctx, "squares1", [P, T])
            with ExitStack() as inner:
                Hh = kit.sb(inner, "Mh", [P, KD, T], F32R)
                Hl = kit.sb(inner, "Ml", [P, KD, T], F32R)
                raw = weight_buffer(kit, inner, "wo", KD)
                with ExitStack() as pre:
                    R4 = kit.sb(pre, "R4", [P, HEADS, T])
                    gs = kit.sb(pre, "gs", [P, 1])
                    ones_head = kit.sb(pre, "ones_head", [P, 1])
                    subln = kit.sem("subln")
                    with nc.Block() as block:
                        @block.vector
                        def _(dve):
                            nc.vector.memset(ones_head[:], 1.0 / P).then_inc(subln, 1)
                            nc.vector.tensor_scalar(gs[:], param("g_subln", 1), 1.0 - LAM_INIT, None,
                                                    ALU.mult).then_inc(subln, 1)
                            dve.wait_ge(subln, 2)
                    rms_rows(kit, "rms_o", Y, R4[:], HEADS, ones_head[:], epsc[:, 0:1], ident[:], per_tile=True,
                             loads=[oT[h] for h in range(HEADS)])
                    scale_split(kit, "split_o", Y, 4, T, Hh, Hl, lambda k: gs[:], lambda k: R4[:, k, :])
                    scale_split(kit, "split_r", Y[:, 4:8], 4, T, Hh[:, 4:8], Hl[:, 4:8],
                                ahead=first_units(raw, a["w_o"]))
                project(kit, "wo", KD, KD, 1, a["w_o"], Hh, Hl, third, lambda c: ToSbufSquared(kit, c, "wo", third, Y, SQ[:]),
                        raw, prefetch=[(X[:], x_view)])
            R = kit.sb(ctx, "R1", [P, T])
            rms_rows(kit, "rms_m", Y, R[:], KD, ones[:], epsc[:, 0:1], ident[:], sums=SQ[:])
            add_scaled(kit, "add_m", Y, param("g_mix_post", KD), R[:], X, store=x1, sums=SQ[:])
            rms_rows(kit, "rms_f", X, R[:], KD, ones[:], epsc[:, 0:1], ident[:], sums=SQ[:])
            scale_split(kit, "store_h2", X, KD, T, None, None, gain("g_ffn_pre"), lambda k: R[:], store=h2)
        kit.retire()

        with ExitStack() as ctx:
            carry = kit.sb(ctx, "carry", [P, 2 * FT, 2])
            states = kit.sb(ctx, "states", [P, 2 * FT, 2 * NB])
            conv_out = kit.sb(ctx, "conv_out", [P, 2 * FT, 2 + 2 * NB])
            cleared = kit.sem("carry_cleared")
            load_phase(kit, "ld_st", [(states[:], a["convT"])])
            with nc.Block() as block:
                @block.vector
                def _(dve):
                    nc.vector.memset(carry[:], 0.0).then_inc(cleared, 1)
                    dve.wait_ge(cleared, 1)
            for half in range(2):
                with ExitStack() as inner:
                    Gh = kit.sb(inner, f"Gh{half}", [P, FT, TH], F32R)
                    Gl = kit.sb(inner, f"Gl{half}", [P, FT, TH], F32R)
                    raw_down = weight_buffer(kit, inner, f"dn{half}", FT // 2)
                    with ExitStack() as up:
                        Hh = kit.sb(up, f"Uh{half}", [P, KD, TH], F32R)
                        Hl = kit.sb(up, f"Ul{half}", [P, KD, TH], F32R)
                        raw = weight_buffer(kit, up, f"up{half}", KD)
                        with ExitStack() as pre:
                            H = kit.sb(pre, f"H2{half}", [P, KD, TH])
                            scale_split(kit, f"split_h{half}", H, KD, TH, Hh, Hl, ahead=first_units(raw, a["w_up"]),
                                        loads=[h2[:, k, half * TH:(half + 1) * TH] for k in range(KD)])
                        project(kit, f"up{half}", 2 * FT, KD, 1, a["w_up"], Hh, Hl, quarter,
                                lambda c: ConvGate(kit, c, f"cg{half}", quarter, par, carry, states, conv_out, Gh, Gl,
                                                   half == 1), raw, prefetch=first_units(raw_down, a["w_down"]))
                    down = o["fT"].rearrange("(m p) t -> m p t", p=P)[:, :, half * TH:(half + 1) * TH]
                    project(kit, f"dn{half}", KD, FT // 2, 2, a["w_down"], Gh, Gl, quarter,
                            lambda c: ToDram(kit, c, f"dn{half}", quarter, lambda m: down[m] if isinstance(m, int) else
                                             down[ds(m, 1)].rearrange("a p t -> (a p) t")), raw_down)
                kit.retire()
            load_phase(kit, "st_cv", [(o["conv_out"], conv_out[:])])

        with ExitStack() as ctx:
            X = kit.sb(ctx, "X2", [P, KD, T])
            E = kit.sb(ctx, "E", [P, PLE // P, T])
            SQ = kit.sb(ctx, "squares2", [P, T])
            R = kit.sb(ctx, "R2", [P, T])
            Y = kit.sb(ctx, "Y2", [P, KD, T])
            rms_rows(kit, "rms_d", Y, R[:], KD, ones[:], epsc[:, 0:1], ident[:], loads=[fT[:, k] for k in range(KD)],
                     also=[(X[:], x1), (E[:], a["pT"].rearrange("(k p) t -> p k t", p=P))])
            add_scaled(kit, "add_d", Y, param("g_ffn_post", KD), R[:], X)
            with ExitStack() as inner:
                Eh = kit.sb(inner, "Eh", [P, PLE // P, T], F32R)
                El = kit.sb(inner, "El", [P, PLE // P, T], F32R)
                raw = weight_buffer(kit, inner, "ple", PLE // P)
                scale_split(kit, "split_p", E, PLE // P, T, Eh, El, ahead=first_units(raw, a["w_ple"]))
                project(kit, "ple", KD, PLE // P, 1, a["w_ple"], Eh, El, third,
                        lambda c: ToSbuf(kit, c, "ple", third, Y, 0.5), raw)
            with ExitStack() as inner:
                Hh = kit.sb(inner, "X2h", [P, KD, T], F32R)
                Hl = kit.sb(inner, "X2l", [P, KD, T], F32R)
                raw = weight_buffer(kit, inner, "pg", KD)
                scale_split(kit, "split_x2", X, KD, T, Hh, Hl, ahead=first_units(raw, a["w_gate"]))
                project(kit, "pg", KD, KD, 1, a["w_gate"], Hh, Hl, third, lambda c: Gate(kit, c, "pg", third, Y, SQ[:]),
                        raw)
            rms_rows(kit, "rms_p", Y, R[:], KD, ones[:], epsc[:, 0:1], ident[:], sums=SQ[:])
            add_scaled(kit, "add_p", Y, param("g_ple", KD), R[:], X, store=o["yT"].rearrange("(k p) t -> p k t", p=P))


OUTS = {"yT": (D, T), "projT": (N_IN, T), "wkv_prompt": (P, NPAIR, C), "wkv_sample": (NB * 8, 2, 32, 64),
        "conv_out": (P, 2 * FT, 2 + 2 * NB)}
SCRATCH = {"oT": (512, T), "x1T": (D, T), "h2T": (D, T), "fT": (D, T), "bonus": (512, T), "gate": (512, T),
           "sd": (NS, 8, NSTEP, 64), "ysd": (NS, 8, 2, 32)}


def kernel(**inputs):
    import numpy as np
    import concourse.bacc as bacc
    from concourse import mybir as mb
    from concourse.bass_utils import run_bass_kernel_spmd

    bf16 = mb.dt.np(mb.dt.bfloat16)
    v = {n: np.asarray(x) for n, x in inputs.items()}

    def cols(x, n):
        x = np.ascontiguousarray(x, dtype=x.dtype).reshape(-1)
        return np.pad(x, (0, n * P - x.size)).reshape(n, P).T

    def halves(x):
        g, u = cols(x[:FF], FT), cols(x[FF:], FT)
        return np.stack([g, u], axis=2).reshape(P, 2 * FT)

    def tiles(w, kt, units):
        k, m = units * kt * P, -(-w.shape[1] // P) * P
        w = np.pad(w, ((0, k - w.shape[0]), (0, m - w.shape[1])))
        w = w.reshape(units, kt, P, m // P, P).transpose(3, 0, 2, 1, 4)
        return np.ascontiguousarray(w).reshape(m // P * units, P, kt * P)

    def tokens(p, s):
        return np.ascontiguousarray(np.concatenate([p.reshape(SEQ, -1), s.reshape(NS, -1)]).T)

    par = np.ascontiguousarray(np.concatenate(
        [cols(v[n][0], 8) for n in ("g_mix_pre", "g_mix_post", "g_ffn_pre", "g_ffn_post", "g_ple")]
        + [cols(v["g_subln"][0], 1), cols(v["mu_shift"][0], 14)]
        + [cols(v[n][0], 4) for n in ("w0", "a0", "k_k", "k_a", "r_k", "ln_x_w", "ln_x_b")]
        + [halves(v["conv_w"][0, j]) for j in range(3)] + [halves(v["conv_b"][0])], axis=1))
    comb = np.zeros((P, 17), np.float32)
    new_mask = np.full((P, NB, NS), NEG, np.float32)
    for h in range(HEADS):
        for c in range(2):
            for t in range(NT):
                row = 32 * h + NT * c + t
                comb[row, NT * h + t] = 1.0
                comb[row, 16] = c
                for n in range(NB):
                    new_mask[row, n, NT * n:NT * n + t + 1] = 0.0
    j = np.arange(P) % C
    i = np.arange(C)

    def blocked(m):
        own = (np.arange(P) // C)[:, None] == np.arange(2)[None, :]
        return (m[:, None, :] * own[:, :, None]).astype(np.float32)

    lev = [(j[:, None] == i[None, :]) | ((j[:, None] >> (n + 1) == i[None, :] >> (n + 1))
                                         & (j[:, None] >> n < i[None, :] >> n)) for n in range(NLEV)]
    new_mask = new_mask.reshape(P, NB * NS).astype(bf16)
    wu = v["w_up"][0]
    sc = v["state_conv"][0].reshape(NB * 2, 2 * FF)
    convT = np.ascontiguousarray(np.stack([halves(row) for row in sc], axis=2))
    gate, val = tiles(wu[:, :FF], KD, 1), tiles(wu[:, FF:], KD, 1)
    arrays = {
        "xT": tokens(v["x_prompt"], v["x_sample"]),
        "pT": tokens(v["p_prompt"], v["p_sample"]),
        "par": par,
        "w_in": tiles(v["w_in"][0], KD, 1),
        "w_o": tiles(v["w_o"][0], KD, 1),
        "w_up": np.ascontiguousarray(np.stack([gate, val], axis=1)).reshape(2 * FT, P, KD * P),
        "w_down": tiles(v["w_down"][0], FT // 2, 2),
        "w_ple": tiles(v["w_ple"][0], PLE // P, 1),
        "w_gate": tiles(v["w_ple_gate"][0], KD, 1),
        "convT": convT,
        "ident": np.eye(P, dtype=np.float32),
        "identb": np.eye(P, dtype=bf16),
        "causal": np.where(np.arange(P)[None, :] > np.arange(P)[:, None], NEG, 0.0).astype(bf16),
        "lams": np.tile(np.stack([v[n][0] for n in ("lam_q1", "lam_q2", "lam_k1", "lam_k2")])[None], (P, 1, 1)),
        "comb": comb,
        "w2": v["w2"][0], "a2": v["a2"][0], "g2": v["g2"][0],
        "blockcol": np.kron(np.eye(2), np.ones((C, 1))).astype(np.float32),
        "blockones": np.kron(np.eye(2), np.ones((C, C))).astype(np.float32),
        "blockmean": np.kron(np.eye(2), np.full((C, C), 1 / C)).astype(np.float32),
        "reset": np.tile((np.arange(SEQ) % C != 0)[None], (P, 1)).astype(bf16),
        "strict": blocked(j[:, None] < i[None, :]), "pairbd": blocked(np.ones((P, C))),
        "levbd": np.stack([blocked(m) for m in lev], axis=1),
        "below": (j[:, None] < i[None, :]).astype(np.float32),
        "incl": (j[:, None] <= i[None, :]).astype(np.float32),
        "eye": (j[:, None] == i[None, :]).astype(np.float32),
        "shiftT": np.ascontiguousarray(v["state_shift"][0].reshape(NB, 14, P).transpose(2, 1, 0)),
        "wkv": v["state_wkv"][0].reshape(NB * 8, 2, 32, 64),
        "new_mask": new_mask,
        "table": v["page_table"].reshape(1, -1),
        "k_pool": np.ascontiguousarray(v["cache_k"][0].transpose(0, 3, 2, 1)).reshape(POOL, P, HEADS * PAGE),
        "v_pool": v["cache_v"][0].reshape(POOL, PAGE, HEADS * P),
    }

    nc = bacc.Bacc("TRN2", target_bir_lowering=False, num_devices=1)
    a = {n: nc.dram_tensor("dram_" + n, x.shape, mb.dt.from_np(x.dtype), kind="ExternalInput").ap()
         for n, x in arrays.items()}
    o = {n: nc.dram_tensor("dram_" + n, s, mb.dt.float32, kind="ExternalOutput").ap() for n, s in OUTS.items()}
    o.update({n: nc.dram_tensor("dram_" + n, s, mb.dt.float32).ap() for n, s in SCRATCH.items()})
    build(nc, a, o)
    r = run_bass_kernel_spmd(nc, [{"dram_" + n: x for n, x in arrays.items()}], core_ids=[0]).results[0]
    y, proj, wp, ws, cv = (r["dram_" + n] for n in OUTS)
    kT, vT, sh = proj[512:1024], proj[1024:1536], proj[1536:]
    last = [SEQ + n * NT + NT - 1 for n in range(NB)]

    def split(z, shape):
        z = np.ascontiguousarray(z.T)
        return z[:SEQ].reshape(1, 1, SEQ, *shape), z[SEQ:].reshape(1, NB, NT, *shape)

    y_prompt, y_sample = (z[0] for z in split(y, (D,)))
    (kp, ks), (vp, vs) = split(kT, (HEADS, P)), split(vT, (HEADS, P))
    wp = wp.reshape(2, C, NPAIR, C).transpose(2, 0, 3, 1).reshape(1, 1, 8, C, C)
    cv = cv.reshape(P, FT, 2, 18).transpose(3, 2, 1, 0).reshape(18, 2, FT * P)[:, :, :FF].reshape(18, 2 * FF)
    return (y_prompt, y_sample, kp, vp, ks, vs, sh[:, SEQ - 1].reshape(1, 1, -1), np.ascontiguousarray(wp),
            cv[0:2].reshape(1, 1, 2, -1), np.ascontiguousarray(sh[:, last].T)[None], ws.reshape(1, NB, 8, C, C),
            cv[2:].reshape(1, NB, 2, -1))
```
